# Optimizing a Trainium2 kernel written in Bass

```python
import jax, jax.numpy as jnp
from jax import lax
import numpy as np
import math

D_MODEL = 1024
BATCH = 1
SEQ = 256
DEPTH = 2

CHUNK = 64
N_A_LAYERS = DEPTH // 2
N_B_LAYERS = DEPTH - N_A_LAYERS
MLA_HEADS = 8
Q_LORA = 384
KV_LORA = 256
NOPE_DIM = 128
ROPE_DIM = 64
V_DIM = 128
ROPE_THETA = 10000.0
Q_BLOCK = 128
B_HEADS = 16
B_HEAD_DIM = 64
LEFT_CHUNKS = 8
BAND = (LEFT_CHUNKS + 1) * CHUNK
MAX_REL = 256
REL_TABLE = MAX_REL + CHUNK
D_FF = -(-8 * D_MODEL // (3 * 256)) * 256
EPS = 1e-6


def rms_norm(x, g):
    xf = x.astype(jnp.float32)
    y = xf * lax.rsqrt(jnp.mean(xf * xf, axis=-1, keepdims=True) + EPS)
    return (y * g.astype(jnp.float32)).astype(x.dtype)

def rope_tables(positions, dtype):
    inv = 1.0 / (ROPE_THETA ** (jnp.arange(0, ROPE_DIM, 2, dtype=jnp.float32) / ROPE_DIM))
    ang = positions.astype(jnp.float32)[..., None] * inv
    return jnp.cos(ang).astype(dtype), jnp.sin(ang).astype(dtype)

def apply_rope(t, cos, sin):
    t1, t2 = jnp.split(t, 2, axis=-1)
    return jnp.concatenate([t1 * cos - t2 * sin, t2 * cos + t1 * sin], axis=-1)

def swiglu(h, w_gate, w_up, w_down):
    return (jax.nn.silu(h @ w_gate) * (h @ w_up)) @ w_down

def mla_mixer(h, cos, sin, w_a, g_q, w_uq, g_kv, w_ukv, w_o):
    B, S, _ = h.shape
    a = h @ w_a
    cq, ckv, kr = jnp.split(a, [Q_LORA, Q_LORA + KV_LORA], axis=-1)
    q = (rms_norm(cq, g_q) @ w_uq).reshape(B, S, MLA_HEADS, NOPE_DIM + ROPE_DIM)
    q_nope = q[..., :NOPE_DIM]
    q_rope = apply_rope(q[..., NOPE_DIM:], cos[:, :, None], sin[:, :, None])
    kv = (rms_norm(ckv, g_kv) @ w_ukv).reshape(B, S, MLA_HEADS, NOPE_DIM + V_DIM)
    k_nope, v = kv[..., :NOPE_DIM], kv[..., NOPE_DIM:]
    k_rope = apply_rope(kr, cos, sin)
    scale = (NOPE_DIM + ROPE_DIM) ** -0.5
    n_blk = S // Q_BLOCK
    key_chunk = jnp.arange(S) // CHUNK

    def to_blocks(t):
        return jnp.moveaxis(t.reshape(B, n_blk, Q_BLOCK, *t.shape[2:]), 1, 0)

    def block_attn(args):
        qn, qr, blk = args
        s = (jnp.einsum('bqhd,bkhd->bhqk', qn, k_nope, preferred_element_type=jnp.float32)
             + jnp.einsum('bqhr,bkr->bhqk', qr, k_rope, preferred_element_type=jnp.float32)) * scale
        q_chunk = (blk * Q_BLOCK + jnp.arange(Q_BLOCK)) // CHUNK
        mask = key_chunk[None, :] <= q_chunk[:, None]
        s = jnp.where(mask[None, None], s, -jnp.inf)
        p = jax.nn.softmax(s, axis=-1).astype(v.dtype)
        return jnp.einsum('bhqk,bkhd->bqhd', p, v)

    o = lax.map(block_attn, (to_blocks(q_nope), to_blocks(q_rope), jnp.arange(n_blk)))
    o = jnp.moveaxis(o, 0, 1).reshape(B, S, MLA_HEADS * V_DIM)
    return o @ w_o

def gather_band(t):
    B, S = t.shape[:2]
    n_c = S // CHUNK
    tp = jnp.pad(t, ((0, 0), (LEFT_CHUNKS * CHUNK, 0), (0, 0), (0, 0)))
    tp = tp.reshape(B, n_c + LEFT_CHUNKS, CHUNK, *t.shape[2:])
    band = jnp.stack([tp[:, j:j + n_c] for j in range(LEFT_CHUNKS + 1)], axis=2)
    return band.reshape(B, n_c, BAND, *t.shape[2:])

def shared_kv(x, g_src, w_kv):
    B, S, _ = x.shape
    kv = (rms_norm(x, g_src) @ w_kv).reshape(B, S, 2, B_HEADS, B_HEAD_DIM)
    return gather_band(kv[:, :, 0]), gather_band(kv[:, :, 1])

def chunked_mixer(h, k_band, v_band, w_q, rel_table, w_o):
    B, S, _ = h.shape
    n_c = S // CHUNK
    q = (h @ w_q).reshape(B, n_c, CHUNK, B_HEADS, B_HEAD_DIM)
    dist = LEFT_CHUNKS * CHUNK + jnp.arange(CHUNK)[:, None] - jnp.arange(BAND)[None, :]
    idx = jnp.clip(dist, -(CHUNK - 1), MAX_REL) + (CHUNK - 1)
    bias = rel_table.astype(jnp.float32)[:, idx]
    valid = (jnp.arange(n_c)[:, None] - LEFT_CHUNKS + jnp.arange(BAND)[None, :] // CHUNK) >= 0
    s = jnp.einsum('bnqhd,bnkhd->bnhqk', q, k_band, preferred_element_type=jnp.float32)
    s = s * (B_HEAD_DIM ** -0.5) + bias[None, None]
    s = jnp.where(valid[None, :, None, None, :], s, -jnp.inf)
    p = jax.nn.softmax(s, axis=-1).astype(v_band.dtype)
    o = jnp.einsum('bnhqk,bnkhd->bnqhd', p, v_band).reshape(B, S, B_HEADS * B_HEAD_DIM)
    return o @ w_o

def first_inputs(seed: int = 0) -> dict:
    key = jax.random.key(seed)
    ks = iter(jax.random.split(key, 32))
    f32 = jnp.float32

    def w(shape, fan_in):
        return jax.random.normal(next(ks), shape, f32) * (fan_in ** -0.5)

    def gain(shape):
        return 1.0 + 0.05 * jax.random.normal(next(ks), shape, f32)

    x = jax.random.normal(next(ks), (BATCH, SEQ, D_MODEL), f32)
    offsets = jax.random.randint(next(ks), (BATCH, 1), 0, 4096, dtype=jnp.int32)
    positions = (jnp.arange(SEQ, dtype=jnp.int32)[None, :] + offsets).astype(jnp.int32)
    return {
        "x": x,
        "positions": positions,
        "attn_pre_g": gain((DEPTH, D_MODEL)),
        "attn_post_g": gain((DEPTH, D_MODEL)),
        "ffn_pre_g": gain((DEPTH, D_MODEL)),
        "ffn_post_g": gain((DEPTH, D_MODEL)),
        "ffn_w_gate": w((DEPTH, D_MODEL, D_FF), D_MODEL),
        "ffn_w_up": w((DEPTH, D_MODEL, D_FF), D_MODEL),
        "ffn_w_down": w((DEPTH, D_FF, D_MODEL), D_FF),
        "mla_w_a": w((N_A_LAYERS, D_MODEL, Q_LORA + KV_LORA + ROPE_DIM), D_MODEL),
        "mla_g_q": gain((N_A_LAYERS, Q_LORA)),
        "mla_w_uq": w((N_A_LAYERS, Q_LORA, MLA_HEADS * (NOPE_DIM + ROPE_DIM)), Q_LORA),
        "mla_g_kv": gain((N_A_LAYERS, KV_LORA)),
        "mla_w_ukv": w((N_A_LAYERS, KV_LORA, MLA_HEADS * (NOPE_DIM + V_DIM)), KV_LORA),
        "mla_w_o": w((N_A_LAYERS, MLA_HEADS * V_DIM, D_MODEL), MLA_HEADS * V_DIM),
        "kv_src_g": gain((D_MODEL,)),
        "w_kv_shared": w((D_MODEL, 2 * B_HEADS * B_HEAD_DIM), D_MODEL),
        "b_w_q": w((N_B_LAYERS, D_MODEL, B_HEADS * B_HEAD_DIM), D_MODEL),
        "b_rel_table": 0.2 * jax.random.normal(next(ks), (N_B_LAYERS, B_HEADS, REL_TABLE), f32),
        "b_w_o": w((N_B_LAYERS, B_HEADS * B_HEAD_DIM, D_MODEL), B_HEADS * B_HEAD_DIM),
    }

def first_block(x, positions, attn_pre_g, attn_post_g, ffn_pre_g, ffn_post_g,
              ffn_w_gate, ffn_w_up, ffn_w_down,
              mla_w_a, mla_g_q, mla_w_uq, mla_g_kv, mla_w_ukv, mla_w_o,
              kv_src_g, w_kv_shared, b_w_q, b_rel_table, b_w_o):
    cos, sin = rope_tables(positions, x.dtype)
    k_band = v_band = None
    for layer in range(DEPTH):
        h = rms_norm(x, attn_pre_g[layer])
        if layer < N_A_LAYERS:
            a = layer
            y = mla_mixer(h, cos, sin, mla_w_a[a], mla_g_q[a], mla_w_uq[a],
                          mla_g_kv[a], mla_w_ukv[a], mla_w_o[a])
        else:
            b = layer - N_A_LAYERS
            y = chunked_mixer(h, k_band, v_band, b_w_q[b], b_rel_table[b], b_w_o[b])
        x = x + rms_norm(y, attn_post_g[layer])
        h = rms_norm(x, ffn_pre_g[layer])
        f = swiglu(h, ffn_w_gate[layer], ffn_w_up[layer], ffn_w_down[layer])
        x = x + rms_norm(f, ffn_post_g[layer])
        if layer == N_A_LAYERS - 1:
            k_band, v_band = shared_kv(x, kv_src_g, w_kv_shared)
    return x


DEPTH_2 = 1

HEAD_DIM = 64
N_HEADS_MOBA = 8
N_HEADS_SB = 8
MOBA_WIDTH = N_HEADS_MOBA * HEAD_DIM
SB_WIDTH = N_HEADS_SB * HEAD_DIM
N_BRANCHES = 2
IN_WIDTH = 3 * MOBA_WIDTH + 3 * SB_WIDTH + N_BRANCHES * D_MODEL
MOBA_BLOCK = 256
MOBA_TOPK = 3
MOBA_Q_CHUNK = 16
SB_Q_BLOCK = 128
D_FF_2 = 2816
CONV_WIDTH = 3
REL_BUCKETS = 32
REL_MAX_DIST = 128
NORM_EPS = 1e-6
NEG_INF = -1e30


def rms_norm_2(x, g):
    xf = x.astype(jnp.float32)
    y = xf * lax.rsqrt(jnp.mean(xf * xf, axis=-1, keepdims=True) + NORM_EPS)
    return (y * g.astype(jnp.float32)).astype(x.dtype)

def modulate(h, shift, scale):
    return h * (1.0 + scale[:, None, :]) + shift[:, None, :]

def to_heads(t, n_heads):
    b, s, _ = t.shape
    return t.reshape(b, s, n_heads, HEAD_DIM).transpose(0, 2, 1, 3)

def merge_heads(t):
    b, h, s, hd = t.shape
    return t.transpose(0, 2, 1, 3).reshape(b, s, h * hd)

def t5_bucket(rel):
    n = jnp.maximum(rel, 0)
    max_exact = REL_BUCKETS // 2
    n_f = jnp.maximum(n, max_exact).astype(jnp.float32)
    large = max_exact + (jnp.log(n_f / max_exact) / math.log(REL_MAX_DIST / max_exact)
                         * (REL_BUCKETS - max_exact)).astype(jnp.int32)
    large = jnp.minimum(large, REL_BUCKETS - 1)
    return jnp.where(n < max_exact, n, large)

def moba_attention(q, k, v, rel_table):
    b, h, s, hd = q.shape
    n_blk = -(-s // MOBA_BLOCK)
    s_pad = n_blk * MOBA_BLOCK
    pad = ((0, 0), (0, 0), (0, s_pad - s), (0, 0))
    q = jnp.pad(q, pad)
    k = jnp.pad(k, pad)
    v = jnp.pad(v, pad)
    k_blk = k.reshape(b, h, n_blk, MOBA_BLOCK, hd)
    v_blk = v.reshape(b, h, n_blk, MOBA_BLOCK, hd)
    k_mean = jnp.mean(k_blk.astype(jnp.float32), axis=3).astype(q.dtype)
    n_sel = min(MOBA_TOPK, n_blk)
    scale = hd ** -0.5
    n_chunks = s_pad // MOBA_Q_CHUNK
    q_chunks = jnp.moveaxis(q.reshape(b, h, n_chunks, MOBA_Q_CHUNK, hd), 2, 0)
    b_idx = jnp.arange(b)[:, None, None, None]
    h_idx = jnp.arange(h)[None, :, None, None]
    offs = jnp.arange(MOBA_BLOCK)
    blk_ids = jnp.arange(n_blk)

    def chunk(args):
        qc, ci = args
        q_start = ci * MOBA_Q_CHUNK
        q_pos = q_start + jnp.arange(MOBA_Q_CHUNK)
        own = q_start // MOBA_BLOCK
        gate = jnp.einsum('bhqd,bhnd->bhqn', qc, k_mean).astype(jnp.float32)
        gate = jnp.where(blk_ids < own, gate, NEG_INF)
        _, sel = lax.top_k(gate, n_sel)
        sel_ok = sel < own
        k_sel = k_blk[b_idx, h_idx, sel]
        v_sel = v_blk[b_idx, h_idx, sel]
        s_sel = jnp.einsum('bhqd,bhqnkd->bhqnk', qc, k_sel).astype(jnp.float32) * scale
        rel_sel = q_pos[:, None, None] - (sel[..., None] * MOBA_BLOCK + offs)
        bias_sel = rel_table[h_idx[..., None], t5_bucket(rel_sel)]
        s_sel = jnp.where(sel_ok[..., None], s_sel + bias_sel, NEG_INF)
        k_own = lax.dynamic_slice_in_dim(k, own * MOBA_BLOCK, MOBA_BLOCK, axis=2)
        v_own = lax.dynamic_slice_in_dim(v, own * MOBA_BLOCK, MOBA_BLOCK, axis=2)
        s_own = jnp.einsum('bhqd,bhkd->bhqk', qc, k_own).astype(jnp.float32) * scale
        rel_own = q_pos[:, None] - (own * MOBA_BLOCK + offs)[None, :]
        bias_own = rel_table[:, t5_bucket(rel_own)]
        s_own = jnp.where(rel_own >= 0, s_own + bias_own, NEG_INF)
        logits = jnp.concatenate(
            [s_sel.reshape(b, h, MOBA_Q_CHUNK, n_sel * MOBA_BLOCK), s_own], axis=-1)
        p = jax.nn.softmax(logits, axis=-1).astype(v.dtype)
        p_sel = p[..., :n_sel * MOBA_BLOCK].reshape(b, h, MOBA_Q_CHUNK, n_sel, MOBA_BLOCK)
        p_own = p[..., n_sel * MOBA_BLOCK:]
        return (jnp.einsum('bhqnk,bhqnkd->bhqd', p_sel, v_sel)
                + jnp.einsum('bhqk,bhkd->bhqd', p_own, v_own))

    out = lax.map(chunk, (q_chunks, jnp.arange(n_chunks)))
    return jnp.moveaxis(out, 0, 2).reshape(b, h, s_pad, hd)[:, :, :s]

def stick_breaking_attention(q, k, v):
    b, h, s, hd = q.shape
    n_qb = s // SB_Q_BLOCK
    scale = hd ** -0.5
    k_pos = jnp.arange(s)
    q_blocks = jnp.moveaxis(q.reshape(b, h, n_qb, SB_Q_BLOCK, hd), 2, 0)

    def block(args):
        qb, bi = args
        q_pos = bi * SB_Q_BLOCK + jnp.arange(SB_Q_BLOCK)
        z = jnp.einsum('bhqd,bhkd->bhqk', qb, k).astype(jnp.float32) * scale
        past = k_pos[None, :] < q_pos[:, None]
        log_beta = jax.nn.log_sigmoid(z)
        log_keep = jnp.where(past, jax.nn.log_sigmoid(-z), 0.0)
        log_later = lax.cumsum(log_keep, axis=3, reverse=True) - log_keep
        a = jnp.where(past, jnp.exp(log_beta + log_later), 0.0)
        return jnp.einsum('bhqk,bhkd->bhqd', a.astype(v.dtype), v)

    out = lax.map(block, (q_blocks, jnp.arange(n_qb)))
    return jnp.moveaxis(out, 0, 2).reshape(b, h, s, hd)

def causal_depthwise_conv(u, w, bias):
    ch = u.shape[-1]
    out = lax.conv_general_dilated(
        u, w[:, None, :], window_strides=(1,), padding=[(CONV_WIDTH - 1, 0)],
        dimension_numbers=('NWC', 'WIO', 'NWC'), feature_group_count=ch)
    return out + bias

def second_inputs(seed: int = 0) -> dict:
    key = jax.random.key(seed)
    ks = jax.random.split(key, 16)
    f32 = jnp.float32
    nrm = lambda k, shp, sc: jax.random.normal(k, shp, f32) * sc
    return {
        'x': nrm(ks[0], (BATCH, SEQ, D_MODEL), 1.0),
        'c': nrm(ks[1], (BATCH, D_MODEL), 1.0),
        'w_ada': nrm(ks[2], (DEPTH_2, D_MODEL, 6 * D_MODEL), D_MODEL ** -0.5),
        'b_ada': nrm(ks[3], (DEPTH_2, 6 * D_MODEL), 0.02),
        'g_mix': 1.0 + nrm(ks[4], (DEPTH_2, D_MODEL), 0.05),
        'w_in': nrm(ks[5], (DEPTH_2, D_MODEL, IN_WIDTH), D_MODEL ** -0.5),
        'w_br_moba': nrm(ks[6], (DEPTH_2, MOBA_WIDTH, D_MODEL), MOBA_WIDTH ** -0.5),
        'w_br_sb': nrm(ks[7], (DEPTH_2, SB_WIDTH, D_MODEL), SB_WIDTH ** -0.5),
        'w_out': nrm(ks[8], (DEPTH_2, D_MODEL, D_MODEL), D_MODEL ** -0.5),
        'rel_bias': nrm(ks[9], (N_HEADS_MOBA, REL_BUCKETS), 0.5),
        'g_ffn': 1.0 + nrm(ks[10], (DEPTH_2, D_MODEL), 0.05),
        'w_up': nrm(ks[11], (DEPTH_2, D_MODEL, 2 * D_FF_2), D_MODEL ** -0.5),
        'w_conv': nrm(ks[12], (DEPTH_2, CONV_WIDTH, 2 * D_FF_2), CONV_WIDTH ** -0.5),
        'b_conv': nrm(ks[13], (DEPTH_2, 2 * D_FF_2), 0.02),
        'w_down': nrm(ks[14], (DEPTH_2, D_FF_2, D_MODEL), D_FF_2 ** -0.5),
        'g_final': 1.0 + nrm(ks[15], (D_MODEL,), 0.05),
    }

def second_block(x, c, w_ada, b_ada, g_mix, w_in, w_br_moba, w_br_sb, w_out, rel_bias,
              g_ffn, w_up, w_conv, b_conv, w_down, g_final):
    splits = list(np.cumsum([MOBA_WIDTH, MOBA_WIDTH, MOBA_WIDTH, SB_WIDTH, SB_WIDTH, SB_WIDTH]))
    c_act = jax.nn.silu(c)
    for l in range(DEPTH_2):
        mod = c_act @ w_ada[l] + b_ada[l]
        sh_m, sc_m, gt_m, sh_f, sc_f, gt_f = jnp.split(mod, 6, axis=-1)
        h = modulate(rms_norm_2(x, g_mix[l]), sh_m, sc_m)
        proj = jnp.einsum('bsd,de->bse', h, w_in[l])
        qa, ka, va, qb, kb, vb, gate_logits = jnp.split(proj, splits, axis=-1)
        oa = moba_attention(to_heads(qa, N_HEADS_MOBA), to_heads(ka, N_HEADS_MOBA),
                            to_heads(va, N_HEADS_MOBA), rel_bias)
        ob = stick_breaking_attention(to_heads(qb, N_HEADS_SB), to_heads(kb, N_HEADS_SB),
                                      to_heads(vb, N_HEADS_SB))
        ya = jnp.einsum('bse,ed->bsd', merge_heads(oa), w_br_moba[l])
        yb = jnp.einsum('bse,ed->bsd', merge_heads(ob), w_br_sb[l])
        gates = jax.nn.sigmoid(gate_logits.astype(jnp.float32)).astype(x.dtype)
        g_a, g_b = jnp.split(gates, 2, axis=-1)
        mixed = jnp.einsum('bsd,de->bse', g_a * ya + g_b * yb, w_out[l])
        x = x + gt_m[:, None, :] * mixed
        h2 = modulate(rms_norm_2(x, g_ffn[l]), sh_f, sc_f)
        u = jnp.einsum('bsd,df->bsf', h2, w_up[l])
        u = causal_depthwise_conv(u, w_conv[l], b_conv[l])
        u_val, u_gate = jnp.split(u, 2, axis=-1)
        y = jnp.einsum('bsf,fd->bsd', jax.nn.gelu(u_gate) * u_val, w_down[l])
        x = x + gt_f[:, None, :] * y
    return rms_norm_2(x, g_final)


def setup_inputs(seed=0):
    out = dict(first_inputs(seed))
    for name, value in second_inputs(seed + 1).items():
        if name != "x":
            out[name + "_2"] = value
    return out


def reference(
    x, positions, attn_pre_g, attn_post_g, ffn_pre_g, ffn_post_g, ffn_w_gate, ffn_w_up,
    ffn_w_down, mla_w_a, mla_g_q, mla_w_uq, mla_g_kv, mla_w_ukv, mla_w_o, kv_src_g, w_kv_shared,
    b_w_q, b_rel_table, b_w_o, c_2, w_ada_2, b_ada_2, g_mix_2, w_in_2, w_br_moba_2, w_br_sb_2,
    w_out_2, rel_bias_2, g_ffn_2, w_up_2, w_conv_2, b_conv_2, w_down_2, g_final_2,
):
    x = first_block(
        x, positions, attn_pre_g, attn_post_g, ffn_pre_g, ffn_post_g, ffn_w_gate, ffn_w_up,
        ffn_w_down, mla_w_a, mla_g_q, mla_w_uq, mla_g_kv, mla_w_ukv, mla_w_o, kv_src_g,
        w_kv_shared, b_w_q, b_rel_table, b_w_o,
    )
    return second_block(
        x, c_2, w_ada_2, b_ada_2, g_mix_2, w_in_2, w_br_moba_2, w_br_sb_2, w_out_2, rel_bias_2,
        g_ffn_2, w_up_2, w_conv_2, b_conv_2, w_down_2, g_final_2,
    )


_drawn_inputs = setup_inputs


def setup_inputs(seed=0):
    import zlib

    import numpy as np

    out = dict(_drawn_inputs(seed))
    spreads = {}
    factors = {'b_ada_2': 3.148, 'g_mix_2': 5.045, 'rel_bias_2': 3.852, 'g_ffn_2': 2.79, 'b_conv_2': 8.0}
    for name, (base, spread) in spreads.items():
        noise = np.random.default_rng([zlib.crc32(name.encode()), seed]).standard_normal(out[name].shape)
        drawn = base * np.exp(spread * noise) if base else spread * noise
        out[name] = __import__('jax').numpy.asarray(drawn.astype(out[name].dtype))
    for name, factor in factors.items():
        out[name] = (out[name] * factor).astype(out[name].dtype)
    return out
```

```python
from contextlib import ExitStack

import numpy as np
import concourse.bass as bass
from concourse import mybir

F32 = mybir.dt.float32
F32R = mybir.dt.float32r
I32 = mybir.dt.int32
ALU = mybir.AluOpType
ACT = mybir.ActivationFunctionType

T = 256
P = 128
D = 1024
FF = 2816
NF = FF // P
PIECE = 16
RAW = 4
SPLIT = 3
EPS = 1e-6
NEG = -1e30
C1 = 6.28125
C2 = float(np.float32(0.0019353071795864769).view(np.uint32) & 0xFFFFF000 and
           (np.array([np.float32(0.0019353071795864769).view(np.uint32) & 0xFFFFE000], np.uint32).view(np.float32)[0]))
C3 = float(2.0 * np.pi - C1 - C2)
MAGIC = 12582912.0

COLS = {}
_at = 0
for _name, _n in (("pre0", 8), ("pre1", 8), ("post0", 8), ("post1", 8), ("fpre0", 8), ("fpre1", 8), ("fpost0", 8),
                  ("fpost1", 8), ("kvsrc", 8), ("gq", 3), ("gkv", 2), ("gmix", 8), ("gffn", 8), ("gfin", 8), ("c", 8),
                  ("bada", 48), ("cw0", 44), ("cw1", 44), ("cw2", 44), ("cb", 44), ("inv", 1)):
    COLS[_name] = (_at, _n)
    _at += _n
NCOL = _at

STREAM = [("wa", 56), ("wuk", 16), ("wuv", 16), ("wuq", 36), ("wo0", 64), ("gu0", 352), ("dn0", 176),
          ("wkv_v", 64), ("wkv_k", 64), ("wq1", 64), ("wo1", 64), ("gu1", 352), ("dn1", 176),
          ("win_v", 64), ("win_k", 64), ("win_q", 64), ("win_g", 128), ("wbr", 64), ("wout", 64),
          ("up2", 704 // 2), ("dn2", 176)]


class Lane:

    def __init__(self, name, sem):
        self.name, self.sem, self.count, self.ops, self.seen = name, sem, 0, [], {}

    def wait(self, *tokens):
        for t in tokens:
            if t is None:
                continue
            if isinstance(t, list):
                self.wait(*t)
                continue
            sem, value = t
            if self.seen.get(id(sem), 0) < value:
                self.seen[id(sem)] = value
                self.ops.append(lambda e, s=sem, v=value: e.wait_ge(s, v))

    def do(self, fn, mark=True):
        if not mark:
            self.ops.append(fn)
            return None
        self.count += 1
        self.ops.append(lambda e: fn(e).then_inc(self.sem, 1))
        return (self.sem, self.count)

    def dma(self, out, src, sem, value):
        self.ops.append(lambda e: e.dma_start(out, src).then_inc(sem, 16))
        return (sem, value)

    def play(self, e):
        for op in self.ops:
            op(e)


class Pool:

    def __init__(self, items):
        self.free = [(x, []) for x in items]

    def get(self):
        assert self.free, "no buffer is free"
        return self.free.pop(0)

    def put(self, item, *readers):
        self.free.append((item, list(readers)))


def build(nc, a):
    ctx = ExitStack()
    with ctx:
        def sb(name, shape, dt=F32, scope=ctx):
            return scope.enter_context(nc.sbuf_tensor("s_" + name, shape, dt))

        def sem(name):
            return ctx.enter_context(nc.semaphore(name))

        pe, act, dve, pool, sp = (Lane(n, sem("done_" + n)) for n in ("pe", "act", "dve", "pool", "sp"))

        raw = [sb(f"raw{i}", [P, PIECE * P]) for i in range(RAW)]
        whi = [sb(f"whi{i}", [P, PIECE * P], F32R) for i in range(SPLIT)]
        wlo = [sb(f"wlo{i}", [P, PIECE * P], F32R) for i in range(SPLIT)]
        xT = sb("xT", [P, 8, T])
        hh = sb("hh", [P, 8, T], F32R)
        hl = sb("hl", [P, 8, T], F32R)
        yb = sb("yb", [P, 8, T])
        adacc = sb("adacc", [P, 2048])
        cols = sb("cols", [P, NCOL])
        modv = sb("modv", [P, 48])
        cact = sb("cact", [P, 8])
        gs2 = sb("gs2", [P, 16])
        mask0 = sb("mask0", [P, T])
        ones = sb("ones", [P, P])
        tri = sb("tri", [P, P])
        negones = sb("negones", [P, P])
        ident = sb("ident", [P, P])
        Rt = Pool([sb(f"R{i}", [P, T + 2]) for i in range(3)])
        Lt = Pool([sb(f"L{i}", [P, T + 2]) for i in range(1)])
        sqacc = Pool([sb(f"sqacc{i}", [P, T]) for i in range(3)])
        tmp = Pool([sb(f"tmp{i}", [P, T]) for i in range(10)])
        small = Pool([sb(f"small{i}", [P, 8]) for i in range(6)])

        banks = Pool([ctx.enter_context(nc.psum_tensor(f"bank{i}", [P, 512], F32)) for i in range(8)])

        s_raw = [sem(f"s_raw{i}") for i in range(RAW)]
        s_in = [sem(f"s_in{i}") for i in range(6)]
        s_out = sem("s_out")

        def col(name, j=0, n=1):
            at = COLS[name][0] + j
            return cols[:, at:at + n]

        t_x = sp.dma(xT[:, :, :], a["xT"], s_in[0], 16)
        t_cols = sp.dma(cols[:, :], a["cols"], s_in[1], 16)

        pieces = []
        for name, n in STREAM:
            at = 0
            while at < n:
                k = min(PIECE, n - at)
                pieces.append(("w", name, at, k))
                at += k
        ada = [("ada", "wada", i * PIECE, PIECE) for i in range(24)]
        merged = []
        fed = 0
        for p in pieces:
            merged.append(p)
            if p[1] in ("gu0", "dn0", "gu1", "dn1"):
                fed += 1
                if fed % 2 == 0 and ada:
                    merged.append(ada.pop(0))
        assert not ada
        pieces = merged
        wants = {"dma": 0, "split": 0, "use": 0}
        slot_readers = [[] for _ in range(RAW)]
        split_free = Pool(list(range(SPLIT)))
        ready = {}
        acc_readers = [None]
        ada_done = {}

        def load_next():
            i = wants["dma"]
            _, name, at, k = pieces[i]
            sp.wait(*slot_readers[i % RAW])
            sp.dma(raw[i % RAW][:, 0:k * P], a[name][:, at * P * P:(at + k) * P * P].rearrange("a (p n) -> (a p) n", p=P),
                   s_raw[i % RAW], 0)
            wants["dma"] += 1

        def arrived(i):
            return (s_raw[i % RAW], 16 * (i // RAW + 1))

        def split_next():
            i = wants["split"]
            while wants["dma"] < len(pieces) and wants["dma"] < i + RAW:
                load_next()
            kind, _, at, k = pieces[i]
            src = raw[i % RAW]
            if kind == "ada":
                step = at // PIECE
                kc = step % 8
                dve.wait(arrived(i), t_cact)
                if kc == 0:
                    dve.wait(acc_readers[0])
                    t = dve.do(lambda e: e.tensor_scalar(adacc[:, :], src[:, :], cact[:, 0:1], None, ALU.mult))
                else:
                    dve.wait(ada_done["t"])
                    t = dve.do(lambda e: e.scalar_tensor_tensor(out=adacc[:, :], in0=src[:, :],
                                                                scalar=cact[:, kc:kc + 1], in1=adacc[:, :],
                                                                op0=ALU.mult, op1=ALU.add))
                ada_done["t"] = t
                slot_readers[i % RAW] = [t]
                wants["split"] += 1
                if kc == 7:
                    ada_sum(step // 8, t)
                return
            s, free = split_free.get()
            w = k * P
            act.wait(arrived(i), *free)
            t_hi = act.do(lambda e: e.activation(whi[s][:, 0:w], src[:, 0:w], ACT.Copy))
            dve.wait(arrived(i), t_hi, *free)
            t_lo = dve.do(lambda e: e.tensor_tensor(wlo[s][:, 0:w], src[:, 0:w], whi[s][:, 0:w].bitcast(F32),
                                                    ALU.subtract))
            slot_readers[i % RAW] = [t_hi, t_lo]
            ready[i] = (s, t_hi, t_lo)
            wants["split"] += 1

        def ada_sum(g, t_acc):
            bank, free = banks.get()
            pe.wait(t_acc, t_const, *free)
            for j in range(16):
                t = pe.do(lambda e, j=j: e.matmul(bank[:, j:j + 1], adacc[:, j * P:(j + 1) * P], ones[:, 0:1],
                                                  start=True, stop=True), mark=(j == 15))
            acc_readers[0] = t
            dve.wait(t, t_cols)
            t2 = dve.do(lambda e: e.tensor_tensor(modv[:, g * 16:(g + 1) * 16], bank[:, 0:16],
                                                  col("bada", g * 16, 16), ALU.add))
            banks.put(bank, t2)
            mod_ready[g] = t2

        mod_ready = {}

        class Weights:

            def __init__(self, name):
                self.name, self.left, self.at, self.i = name, 0, 0, None

            def tile(self, n=1):
                if self.left == 0:
                    i = wants["use"]
                    while pieces[i][0] == "ada":
                        i += 1
                    assert pieces[i][1] == self.name, (pieces[i], self.name)
                    ahead = i
                    count = 0
                    while ahead < len(pieces) and count < SPLIT:
                        if pieces[ahead][0] == "w":
                            count += 1
                        ahead += 1
                    while wants["split"] < ahead and (split_free.free or pieces[wants["split"]][0] == "ada"):
                        split_next()
                    self.i, self.left, self.at = i, pieces[i][3], 0
                    wants["use"] = i + 1
                    s, t_hi, t_lo = ready[i]
                    pe.wait(t_hi, t_lo)
                    self.s = s
                at = self.at
                self.at += n
                self.left -= n
                return (whi[self.s][:, at * P:(at + n) * P], wlo[self.s][:, at * P:(at + n) * P])

            def used(self, t):
                split_free.put(self.s, t)

        def product(wts, nk, xh, xl, out, t_x):
            for k in range(nk):
                hi, lo = wts.tile()
                pe.wait(*t_x[k])
                a_h, a_l = xh[:, k, :], xl[:, k, :]
                pe.do(lambda e, hi=hi, a_h=a_h, k=k: e.matmul(out, hi, a_h, start=(k == 0), stop=False), mark=False)
                pe.do(lambda e, hi=hi, a_l=a_l: e.matmul(out, hi, a_l, start=False, stop=False), mark=False)
                last = wts.left == 0 or k == nk - 1
                t = pe.do(lambda e, lo=lo, a_h=a_h, k=k: e.matmul(out, lo, a_h, start=False, stop=(k == nk - 1)),
                          mark=last)
                if wts.left == 0:
                    wts.used(t)
            return t

        background = [None]

        def step():
            if background[0] is not None:
                try:
                    next(background[0])
                except StopIteration:
                    background[0] = None

        def drain():
            n = 0
            while background[0] is not None:
                step()
                n += 1
                assert n < 10000, "the background is stuck"

        def gemm(name, ntiles, nk, xh, xl, t_x, evac, per_bank=2, steps=0):
            wts = Weights(name)
            n = 0
            while n < ntiles:
                m = min(per_bank, ntiles - n)
                bank, free = banks.get()
                pe.wait(*free)
                for j in range(m):
                    t = product(wts, nk, xh, xl, bank[:, j * T:(j + 1) * T], t_x)
                    for _ in range(steps):
                        step()
                readers = evac(n, m, bank, t)
                banks.put(bank, *readers)
                n += m

        def gemm_tokens(name, ngroups, nk, xh, xl, t_x, evac):
            wts = Weights(name)
            for g in range(ngroups):
                b0, f0 = banks.get()
                b1, f1 = banks.get()
                pe.wait(*f0, *f1)
                for k in range(nk):
                    hi, lo = wts.tile(4)
                    pe.wait(*t_x[k])
                    for tb, bank in ((0, b0), (1, b1)):
                        a_h, a_l = xh[:, k, tb * P:(tb + 1) * P], xl[:, k, tb * P:(tb + 1) * P]
                        pe.do(lambda e, b=bank, x=a_h, w=hi, k=k: e.matmul(b[:, :], x, w, start=(k == 0), stop=False),
                              mark=False)
                        pe.do(lambda e, b=bank, x=a_h, w=lo: e.matmul(b[:, :], x, w, start=False, stop=False),
                              mark=False)
                        t = pe.do(lambda e, b=bank, x=a_l, w=hi, k=k: e.matmul(b[:, :], x, w, start=False,
                                                                               stop=(k == nk - 1)))
                    if wts.left == 0:
                        wts.used(t)
                for tb, bank in ((0, b0), (1, b1)):
                    banks.put(bank, *evac(g, tb, bank, t))

        def t_pe_now():
            return (pe.sem, pe.count)

        class Stat:

            def __init__(self):
                self.acc, self.free = sqacc.get()
                self.t = None

            def add(self, src, t_src):
                if self.t is None:
                    act.wait(t_src, *self.free)
                    self.t = act.do(lambda e: e.activation(self.acc[:, :], src, ACT.Square))
                    return self.t
                sq, free = tmp.get()
                act.wait(t_src, *free)
                t = act.do(lambda e: e.activation(sq[:, :], src, ACT.Square))
                dve.wait(t, self.t)
                self.t = dve.do(lambda e: e.tensor_tensor(self.acc[:, :], self.acc[:, :], sq[:, :], ALU.add))
                tmp.put(sq, self.t)
                return t

            def finish(self, n):
                bank, free = banks.get()
                pe.wait(self.t, t_const, *free)
                acc = self.acc
                pe.do(lambda e: e.matmul(bank[:, 0:T], ones[:, :], acc[:, :], start=True, stop=True), mark=False)
                pe.do(lambda e: e.matmul(bank[:, T:T + 1], acc[:, 0:P], ones[:, 0:1], start=True, stop=True),
                      mark=False)
                t = pe.do(lambda e: e.matmul(bank[:, T + 1:T + 2], acc[:, P:T], ones[:, 0:1], start=True, stop=True))
                sqacc.put(acc, t)
                R, rfree = Rt.get()
                log, lfree = Lt.get()
                act.wait(t, t_const, *lfree)
                t1 = act.do(lambda e: e.activation(log[:, :], bank[:, 0:T + 2], ACT.Ln, scale=1.0 / n,
                                                   bias=epsc[:, 0:1]))
                banks.put(bank, t1)
                act.wait(t1, *rfree)
                t2 = act.do(lambda e: e.activation(R[:, :], log[:, :], ACT.Exp, scale=-0.5))
                Lt.put(log, t2)
                return R, t2

        def split_scaled(src, gain, oh, ol, t_src, free=()):
            act.wait(t_src, t_cols, *free)
            t_h = act.do(lambda e: e.activation(oh, src, ACT.Copy, scale=gain))
            dve.wait(t_h, t_src, t_cols, *free)
            t_l = dve.do(lambda e: e.scalar_tensor_tensor(out=ol, in0=src, scalar=gain, in1=oh.bitcast(F32),
                                                          op0=ALU.mult, op1=ALU.subtract))
            return (t_h, t_l)

        def split_plain(src, oh, ol, t_src, free=()):
            act.wait(t_src, *free)
            t_h = act.do(lambda e: e.activation(oh, src, ACT.Copy))
            dve.wait(t_h, t_src, *free)
            t_l = dve.do(lambda e: e.tensor_tensor(ol, src, oh.bitcast(F32), ALU.subtract))
            return (t_h, t_l)

        def add_normed(y, t_y, gain, R, t_r, free, then):
            for j in range(8):
                u, ufree = tmp.get()
                dve.wait(t_y[j], t_r, *ufree)
                t1 = dve.do(lambda e, j=j, u=u: e.scalar_tensor_tensor(out=u[:, :], in0=y[:, j, :],
                                                                       scalar=col(gain, j), in1=R[:, 0:T],
                                                                       op0=ALU.mult, op1=ALU.mult))
                dve.wait(t1, *free)
                t2 = dve.do(lambda e, j=j, u=u: e.tensor_tensor(xT[:, j, :], xT[:, j, :], u[:, :], ALU.add))
                tmp.put(u, t2)
                then(j, t2)
            return t2

        epsc = sb("epsc", [P, 2])
        pool.do(lambda e: e.memset(epsc[:, 0:1], EPS), mark=False)
        pool.do(lambda e: e.memset(epsc[:, 1:2], float(np.pi / 2)), mark=False)
        pool.do(lambda e: e.memset(ones[:, :], 1.0), mark=False)
        pool.do(lambda e: e.memset(negones[:, :], -1.0), mark=False)
        pool.do(lambda e: e.memset(mask0[:, :], 0.0), mark=False)
        pool.do(lambda e: e.memset(ident[:, :], 0.0), mark=False)
        t_set = pool.do(lambda e: e.memset(tri[:, :], -1.0))
        pool.wait(t_set)
        pool.do(lambda e: e.memset(mask0[0:64, 192:256], NEG), mark=False)
        pool.do(lambda e: e.affine_select(out=ident[:, :], in_=ident[:, :], compare_op=ALU.not_equal, fill=1.0,
                                          base=0, pattern=[[-1, P]], channel_multiplier=1), mark=False)
        t_const = pool.do(lambda e: e.affine_select(out=tri[:, :], in_=tri[:, :], compare_op=ALU.is_ge, fill=0.0,
                                                    base=0, pattern=[[-1, P]], channel_multiplier=1))

        act.wait(t_cols)
        t_cact = act.do(lambda e: e.activation(cact[:, :], col("c", 0, 8), ACT.Silu))

        att = ExitStack()
        cosb, sinb, posi = adacc[:, 0:T], adacc[:, T:2 * T], adacc[:, 2 * T:3 * T].bitcast(I32)
        cq = yb
        cqh = sb("cqh", [P, 5, T], F32R, scope=att)
        cql = sb("cql", [P, 5, T], F32R, scope=att)

        def attention_buffers(scope, tag, nq, nk_):
            return dict(
                Q=sb("Q" + tag, [P, nq, T], scope=scope), K=sb("K" + tag, [P, nk_, T], scope=scope),
                V=sb("V" + tag, [P, 2, 1024], scope=scope),
                S=Pool([sb(f"S{tag}{i}", [P, 384], scope=scope) for i in range(3)]),
                PT=Pool([sb(f"PT{tag}{i}", [P, 384], scope=scope) for i in range(2)]),
                O=Pool([sb(f"O{tag}{i}", [P, 2, P], scope=scope) for i in range(2)]),
                oh=sb("oh" + tag, [P, 8, T], F32R, scope=scope), ol=sb("ol" + tag, [P, 8, T], F32R, scope=scope))

        A = attention_buffers(att, "0", 12, 10)
        Q0, K0, V0 = A["Q"], A["K"], A["V"]

        t_pos = sp.dma(posi, a["pos"], s_in[2], 16)

        def rope_table():
            ang, f1 = tmp.get()
            k_, f2 = tmp.get()
            r_, f3 = tmp.get()
            dve.wait(t_pos, t_cols, *f1, *f2, *f3)
            t = dve.do(lambda e: e.tensor_copy(r_[:, :], posi))
            dve.wait(t)
            t = dve.do(lambda e: e.tensor_scalar(ang[:, :], r_[:, :], col("inv"), None, ALU.mult))
            dve.wait(t)
            t = dve.do(lambda e: e.tensor_scalar(k_[:, :], ang[:, :], float(1 / (2 * np.pi)), MAGIC, ALU.mult,
                                                 ALU.add))
            dve.wait(t)
            t = dve.do(lambda e: e.tensor_scalar(k_[:, :], k_[:, :], -MAGIC, None, ALU.add))
            src, dst = ang, r_
            for c in (C1, C2, C3):
                dve.wait(t)
                t = dve.do(lambda e, c=c, s=src, d=dst: e.scalar_tensor_tensor(
                    out=d[:, :], in0=k_[:, :], scalar=-c, in1=s[:, :], op0=ALU.mult, op1=ALU.add))
                src, dst = dst, src
            dve.wait(t)
            t = dve.do(lambda e, s=src: e.tensor_scalar(s[:, :], s[:, :], 3.1415925, -3.1415925, ALU.min, ALU.max))
            act.wait(t, t_const)
            t1 = act.do(lambda e, s=src: e.activation(sinb, s[:, :], ACT.Sin))
            t2 = act.do(lambda e, s=src, d=dst: e.activation(d[:, :], s[:, :], ACT.Abs))
            act.wait(t2)
            t3 = act.do(lambda e, d=dst: e.activation(cosb, d[:, :], ACT.Sin, scale=-1.0, bias=epsc[:, 1:2]))
            for b in (ang, k_, r_):
                tmp.put(b, t1, t3)
            return [t1, t3]

        t_rope = rope_table()

        t_h = [split_scaled(xT[:, k, :], col("pre0", k), hh[:, k, :], hl[:, k, :], t_x) for k in range(8)]
        stat = Stat()
        for k in range(8):
            stat.add(xT[:, k, :], t_x)
        R0, t_R0 = stat.finish(D)

        def scaled(dst, src, R, t_src, t_r, free=()):
            dve.wait(t_src, t_r, *free)
            return dve.do(lambda e: e.tensor_tensor(dst, src, R[:, 0:T], ALU.mult))

        stat_q, stat_kv = Stat(), Stat()
        t_cq = [None] * 5
        krt = []

        def evac_a(n, m, bank, t):
            out = []
            for j in range(m):
                f = n + j
                src = bank[:, j * T:(j + 1) * T]
                if f < 5:
                    t1 = scaled(cq[:, f, :], src, R0, t, t_R0)
                    (stat_q if f < 3 else stat_kv).add(cq[:, f, :], t1)
                    t_cq[f] = split_scaled(cq[:, f, :], col("gq", f) if f < 3 else col("gkv", f - 3), cqh[:, f, :],
                                           cql[:, f, :], t1)
                else:
                    b, free = tmp.get()
                    t1 = scaled(b[:, :], src, R0, t, t_R0, free)
                    krt.append((b, t1))
                out.append(t1)
            return out

        gemm("wa", 7, 8, hh, hl, t_h, evac_a)
        t_R0_used = krt[-1][1]

        def rotate(a1, a2, o1, o2, t_in):
            u, fu = tmp.get()
            v, fv = tmp.get()
            dve.wait(t_in, t_rope, *fu, *fv)
            t1 = dve.do(lambda e: e.tensor_tensor(u[:, :], a2, sinb, ALU.mult))
            t2 = dve.do(lambda e: e.tensor_tensor(v[:, :], a1, sinb, ALU.mult))
            t3 = dve.do(lambda e: e.tensor_tensor(o1, a1, cosb, ALU.mult))
            t4 = dve.do(lambda e: e.tensor_tensor(o2, a2, cosb, ALU.mult))
            dve.wait(t3)
            t5 = dve.do(lambda e: e.tensor_tensor(o1, o1, u[:, :], ALU.subtract))
            dve.wait(t4)
            t6 = dve.do(lambda e: e.tensor_tensor(o2, o2, v[:, :], ALU.add))
            tmp.put(u, t5)
            tmp.put(v, t6)
            return t6

        (k1b, tk1), (k2b, tk2) = krt
        t_krope = rotate(k1b[:, :], k2b[:, :], K0[:, 8, :], K0[:, 9, :], tk2)
        tmp.put(k1b, t_krope)
        tmp.put(k2b, t_krope)
        Rkv, t_Rkv = stat_kv.finish(256)
        Rq, t_Rq = stat_q.finish(384)

        t_K, t_V, t_Q = {}, {}, {}

        def evac_into(dst, toks, R, t_r, free=(), base=0):
            def evac(n, m, bank, t):
                dve.wait(t, t_r, *free)
                out = []
                for j in range(m):
                    tt = dve.do(lambda e, j=j: e.tensor_tensor(dst[:, base + n + j, :], bank[:, j * T:(j + 1) * T],
                                                               R[:, 0:T], ALU.mult))
                    toks[n + j] = tt
                    out.append(tt)
                return out
            return evac

        def evac_tokens(dst, toks, R, t_r, free=()):
            def evac(g, tb, bank, t):
                act.wait(t, t_r, *free)
                if R is None:
                    tt = act.do(lambda e: e.activation(dst[:, tb, g * 512:(g + 1) * 512], bank[:, :], ACT.Copy))
                else:
                    tt = act.do(lambda e: e.activation(dst[:, tb, g * 512:(g + 1) * 512], bank[:, :], ACT.Copy,
                                                       scale=R[:, T + tb:T + tb + 1]))
                toks[g] = tt
                return [tt]
            return evac

        gemm("wuk", 8, 2, cqh[:, 3:5, :], cql[:, 3:5, :], t_cq[3:5], evac_into(K0, t_K, Rkv, t_Rkv))
        gemm_tokens("wuv", 2, 2, cqh[:, 3:5, :], cql[:, 3:5, :], t_cq[3:5], evac_tokens(V0, t_V, Rkv, t_Rkv))

        def out_chunk(A, c, o, t_o):
            bank, free = banks.get()
            pe.wait(t_o, t_const, *free)
            pe.do(lambda e: e.transpose(bank[:, 0:P], o[:, 0, :], ident[:, :]), mark=False)
            t = pe.do(lambda e: e.transpose(bank[:, P:T], o[:, 1, :], ident[:, :]))
            A["O"].put(o, t)
            oh, ol = A["oh"][:, c, :], A["ol"][:, c, :]
            t_hl = split_plain(bank[:, 0:T], oh, ol, t)
            banks.put(bank, *t_hl)
            A["t_o"][c] = t_hl

        def values(A, h, dv, v0, left, right, t_in, scale, release):
            bank, free = banks.get()
            pe.wait(t_in, *free)
            pe.wait(*A["t_v"](h))
            VL = A["V"]
            p = left
            pe.do(lambda e: e.matmul(bank[:, 0:dv], p[:, 0:P], VL[:, 0, v0:v0 + dv], start=True, stop=True),
                  mark=False)
            pe.do(lambda e: e.matmul(bank[:, dv:2 * dv], p[:, P:T], VL[:, 0, v0:v0 + dv], start=True, stop=False),
                  mark=False)
            t = pe.do(lambda e: e.matmul(bank[:, dv:2 * dv], p[:, T:384], VL[:, 1, v0:v0 + dv], start=False,
                                         stop=True))
            release(t)
            per = P // dv
            if h % per == 0:
                A["o_now"] = A["O"].get()
                A["o_toks"] = []
            o, ofree = A["o_now"]
            at = (h % per) * dv
            toks = []
            for qb in range(2):
                dve.wait(t, *ofree)
                if scale is None:
                    tt = dve.do(lambda e, qb=qb: e.tensor_copy(o[:, qb, at:at + dv], bank[:, qb * dv:(qb + 1) * dv]))
                else:
                    rinv, t_rinv = scale
                    dve.wait(t_rinv)
                    tt = dve.do(lambda e, qb=qb: e.tensor_scalar(o[:, qb, at:at + dv], bank[:, qb * dv:(qb + 1) * dv],
                                                                 rinv[:, qb:qb + 1], None, ALU.mult))
                toks.append(tt)
            banks.put(bank, tt)
            A["o_toks"] += toks
            return h % per == per - 1, o, A["o_toks"], tt

        def soft_scores(A, h, parts, t_in, bias, scale):
            bank, free = banks.get()
            pe.wait(t_in, *free)
            n = len(parts)
            for i, (q, k) in enumerate(parts):
                t = pe.do(lambda e, q=q, k=k, i=i: e.matmul(bank[:, 0:P], q[:, 0:P], k[:, 0:P], start=(i == 0),
                                                            stop=(i == n - 1)), mark=False)
            for i, (q, k) in enumerate(parts):
                t = pe.do(lambda e, q=q, k=k, i=i: e.matmul(bank[:, P:384], q[:, P:T], k, start=(i == 0),
                                                            stop=(i == n - 1)), mark=(i == n - 1))
            s, sfree = A["S"].get()
            w, wfree = small.get()
            dve.wait(t, A["t_bias"], *sfree, *wfree)
            dve.do(lambda e: e.tensor_tensor_reduce(out=s[:, 0:P], in0=bank[:, 0:P], in1=bias[:, P:T], scale=1.0,
                                                    scalar=-3e38, op0=ALU.add, op1=ALU.max, accum_out=w[:, 0:1]))
            t1 = dve.do(lambda e: e.tensor_tensor_reduce(out=s[:, P:384], in0=bank[:, P:384], in1=bias[:, 0:T],
                                                         scale=1.0, scalar=-3e38, op0=ALU.add, op1=ALU.max,
                                                         accum_out=w[:, 1:2]))
            banks.put(bank, t1)
            dve.wait(t1)
            t2 = dve.do(lambda e: e.tensor_scalar(w[:, 2:4], w[:, 0:2], -scale, None, ALU.mult))
            act.wait(t2)
            act.do(lambda e: e.activation(s[:, 0:P], s[:, 0:P], ACT.Exp, scale=scale, bias=w[:, 2:3],
                                          accum_out=w[:, 4:5]))
            t3 = act.do(lambda e: e.activation(s[:, P:384], s[:, P:384], ACT.Exp, scale=scale, bias=w[:, 3:4],
                                               accum_out=w[:, 5:6]))
            return s, w, t3

        def soft_values(A, h, dv, v0, got):
            s, w, t3 = got
            bank, free = banks.get()
            pe.wait(t3, t_const, *free)
            for i in range(3):
                t = pe.do(lambda e, i=i: e.transpose(bank[:, i * P:(i + 1) * P], s[:, i * P:(i + 1) * P],
                                                     ident[:, :]), mark=(i == 2))
            A["S"].put(s, t)
            pt, pfree = A["PT"].get()
            act.wait(t, *pfree)
            t4 = act.do(lambda e: e.activation(pt[:, :], bank[:, 0:384], ACT.Copy))
            banks.put(bank, t4)
            dve.wait(t3)
            t5 = dve.do(lambda e: e.reciprocal(w[:, 6:8], w[:, 4:6]))
            yield
            full, o, toks, last = values(A, h, dv, v0, pt, None, t4, (w[:, 6:8], t5), lambda t: A["PT"].put(pt, t))
            small.put(w, last)
            if full:
                yield
                out_chunk(A, h * dv // P, o, toks)

        def soft_attention(A, heads, dv, parts_of, scale):
            before = None
            for h in heads:
                while not A["have"](h):
                    yield
                parts, t_in, bias = parts_of(h)
                now = (h, soft_scores(A, h, parts, t_in, bias, scale))
                yield
                if before is not None:
                    yield from soft_values(A, before[0], dv, A["v0"](before[0]), before[1])
                    yield
                before = now
            yield from soft_values(A, before[0], dv, A["v0"](before[0]), before[1])

        t_qr = {}

        def mla_parts(h):
            g = h % 4
            c = h // 4
            lo, hi = 32 * g, 32 * g + 32
            return ([(Q0[:, h, :], K0[:, h, :]), (Q0[lo:hi, 8 + c, :], K0[lo:hi, 8, :]),
                     (Q0[lo:hi, 10 + c, :], K0[lo:hi, 9, :])], [t_Q[h], t_K[h], t_qr[c], t_krope], mask0)

        A.update(t_o=[None] * 8, t_v=lambda h: [t_V[h // 4]], v0=lambda h: h * P, t_bias=t_const,
                 have=lambda h: h in t_Q and (h // 4) in t_qr)
        background[0] = soft_attention(A, range(8), P, mla_parts, float(192.0 ** -0.5))

        ORDER = [8, 10, 9, 11, 0, 1, 2, 3, 4, 5, 6, 7]

        def evac_q(n, m, bank, t):
            out = []
            dve.wait(t, t_Rq)
            for j in range(m):
                d = ORDER[n + j]
                tt = dve.do(lambda e, j=j, d=d: e.tensor_tensor(Q0[:, d, :], bank[:, j * T:(j + 1) * T], Rq[:, 0:T],
                                                                ALU.mult))
                if d < 8:
                    t_Q[d] = tt
                out.append(tt)
            if n < 4:
                c = n // 2
                u, fu = tmp.get()
                v, fv = tmp.get()
                q1, q2 = Q0[:, 8 + c, :], Q0[:, 10 + c, :]
                dve.wait(tt, t_rope, *fu, *fv)
                dve.do(lambda e: e.tensor_tensor(u[:, :], q2, sinb, ALU.mult), mark=False)
                t2 = dve.do(lambda e: e.tensor_tensor(v[:, :], q1, sinb, ALU.mult))
                dve.wait(t2)
                dve.do(lambda e: e.tensor_tensor(q1, q1, cosb, ALU.mult), mark=False)
                t4 = dve.do(lambda e: e.tensor_tensor(q2, q2, cosb, ALU.mult))
                dve.wait(t4)
                dve.do(lambda e: e.tensor_tensor(q1, q1, u[:, :], ALU.subtract), mark=False)
                t6 = dve.do(lambda e: e.tensor_tensor(q2, q2, v[:, :], ALU.add))
                tmp.put(u, t6)
                tmp.put(v, t6)
                t_qr[c] = t6
            return out

        gemm("wuq", 12, 3, cqh, cql, t_cq[0:3], evac_q, steps=1)
        drain()
        Rt.put(R0, t_R0_used)
        Rt.put(Rkv, t_V[1], t_K[7])
        Rt.put(Rq, t_Q[7])

        def project_and_add(name, A, t_o, gain, pre):
            t_y = {}
            stat = Stat()

            def evac(n, m, bank, t):
                out = []
                for j in range(m):
                    src = bank[:, j * T:(j + 1) * T]
                    act.wait(t)
                    ty = act.do(lambda e, j=j, src=src: e.activation(yb[:, n + j, :], src, ACT.Copy))
                    ts = stat.add(src, t)
                    t_y[n + j] = ty
                    out += [ty, ts]
                return out

            gemm(name, 8, A["nk"], A["oh"], A["ol"], t_o, evac)
            R, t_r = stat.finish(D)
            t_h = []
            nxt = Stat()

            def then(j, t):
                if pre is not None:
                    t_h.append(split_scaled(xT[:, j, :], col(pre, j), hh[:, j, :], hl[:, j, :], t))
            t_last = []

            def then2(j, t):
                then(j, t)
                t_last.append(t)
            add_normed(yb, t_y, gain, R, t_r, (), then2)
            Rt.put(R, t_last[-1])
            for j in range(8):
                nxt.add(xT[:, j, :], t_last[j])
            R2, t_r2 = nxt.finish(D)
            return t_h, R2, t_r2, t_last

        A["nk"] = 8
        t_h, R1, t_R1, t_xs = project_and_add("wo0", A, A["t_o"], "post0", "fpre0")
        att.close()

        def feed_forward(layer, t_h, R, t_r, pre):
            scope = ExitStack()
            ph = sb(f"ph{layer}", [P, NF, T], F32R, scope=scope)
            pl = sb(f"pl{layer}", [P, NF, T], F32R, scope=scope)
            t_p = [None] * NF
            late = []

            def first(n, bank, t):
                g, fg = tmp.get()
                u, fu = tmp.get()
                dve.wait(t, t_r, *fg, *fu)
                t1 = dve.do(lambda e: e.tensor_tensor(g[:, :], bank[:, 0:T], R[:, 0:T], ALU.mult))
                t2 = dve.do(lambda e: e.tensor_tensor(u[:, :], bank[:, T:2 * T], R[:, 0:T], ALU.mult))
                act.wait(t1)
                t3 = act.do(lambda e: e.activation(g[:, :], g[:, :], ACT.Silu))
                return g, u, t2, t3

            def second(n, g, u, t2, t3):
                dve.wait(t2, t3)
                t4 = dve.do(lambda e: e.tensor_tensor(u[:, :], u[:, :], g[:, :], ALU.mult))
                tmp.put(g, t4)
                act.wait(t4)
                t5 = act.do(lambda e: e.activation(ph[:, n, :], u[:, :], ACT.Copy))
                return u, t5

            def third(n, u, t5):
                dve.wait(t5)
                t6 = dve.do(lambda e: e.tensor_tensor(pl[:, n, :], u[:, :], ph[:, n, :].bitcast(F32), ALU.subtract))
                tmp.put(u, t6)
                t_p[n] = (t5, t6)

            stage2, stage3 = [], []

            def advance(n, item):
                if stage3:
                    third(*stage3.pop(0))
                if stage2:
                    m, *rest = stage2.pop(0)
                    stage3.append((m, *second(m, *rest)))
                if item is not None:
                    stage2.append((n, *item))

            def evac(n, m, bank, t):
                item = first(n // 2, bank, t)
                advance(n // 2, item)
                return [item[2]]

            gemm(f"gu{layer}", 2 * NF, 8, hh, hl, t_h, evac)
            while stage2 or stage3:
                advance(None, None)
            Rt.put(R, t_p[NF - 1][1])
            B = {"nk": NF, "oh": ph, "ol": pl}
            t_h2, R2, t_r2, t_xs = project_and_add(f"dn{layer}", B, t_p, f"fpost{layer}", pre)
            scope.close()
            return t_h2, R2, t_r2, t_xs

        t_h, R2, t_R2, t_xs = feed_forward(0, t_h, R1, t_R1, "kvsrc")

        att = ExitStack()
        A = attention_buffers(att, "1", 8, 8)
        Q1, K1, V1 = A["Q"], A["K"], A["V"]
        bias1 = sb("bias1", [P, 16, T], scope=att)
        sp.wait(t_pe_now())
        t_bias = sp.dma(bias1[:, :, :], a["relb"], s_in[3], 16)
        pool.wait(t_bias)
        t_b8 = pool.do(lambda e: e.tensor_scalar(bias1[:, :, :], bias1[:, :, :], 8.0, None, ALU.mult))
        pool.wait(t_b8)
        t_bm = pool.do(lambda e: e.memset(bias1[0:64, :, 192:256], NEG))
        t_K, t_V, t_Q = {}, {}, {}
        gemm_tokens("wkv_v", 2, 8, hh, hl, t_h, evac_tokens(V1, t_V, R2, t_R2))
        gemm("wkv_k", 8, 8, hh, hl, t_h, evac_into(K1, t_K, R2, t_R2))
        t_h = [split_scaled(xT[:, k, :], col("pre1", k), hh[:, k, :], hl[:, k, :], t_xs[k], (t_K[7],))
               for k in range(8)]

        def b_parts(h, Q1=Q1, K1=K1, t_Q=t_Q, t_K=t_K):
            lo = 64 * (h % 2)
            c = h // 2
            return ([(Q1[lo:lo + 64, c, :], K1[lo:lo + 64, c, :])], [t_Q[c], t_K[c]], bias1[:, h, :])

        A.update(t_o=[None] * 8, t_v=lambda h, t_V=t_V: [t_V[h // 8]], v0=lambda h: h * 64, t_bias=t_bm,
                 have=lambda h, t_Q=t_Q: (h // 2) in t_Q)
        background[0] = soft_attention(A, range(16), 64, b_parts, 0.125)
        gemm("wq1", 8, 8, hh, hl, t_h, evac_into(Q1, t_Q, R2, t_R2), steps=4)
        drain()
        Rt.put(R2, t_Q[7], t_V[1])
        A["nk"] = 8
        t_h, R3, t_R3, t_xs = project_and_add("wo1", A, A["t_o"], "post1", "fpre1")
        att.close()
        t_h, R4, t_R4, t_xs = feed_forward(1, t_h, R3, t_R3, None)

        dve.wait(mod_ready[0], mod_ready[1], mod_ready[2])
        dve.do(lambda e: e.scalar_tensor_tensor(out=gs2[:, 0:8], in0=modv[:, 8:16], scalar=1.0, in1=col("gmix", 0, 8),
                                                op0=ALU.add, op1=ALU.mult))
        t_gs = dve.do(lambda e: e.scalar_tensor_tensor(out=gs2[:, 8:16], in0=modv[:, 32:40], scalar=1.0,
                                                       in1=col("gffn", 0, 8), op0=ALU.add, op1=ALU.mult))

        def modulated(g0, s0, R, t_r, t_xs, free=()):
            out = []
            for j in range(8):
                u, fu = tmp.get()
                dve.wait(t_xs[j], t_r, t_gs, *fu)
                t1 = dve.do(lambda e, j=j, u=u: e.scalar_tensor_tensor(
                    out=u[:, :], in0=xT[:, j, :], scalar=gs2[:, g0 + j:g0 + j + 1], in1=R[:, 0:T], op0=ALU.mult,
                    op1=ALU.mult))
                act.wait(t1, mod_ready[0], mod_ready[1], *free)
                t2 = act.do(lambda e, j=j, u=u: e.activation(hh[:, j, :], u[:, :], ACT.Identity,
                                                             bias=modv[:, s0 + j:s0 + j + 1]))
                dve.wait(t2, t1)
                t3 = dve.do(lambda e, j=j, u=u: e.scalar_tensor_tensor(
                    out=hl[:, j, :], in0=u[:, :], scalar=modv[:, s0 + j:s0 + j + 1], in1=hh[:, j, :].bitcast(F32),
                    op0=ALU.add, op1=ALU.subtract))
                tmp.put(u, t3)
                out.append((t2, t3))
            Rt.put(R, t1)
            return out

        t_h = modulated(0, 0, R4, t_R4, t_xs)
        att = ExitStack()
        A = attention_buffers(att, "2", 8, 8)
        Q2, K2, V2 = A["Q"], A["K"], A["V"]
        gates = yb
        gates2 = adacc
        t_K, t_V, t_Q, t_G = {}, {}, {}, {}
        bias2 = sb("bias2", [P, 8, T], scope=att)
        sp.wait(t_pe_now())
        t_bias2 = sp.dma(bias2[:, :, :], a["relm"], s_in[4], 16)
        pool.wait(t_bias2)
        t_b8 = pool.do(lambda e: e.tensor_scalar(bias2[:, 0:8, :], bias2[:, 0:8, :], 8.0, None, ALU.mult))
        pool.wait(t_b8)
        t_bm2 = pool.do(lambda e: e.affine_select(out=bias2[:, 0:8, :], in_=bias2[:, 0:8, :], compare_op=ALU.is_ge,
                                                  fill=NEG, base=128, pattern=[[0, 8], [-1, T]],
                                                  channel_multiplier=1))

        def evac_copy(dst_of, toks):
            def evac(n, m, bank, t):
                act.wait(t)
                out = []
                for j in range(m):
                    tt = act.do(lambda e, j=j: e.activation(dst_of(n + j), bank[:, j * T:(j + 1) * T], ACT.Copy))
                    toks[n + j] = tt
                    out.append(tt)
                return out
            return evac

        gemm_tokens("win_v", 2, 8, hh, hl, t_h, evac_tokens(V2, t_V, None, None))
        gemm("win_k", 8, 8, hh, hl, t_h, evac_copy(lambda n: K2[:, n, :], t_K))

        def m_parts(h, Q2=Q2, K2=K2, t_Q=t_Q, t_K=t_K):
            lo = 64 * (h % 2)
            c = h // 2
            return ([(Q2[lo:lo + 64, c, :], K2[lo:lo + 64, c, :])], [t_Q[c], t_K[c]], bias2[:, h, :])

        def stick_scores(A, h):
            lo = 64 * (h % 2)
            c = h // 2
            q, k = Q2[lo:lo + 64, c, :], K2[lo:lo + 64, c, :]
            bank, free = banks.get()
            pe.wait(t_Q[c], t_K[c], *free)
            pe.do(lambda e: e.matmul(bank[:, 0:T], k[:, 0:P], q, start=True, stop=True), mark=False)
            t = pe.do(lambda e: e.matmul(bank[:, T:384], k[:, P:T], q[:, P:T], start=False, stop=True,
                                         skip_group_check=True))
            s, sfree = A["S"].get()
            r, rfree = A["PT"].get()
            act.wait(t, *sfree)
            t1 = act.do(lambda e: e.activation(s[:, :], bank[:, 0:384], ACT.Abs))
            act.wait(t1)
            t2 = act.do(lambda e: e.activation(s[:, :], s[:, :], ACT.Exp, scale=-0.125))
            act.wait(t2)
            t3 = act.do(lambda e: e.activation(s[:, :], s[:, :], ACT.Ln, bias=ones[:, 0:1]))
            dve.wait(t1, *rfree)
            t4 = dve.do(lambda e: e.tensor_scalar(r[:, :], bank[:, 0:384], 0.0, None, ALU.max))
            dve.wait(t3, t4)
            t5 = dve.do(lambda e: e.scalar_tensor_tensor(out=r[:, :], in0=s[:, :], scalar=8.0, in1=r[:, :],
                                                         op0=ALU.mult, op1=ALU.add))
            A["S"].put(s, t5)
            t6 = past_only(r, t5)
            return bank, r, [t1, t4, t6]

        def past_only(r, t):
            pool.wait(t)
            pool.do(lambda e: e.affine_select(out=r[:, 0:P], in_=r[:, 0:P], compare_op=ALU.is_gt, fill=0.0,
                                              base=0, pattern=[[1, P]], channel_multiplier=-1), mark=False)
            return pool.do(lambda e: e.affine_select(out=r[:, T:384], in_=r[:, T:384], compare_op=ALU.is_gt, fill=0.0,
                                                     base=0, pattern=[[1, P]], channel_multiplier=-1))

        def stick_sums(A, got):
            bank, r, toks = got
            pe.wait(toks, t_const)
            pe.do(lambda e: e.matmul(bank[:, 0:T], tri[:, :], r[:, 0:T], start=False, stop=False,
                                     skip_group_check=True), mark=False)
            pe.do(lambda e: e.matmul(bank[:, P:T], negones[:, :], r[:, T:384], start=False, stop=False,
                                     skip_group_check=True), mark=False)
            t = pe.do(lambda e: e.matmul(bank[:, T:384], tri[:, :], r[:, T:384], start=False, stop=True,
                                         skip_group_check=True))
            s, sfree = A["S"].get()
            dve.wait(t, *sfree)
            t1 = dve.do(lambda e: e.tensor_scalar(s[:, :], bank[:, 0:384], 0.0, None, ALU.min))
            banks.put(bank, t1)
            A["PT"].put(r, t)
            act.wait(t1)
            t2 = act.do(lambda e: e.activation(s[:, :], s[:, :], ACT.Exp, scale=0.125))
            return s, past_only(s, t2)

        def stick_attention(A, heads):
            before = None
            done = []

            def finish(h, s, t6):
                full, o, toks, _ = values(A, h, 64, h * 64, s, None, t6, None, lambda t: A["S"].put(s, t))
                if full:
                    out_chunk(A, h // 2, o, toks)

            for h in heads:
                while not A["have"](h):
                    yield
                now = (h, stick_scores(A, h))
                yield
                if before is not None:
                    s, t6 = stick_sums(A, before[1])
                    yield
                    finish(before[0], s, t6)
                    yield
                before = now
            s, t6 = stick_sums(A, before[1])
            yield
            finish(before[0], s, t6)

        def both(A):
            yield from soft_attention(A, range(8), 64, m_parts, 0.125)
            yield
            yield from stick_attention(A, range(8, 16))

        A.update(t_o=[None] * 8, t_v=lambda h, t_V=t_V: [t_V[h // 8]], v0=lambda h: h * 64, t_bias=t_bm2,
                 have=lambda h, t_Q=t_Q: (h // 2) in t_Q)
        background[0] = both(A)
        gemm("win_q", 8, 8, hh, hl, t_h, evac_copy(lambda n: Q2[:, n, :], t_Q), steps=4)
        act.wait(acc_readers[0])
        gemm("win_g", 16, 8, hh, hl, t_h,
             evac_copy(lambda n: gates[:, n, :] if n < 8 else gates2[:, (n - 8) * T:(n - 7) * T], t_G), steps=4)
        drain()
        act.wait(t_G[15])
        t_g1 = act.do(lambda e: e.activation(gates[:, :, :], gates[:, :, :], ACT.Sigmoid))
        t_g2 = act.do(lambda e: e.activation(gates2[:, :], gates2[:, :], ACT.Sigmoid))

        t_m = [None] * 8
        wts = Weights("wbr")
        for n in range(8):
            bank, free = banks.get()
            pe.wait(*free)
            for b in range(2):
                t = product(wts, 4, A["oh"][:, 4 * b:4 * b + 4, :], A["ol"][:, 4 * b:4 * b + 4, :],
                            bank[:, b * T:(b + 1) * T], A["t_o"][4 * b:4 * b + 4])
            u, fu = tmp.get()
            v, fv = tmp.get()
            dve.wait(t, t_g1, t_g2, *fu, *fv)
            t1 = dve.do(lambda e, n=n, u=u, bank=bank: e.tensor_tensor(u[:, :], bank[:, 0:T], gates[:, n, :],
                                                                       ALU.mult))
            t2 = dve.do(lambda e, n=n, v=v, bank=bank: e.tensor_tensor(v[:, :], bank[:, T:2 * T],
                                                                       gates2[:, n * T:(n + 1) * T], ALU.mult))
            banks.put(bank, t2)
            dve.wait(t1, t2)
            t3 = dve.do(lambda e, u=u, v=v: e.tensor_tensor(u[:, :], u[:, :], v[:, :], ALU.add))
            tmp.put(v, t3)
            t_m[n] = split_plain(u[:, :], hh[:, n, :], hl[:, n, :], t3)
            tmp.put(u, *t_m[n])
        stat = Stat()
        t_xs = [None] * 8

        def evac_add(gate0, after):
            def evac(n, m, bank, t):
                out = []
                for j in range(m):
                    dve.wait(t)
                    tt = dve.do(lambda e, j=j: e.scalar_tensor_tensor(
                        out=xT[:, n + j, :], in0=bank[:, j * T:(j + 1) * T],
                        scalar=modv[:, gate0 + n + j:gate0 + n + j + 1], in1=xT[:, n + j, :], op0=ALU.mult,
                        op1=ALU.add))
                    t_xs[n + j] = tt
                    after.add(xT[:, n + j, :], tt)
                    out.append(tt)
                return out
            return evac

        gemm("wout", 8, 8, hh, hl, t_m, evac_add(16, stat))
        att.close()
        R5, t_R5 = stat.finish(D)
        t_h = modulated(8, 24, R5, t_R5, t_xs)

        ffn = ExitStack()
        ph = sb("ph2", [P, NF, T], F32R, scope=ffn)
        pl = sb("pl2", [P, NF, T], F32R, scope=ffn)
        t_p = [None] * NF

        def centre(f, src, t):
            c, fc = tmp.get()
            act.wait(t, *fc)
            t1 = act.do(lambda e: e.activation(c[:, :], src, ACT.Identity, scale=col("cw2", f), bias=col("cb", f)))
            return c, t1

        def convolved(f, c, src, t1):
            dve.wait(t1)
            return dve.do(lambda e: e.scalar_tensor_tensor(out=c[:, 1:T], in0=src[:, 0:T - 1], scalar=col("cw1", f),
                                                           in1=c[:, 1:T], op0=ALU.mult, op1=ALU.add))

        def convolved2(f, c, src, t2):
            dve.wait(t2)
            return dve.do(lambda e: e.scalar_tensor_tensor(out=c[:, 2:T], in0=src[:, 0:T - 2], scalar=col("cw0", f),
                                                           in1=c[:, 2:T], op0=ALU.mult, op1=ALU.add))

        stage2, stage3 = [], []

        def second(n, v, tv, g, tg):
            dve.wait(tv, tg)
            t4 = dve.do(lambda e: e.tensor_tensor(v[:, :], v[:, :], g[:, :], ALU.mult))
            tmp.put(g, t4)
            act.wait(t4)
            return v, act.do(lambda e: e.activation(ph[:, n, :], v[:, :], ACT.Copy))

        def third(n, u, t5):
            dve.wait(t5)
            t6 = dve.do(lambda e: e.tensor_tensor(pl[:, n, :], u[:, :], ph[:, n, :].bitcast(F32), ALU.subtract))
            tmp.put(u, t6)
            t_p[n] = (t5, t6)

        def advance(item):
            if stage3:
                third(*stage3.pop(0))
            if stage2:
                m, *rest = stage2.pop(0)
                stage3.append((m, *second(m, *rest)))
            if item is not None:
                stage2.append(item)

        def evac_up(n, m, bank, t):
            f = n // 2
            v, tv = centre(f, bank[:, 0:T], t)
            g, tg = centre(NF + f, bank[:, T:2 * T], t)
            tv = convolved(f, v, bank[:, 0:T], tg)
            tg = convolved(NF + f, g, bank[:, T:2 * T], tg)
            tv = convolved2(f, v, bank[:, 0:T], tv)
            tg = convolved2(NF + f, g, bank[:, T:2 * T], tg)
            act.wait(tg)
            tg2 = act.do(lambda e: e.activation(g[:, :], g[:, :], ACT.Gelu_apprx_tanh))
            advance((f, v, tv, g, tg2))
            return [tv, tg]

        gemm("up2", 2 * NF, 8, hh, hl, t_h, evac_up)
        while stage2 or stage3:
            advance(None)
        stat = Stat()
        gemm("dn2", 8, NF, ph, pl, t_p, evac_add(40, stat))
        ffn.close()
        R6, t_R6 = stat.finish(D)
        for j in range(8):
            dve.wait(t_xs[j], t_R6)
            t = dve.do(lambda e, j=j: e.scalar_tensor_tensor(out=yb[:, j, :], in0=xT[:, j, :], scalar=col("gfin", j),
                                                             in1=R6[:, 0:T], op0=ALU.mult, op1=ALU.mult))
            if j % 4 == 3:
                sp.wait(t)
                sp.dma(a["out"][:, j - 3:j + 1, :], yb[:, j - 3:j + 1, :], s_out, 0)
        sp.wait((s_out, 32))
        assert wants["split"] == len(pieces)

        with nc.Block() as block:
            @block.sync
            def _(e):
                sp.play(e)

            @block.tensor
            def _(e):
                pe.play(e)

            @block.scalar
            def _(e):
                act.play(e)

            @block.vector
            def _(e):
                dve.play(e)

            @block.gpsimd
            def _(e):
                pool.play(e)


def _tiles(w, order=None):
    k, n = w.shape
    t = w.reshape(k // P, P, n // P, P).transpose(2, 0, 1, 3)
    return t if order is None else t[order]


def _pieces(tiles):
    tiles = tiles.reshape(-1, P, P)
    return np.concatenate([tiles[i:i + PIECE].transpose(1, 0, 2).reshape(-1) for i in range(0, len(tiles), PIECE)])[None]


def _tokens(w):
    k, n = w.shape
    return _pieces(w.reshape(k // P, P, n // 512, 4, P).transpose(2, 0, 3, 1, 4))


def _bucket_index():
    n = np.arange(256)
    large = 16 + (np.log(np.maximum(n, 16).astype(np.float32) / np.float32(16)) / np.float32(np.log(8.0))
                  * np.float32(16)).astype(np.int32)
    return np.where(n < 16, n, np.minimum(large, 31))


def _host(i):
    f = {k: np.asarray(v) for k, v in i.items()}
    o = {}
    o["xT"] = f["x"][0].T.reshape(8, P, T).transpose(1, 0, 2)
    o["pos"] = np.broadcast_to(f["positions"][0][None, :], (P, T))
    c8 = lambda v: v.reshape(-1, P).T
    inv = (np.float32(1.0) / (np.float32(10000.0) ** (np.arange(0, 64, 2, dtype=np.float32) / np.float32(64))))
    parts = dict(pre0=f["attn_pre_g"][0], pre1=f["attn_pre_g"][1], post0=f["attn_post_g"][0],
                 post1=f["attn_post_g"][1], fpre0=f["ffn_pre_g"][0], fpre1=f["ffn_pre_g"][1],
                 fpost0=f["ffn_post_g"][0], fpost1=f["ffn_post_g"][1], kvsrc=f["kv_src_g"], gq=f["mla_g_q"][0],
                 gkv=f["mla_g_kv"][0], gmix=f["g_mix_2"][0], gffn=f["g_ffn_2"][0], gfin=f["g_final_2"],
                 c=f["c_2"][0], bada=f["b_ada_2"][0], cw0=f["w_conv_2"][0, 0], cw1=f["w_conv_2"][0, 1],
                 cw2=f["w_conv_2"][0, 2], cb=f["b_conv_2"][0], inv=np.tile(inv.astype(np.float32), 4))
    o["cols"] = np.concatenate([c8(parts[n]) for n in COLS], axis=1)
    wa = f["mla_w_a"][0]
    k1, k2 = wa[:, 640:672], wa[:, 672:704]
    o["wa"] = _pieces(_tiles(np.concatenate([wa[:, :640]] + [k1] * 4 + [k2] * 4, axis=1)))
    uq = f["mla_w_uq"][0].reshape(384, 8, 192)
    rope = [uq[:, 4 * g:4 * g + 4, 128 + 32 * s:160 + 32 * s].reshape(384, P) for g in range(2) for s in range(2)]
    o["wuq"] = _pieces(_tiles(np.concatenate(rope + [uq[:, :, :128].reshape(384, 1024)], axis=1)))
    ukv = f["mla_w_ukv"][0].reshape(256, 8, 256)
    o["wuk"] = _pieces(_tiles(ukv[:, :, :128].reshape(256, 1024)))
    o["wuv"] = _tokens(ukv[:, :, 128:].reshape(256, 1024))
    o["wo0"] = _pieces(_tiles(f["mla_w_o"][0]))
    for l in range(2):
        o[f"gu{l}"] = _pieces(np.stack([_tiles(f["ffn_w_gate"][l]), _tiles(f["ffn_w_up"][l])], axis=1))
        o[f"dn{l}"] = _pieces(_tiles(f["ffn_w_down"][l]))
    o["wkv_k"] = _pieces(_tiles(f["w_kv_shared"][:, :1024]))
    o["wkv_v"] = _tokens(f["w_kv_shared"][:, 1024:])
    o["wq1"] = _pieces(_tiles(f["b_w_q"][0]))
    o["wo1"] = _pieces(_tiles(f["b_w_o"][0]))
    d = 128 + np.arange(P)[:, None] - np.arange(T)[None, :]
    o["relb"] = f["b_rel_table"][0][:, np.clip(d, -63, 256) + 63].transpose(1, 0, 2)
    o["relm"] = f["rel_bias_2"][:, _bucket_index()[np.clip(d, 0, 255)]].transpose(1, 0, 2)
    w = f["w_in_2"][0]
    qa, ka, va, qb, kb, vb = (w[:, 512 * j:512 * (j + 1)] for j in range(6))
    o["win_v"] = _tokens(np.concatenate([va, vb], axis=1))
    o["win_k"] = _pieces(_tiles(np.concatenate([ka, kb], axis=1)))
    o["win_q"] = _pieces(_tiles(np.concatenate([qa, qb], axis=1)))
    o["win_g"] = _pieces(_tiles(w[:, 3072:]))
    o["wbr"] = _pieces(np.stack([_tiles(f["w_br_moba_2"][0]), _tiles(f["w_br_sb_2"][0])], axis=1))
    o["wout"] = _pieces(_tiles(f["w_out_2"][0]))
    up = f["w_up_2"][0]
    o["up2"] = _pieces(np.stack([_tiles(up[:, :FF]), _tiles(up[:, FF:])], axis=1))
    o["dn2"] = _pieces(_tiles(f["w_down_2"][0]))
    o["wada"] = _pieces(f["w_ada_2"][0].reshape(8, P, 3, 16, P).transpose(2, 0, 3, 1, 4))
    return {k: np.ascontiguousarray(v) for k, v in o.items()}


def kernel(**inputs):
    import concourse.bacc as _bacc
    from concourse import mybir as _mybir
    from concourse.bass_utils import run_bass_kernel_spmd as _run

    nc = _bacc.Bacc("TRN2", target_bir_lowering=False, num_devices=1)
    arrays, aps = {}, {}
    for name, v in _host(inputs).items():
        arrays[f"in_{name}"] = v
        aps[name] = nc.dram_tensor(f"in_{name}", v.shape, _mybir.dt.from_np(v.dtype), kind="ExternalInput").ap()
    aps["out"] = nc.dram_tensor("out_0", (P, 8, T), F32, kind="ExternalOutput").ap()
    build(nc, aps)
    r = _run(nc, [arrays], core_ids=[0])
    got = r.results[0]["out_0"]
    return np.ascontiguousarray(got.transpose(1, 0, 2).reshape(D, T).T[None])
```

```python
from contextlib import ExitStack

import numpy as np
import concourse.bass as bass
from concourse import mybir

F32 = mybir.dt.float32
F32R = mybir.dt.float32r
I32 = mybir.dt.int32
ALU = mybir.AluOpType
ACT = mybir.ActivationFunctionType

T = 256
P = 128
D = 1024
FF = 2816
NF = FF // P
PIECE = 16
RAW = 4
SPLIT = 3
EPS = 1e-6
NEG = -1e30
PACE = (0.5, 0.5, 0.67, 0.67, 0.34, 0.34)
C1 = 6.28125
C2 = float(np.float32(0.0019353071795864769).view(np.uint32) & 0xFFFFF000 and
           (np.array([np.float32(0.0019353071795864769).view(np.uint32) & 0xFFFFE000], np.uint32).view(np.float32)[0]))
C3 = float(2.0 * np.pi - C1 - C2)
MAGIC = 12582912.0

COLS = {}
_at = 0
for _name, _n in (("pre0", 8), ("pre1", 8), ("post0", 8), ("post1", 8), ("fpre0", 8), ("fpre1", 8), ("fpost0", 8),
                  ("fpost1", 8), ("kvsrc", 8), ("gq", 3), ("gkv", 2), ("gmix", 8), ("gffn", 8), ("gfin", 8), ("c", 8),
                  ("bada", 48), ("cw0", 44), ("cw1", 44), ("cw2", 44), ("cb", 44), ("inv", 1)):
    COLS[_name] = (_at, _n)
    _at += _n
NCOL = _at

STREAM = [("wa", 56), ("wuk", 16), ("wuv", 16), ("wuq", 36), ("wo0", 64), ("gu0", 352), ("dn0", 176),
          ("wkv_v", 64), ("wkv_k", 64), ("wq1", 64), ("wo1", 64), ("gu1", 352), ("dn1", 176),
          ("win_v", 64), ("win_k", 64), ("win_q", 64), ("win_g", 128), ("wbr", 64), ("wout", 64),
          ("up2", 704 // 2), ("dn2", 176)]


class Lane:

    def __init__(self, name, sem):
        self.name, self.sem, self.count, self.ops, self.seen = name, sem, 0, [], {}

    def wait(self, *tokens):
        for t in tokens:
            if t is None:
                continue
            if isinstance(t, list):
                self.wait(*t)
                continue
            sem, value = t
            if self.seen.get(id(sem), 0) < value:
                self.seen[id(sem)] = value
                self.ops.append(lambda e, s=sem, v=value: e.wait_ge(s, v))

    def do(self, fn, mark=True):
        if not mark:
            self.ops.append(fn)
            return None
        self.count += 1
        self.ops.append(lambda e: fn(e).then_inc(self.sem, 1))
        return (self.sem, self.count)

    def dma(self, out, src, sem, value):
        self.ops.append(lambda e: e.dma_start(out, src).then_inc(sem, 16))
        return (sem, value)

    def play(self, e):
        for op in self.ops:
            op(e)


class Pool:

    def __init__(self, items):
        self.free = [(x, []) for x in items]

    def get(self):
        assert self.free, "no buffer is free"
        return self.free.pop(0)

    def put(self, item, *readers):
        self.free.append((item, list(readers)))


def build(nc, a):
    ctx = ExitStack()
    with ctx:
        def sb(name, shape, dt=F32, scope=ctx):
            return scope.enter_context(nc.sbuf_tensor("s_" + name, shape, dt))

        def sem(name):
            return ctx.enter_context(nc.semaphore(name))

        pe, act, dve, pool, sp = (Lane(n, sem("done_" + n)) for n in ("pe", "act", "dve", "pool", "sp"))

        raw = [sb(f"raw{i}", [P, PIECE * P]) for i in range(RAW)]
        whi = [sb(f"whi{i}", [P, PIECE * P], F32R) for i in range(SPLIT)]
        wlo = [sb(f"wlo{i}", [P, PIECE * P], F32R) for i in range(SPLIT)]
        xT = sb("xT", [P, 8, T])
        hh = sb("hh", [P, 8, T], F32R)
        hl = sb("hl", [P, 8, T], F32R)
        yb = sb("yb", [P, 8, T])
        adacc = sb("adacc", [P, 2048])
        cols = sb("cols", [P, NCOL])
        modv = sb("modv", [P, 48])
        cact = sb("cact", [P, 8])
        gs2 = sb("gs2", [P, 16])
        mask0 = sb("mask0", [P, T])
        ones = sb("ones", [P, P])
        tri = sb("tri", [P, P])
        negones = sb("negones", [P, P])
        ident = sb("ident", [P, P])
        Rt = Pool([sb(f"R{i}", [P, T + 2]) for i in range(3)])
        Lt = Pool([sb(f"L{i}", [P, T + 2]) for i in range(1)])
        sqacc = Pool([sb(f"sqacc{i}", [P, 2 * T]) for i in range(2)])
        squares = Pool([sb(f"sq{i}", [P, 2 * T]) for i in range(1)])
        tmp = Pool([sb(f"tmp{i}", [P, T]) for i in range(7)])
        small = Pool([sb(f"small{i}", [P, 8]) for i in range(6)])

        banks = Pool([ctx.enter_context(nc.psum_tensor(f"bank{i}", [P, 512], F32)) for i in range(8)])

        s_raw = [sem(f"s_raw{i}") for i in range(RAW)]
        s_in = [sem(f"s_in{i}") for i in range(6)]
        s_out = sem("s_out")

        def col(name, j=0, n=1):
            at = COLS[name][0] + j
            return cols[:, at:at + n]

        t_x = sp.dma(xT[:, :, :], a["xT"], s_in[0], 16)
        t_cols = sp.dma(cols[:, :], a["cols"], s_in[1], 16)

        pieces = []
        for name, n in STREAM:
            at = 0
            while at < n:
                k = min(PIECE, n - at)
                pieces.append(("w", name, at, k))
                at += k
        ada = [("ada", "wada", i * PIECE, PIECE) for i in range(24)]
        merged = []
        fed = 0
        for p in pieces:
            merged.append(p)
            if p[1] in ("gu0", "dn0", "gu1", "dn1"):
                fed += 1
                if fed % 3 == 0 or (p[1] in ("dn0", "dn1") and fed % 3 == 1):
                    merged += ada[:1]
                    del ada[:1]
        assert not ada
        pieces = merged
        wants = {"dma": 0, "split": 0, "use": 0}
        slot_readers = [(None, [])] * RAW
        ada_sums = []
        split_free = Pool(list(range(SPLIT)))
        ready = {}
        acc_readers = [None]
        ada_done = {}

        def load_next():
            i = wants["dma"]
            _, name, at, k = pieces[i]
            assert i < RAW or slot_readers[i % RAW][0] == i - RAW
            sp.wait(*slot_readers[i % RAW][1])
            sp.dma(raw[i % RAW][:, 0:k * P], a[name][:, at * P * P:(at + k) * P * P].rearrange("a (p n) -> (a p) n", p=P),
                   s_raw[i % RAW], 0)
            wants["dma"] += 1

        def arrived(i):
            return (s_raw[i % RAW], 16 * (i // RAW + 1))

        pending = []
        background = [None]

        def load_ahead():
            while wants["dma"] < len(pieces) and (
                    wants["dma"] < RAW or slot_readers[wants["dma"] % RAW][0] == wants["dma"] - RAW):
                load_next()

        slow = []

        def split_slowly():
            i = wants["split"]
            kind, _, _, k = pieces[i]
            assert kind == "w"
            wants["split"] += 1
            s, free = split_free.get()

            def parts():
                load_ahead()
                src = raw[i % RAW]
                t_hi = t_lo = None
                for lo in range(0, k, 4):
                    w = slice(lo * P, min(lo + 4, k) * P)
                    if lo % 8 == 0:
                        w2 = slice(lo * P, min(lo + 8, k) * P)
                        act.wait(arrived(i), *free)
                        t_hi = act.do(lambda e, w2=w2: e.activation(whi[s][:, w2], src[:, w2], ACT.Copy))
                        yield
                    dve.wait(arrived(i), t_hi, *free)
                    t_lo = dve.do(lambda e, w=w: e.tensor_tensor(wlo[s][:, w], src[:, w], whi[s][:, w].bitcast(F32),
                                                                 ALU.subtract))
                    if lo + 4 < k:
                        yield
                slot_readers[i % RAW] = (i, [t_hi, t_lo])
                ready[i] = (s, t_hi, t_lo)
                load_ahead()

            slow.append(parts())

        def slow_part():
            if slow:
                try:
                    next(slow[0])
                except StopIteration:
                    slow.pop(0)

        def split_high():
            while slow:
                slow_part()
            i = wants["split"]
            load_ahead()
            kind, _, at, k = pieces[i]
            wants["split"] += 1
            if kind == "ada":
                pending.append((i, None, None, ()))
                return
            s, free = split_free.get()
            src, w = raw[i % RAW], k * P
            act.wait(arrived(i), *free)
            t_hi = act.do(lambda e: e.activation(whi[s][:, 0:w], src[:, 0:w], ACT.Copy))
            pending.append((i, s, t_hi, free))

        def split_low():
            i, s, t_hi, free = pending.pop(0)
            _, _, at, k = pieces[i]
            src, w = raw[i % RAW], k * P
            if s is None:
                kc = (at // PIECE) % 8
                if kc == 0 and ada_sums:
                    ada_sum(*ada_sums.pop(0))
                dve.wait(arrived(i), t_cact)
                if kc == 0:
                    dve.wait(acc_readers[0])
                    t = dve.do(lambda e: e.tensor_scalar(adacc[:, :], src[:, :], cact[:, 0:1], None, ALU.mult))
                else:
                    dve.wait(ada_done["t"])
                    t = dve.do(lambda e: e.scalar_tensor_tensor(out=adacc[:, :], in0=src[:, :],
                                                                scalar=cact[:, kc:kc + 1], in1=adacc[:, :],
                                                                op0=ALU.mult, op1=ALU.add))
                ada_done["t"] = t
                if kc == 7:
                    ada_sums.append((at // PIECE // 8, t, wants["use"]))
                slot_readers[i % RAW] = (i, [t])
                return
            dve.wait(arrived(i), t_hi, *free)
            t_lo = dve.do(lambda e: e.tensor_tensor(wlo[s][:, 0:w], src[:, 0:w], whi[s][:, 0:w].bitcast(F32),
                                                    ALU.subtract))
            slot_readers[i % RAW] = (i, [t_hi, t_lo])
            ready[i] = (s, t_hi, t_lo)

        def refill_high():
            while (wants["split"] < len(pieces) and wants["split"] < wants["use"] + RAW
                   and (split_free.free or pieces[wants["split"]][0] == "ada")):
                if background[0] is not None and pieces[wants["split"]][0] == "w" and not pending:
                    split_slowly()
                else:
                    split_high()

        def refill_low():
            while pending:
                split_low()
            while ada_sums and wants["use"] > ada_sums[0][2] + 2:
                ada_sum(*ada_sums.pop(0))

        def refill():
            refill_high()
            refill_low()

        def ada_sum(g, t_acc, _):
            bank, free = banks.get()
            pe.wait(t_acc, t_const, *free)
            for j in range(16):
                t = pe.do(lambda e, j=j: e.matmul(bank[:, j:j + 1], adacc[:, j * P:(j + 1) * P], ones[:, 0:1],
                                                  start=True, stop=True), mark=(j == 15))
            acc_readers[0] = t
            dve.wait(t, t_cols)
            t2 = dve.do(lambda e: e.tensor_tensor(modv[:, g * 16:(g + 1) * 16], bank[:, 0:16],
                                                  col("bada", g * 16, 16), ALU.add))
            banks.put(bank, t2)
            mod_ready[g] = t2

        mod_ready = {}

        class Weights:

            def __init__(self, name):
                self.name, self.left, self.at, self.i = name, 0, 0, None

            def tile(self, n=1):
                if self.left == 0:
                    i = wants["use"]
                    while pieces[i][0] == "ada":
                        i += 1
                    assert pieces[i][1] == self.name, (pieces[i], self.name)
                    wants["use"] = i + 1
                    while wants["split"] <= i:
                        split_high()
                    refill()
                    while i not in ready:
                        slow_part()
                    self.i, self.left, self.at = i, pieces[i][3], 0
                    s, t_hi, t_lo = ready[i]
                    pe.wait(t_hi, t_lo)
                    self.s = s
                at = self.at
                self.at += n
                self.left -= n
                return (whi[self.s][:, at * P:(at + n) * P], wlo[self.s][:, at * P:(at + n) * P])

            def used(self, t):
                split_free.put(self.s, t)

        def product(wts, tiles, xh, xl, t_x, ks, nk, pace=0):
            for k in ks:
                pe.wait(*t_x[k])
                a_h, a_l = xh[:, k, :], xl[:, k, :]
                for bank, j in tiles:
                    hi, lo = wts.tile()
                    out = bank[:, j * T:(j + 1) * T]
                    first = k == 0 and (j == 0 or len(tiles) == 1)
                    pe.do(lambda e, o=out, w=hi, x=a_h, f=first: e.matmul(o, w, x, start=f, stop=False,
                                                                          skip_group_check=True), mark=False)
                    pe.do(lambda e, o=out, w=hi, x=a_l: e.matmul(o, w, x, start=False, stop=False,
                                                                 skip_group_check=True), mark=False)
                    t = pe.do(lambda e, o=out, w=lo, x=a_h, k=k: e.matmul(o, w, x, start=False, stop=(k == nk - 1),
                                                                          skip_group_check=True),
                              mark=(wts.left == 0 or k == nk - 1))
                    if wts.left == 0:
                        wts.used(t)
                    walk(pace)
            return t

        credit = [0.0]

        def walk(pace):
            slow_part()
            credit[0] += pace
            while credit[0] >= 1:
                credit[0] -= 1
                step()

        def step():
            if background[0] is not None:
                try:
                    next(background[0])
                except StopIteration:
                    background[0] = None

        def drain():
            n = 0
            while background[0] is not None:
                step()
                n += 1
                assert n < 10000, "the background is stuck"

        def gemm(name, ntiles, nk, xh, xl, t_x, evac, lead=0, pace=0, keep=False):
            wts = Weights(name)
            n = 0
            while n < ntiles:
                group = []
                for b in range(max(1, lead // 2) if n == 0 else 1):
                    bank, free = banks.get()
                    pe.wait(*free)
                    group.append((n + 2 * b, bank, min(2, ntiles - n - 2 * b)))
                if len(group) > 1:
                    tiles = [(bank, j) for _, bank, m in group for j in range(m)]
                    t = product(wts, tiles, xh, xl, t_x, range(nk), nk, pace)
                else:
                    for j in range(group[0][2]):
                        t = product(wts, [(group[0][1], j)], xh, xl, t_x, range(nk), nk, pace)
                refill_high()
                for at, bank, m in group:
                    readers = evac(at, m, bank, t)
                    if not keep:
                        banks.put(bank, *readers)
                    n += m
                refill_low()

        def gemm_tokens(name, ngroups, nk, xh, xl, t_x, evac):
            wts = Weights(name)
            for g in range(ngroups):
                b0, f0 = banks.get()
                b1, f1 = banks.get()
                pe.wait(*f0, *f1)
                for k in range(nk):
                    hi, lo = wts.tile(4)
                    pe.wait(*t_x[k])
                    for tb, bank in ((0, b0), (1, b1)):
                        a_h, a_l = xh[:, k, tb * P:(tb + 1) * P], xl[:, k, tb * P:(tb + 1) * P]
                        pe.do(lambda e, b=bank, x=a_h, w=hi, k=k: e.matmul(b[:, :], x, w, start=(k == 0), stop=False),
                              mark=False)
                        pe.do(lambda e, b=bank, x=a_h, w=lo: e.matmul(b[:, :], x, w, start=False, stop=False),
                              mark=False)
                        t = pe.do(lambda e, b=bank, x=a_l, w=hi, k=k: e.matmul(b[:, :], x, w, start=False,
                                                                               stop=(k == nk - 1)))
                    if wts.left == 0:
                        wts.used(t)
                refill_high()
                for tb, bank in ((0, b0), (1, b1)):
                    banks.put(bank, *evac(g, tb, bank, t))
                refill_low()

        def t_pe_now():
            return (pe.sem, pe.count)

        class Stat:

            def __init__(self, n, columns=True):
                self.n, self.columns = n, columns
                self.t = None
                self.done = None

            def add(self, src, w, t_src):
                if self.t is None:
                    assert w == 2 * T
                    self.acc, free = sqacc.get()
                    act.wait(t_src, *free)
                    self.t = act.do(lambda e: e.activation(self.acc[:, :], src, ACT.Square))
                    return self.t
                sq, free = squares.get()
                act.wait(t_src, *free)
                t = act.do(lambda e: e.activation(sq[:, 0:w], src, ACT.Square))
                dve.wait(t, self.t)
                self.t = dve.do(lambda e: e.tensor_tensor(self.acc[:, 0:w], self.acc[:, 0:w], sq[:, 0:w], ALU.add))
                squares.put(sq, self.t)
                return t

            def get(self):
                if self.done is not None:
                    return self.done
                bank, free = banks.get()
                pe.wait(self.t, t_const, *free)
                acc = self.acc
                pe.do(lambda e: e.matmul(bank[:, 0:T], ones[:, :], acc[:, 0:T], start=True, stop=False), mark=False)
                t = pe.do(lambda e: e.matmul(bank[:, 0:T], ones[:, :], acc[:, T:2 * T], start=False, stop=True))
                w = T
                if self.columns:
                    w = T + 2
                    for b in range(2):
                        at = T + b
                        pe.do(lambda e, at=at, b=b: e.matmul(bank[:, at:at + 1], acc[:, b * P:(b + 1) * P],
                                                             ones[:, 0:1], start=True, stop=False), mark=False)
                        t = pe.do(lambda e, at=at, b=b: e.matmul(bank[:, at:at + 1], acc[:, T + b * P:T + (b + 1) * P],
                                                                 ones[:, 0:1], start=False, stop=True))
                sqacc.put(acc, t)
                R, rfree = Rt.get()
                log, lfree = Lt.get()
                act.wait(t, t_const, *lfree)
                t1 = act.do(lambda e: e.activation(log[:, 0:w], bank[:, 0:w], ACT.Ln, scale=1.0 / self.n,
                                                   bias=epsc[:, 0:1]))
                banks.put(bank, t1)
                act.wait(t1, *rfree)
                t2 = act.do(lambda e: e.activation(R[:, 0:w], log[:, 0:w], ACT.Exp, scale=-0.5))
                Lt.put(log, t2)
                self.done = (R, t2)
                return self.done

        def split_scaled(src, gain, oh, ol, t_src, free=()):
            act.wait(t_src, t_cols, *free)
            t_h = act.do(lambda e: e.activation(oh, src, ACT.Copy, scale=gain))
            dve.wait(t_h, t_src, t_cols, *free)
            t_l = dve.do(lambda e: e.scalar_tensor_tensor(out=ol, in0=src, scalar=gain, in1=oh.bitcast(F32),
                                                          op0=ALU.mult, op1=ALU.subtract))
            return (t_h, t_l)

        def split_plain(src, oh, ol, t_src, free=()):
            act.wait(t_src, *free)
            t_h = act.do(lambda e: e.activation(oh, src, ACT.Copy))
            dve.wait(t_h, t_src, *free)
            t_l = dve.do(lambda e: e.tensor_tensor(ol, src, oh.bitcast(F32), ALU.subtract))
            return (t_h, t_l)

        def log_tables():
            act.do(lambda e: e.preload_act_table_set("natural_log_exp_and_others"), mark=False)

        def add_normed(ys, gain, stat, pre):
            R, t_r = stat.get()
            t_xs, t_h, us = [None] * 8, [None] * 8, [None] * 8
            hi = [None] * 8
            nxt = Stat(D)

            def low(j):
                dve.wait(hi[j])
                t_l = dve.do(lambda e, j=j: e.scalar_tensor_tensor(
                    out=hl[:, j, :], in0=xT[:, j, :], scalar=col(pre, j), in1=hh[:, j, :].bitcast(F32),
                    op0=ALU.mult, op1=ALU.subtract))
                t_h[j] = (hi[j], t_l)

            for j in range(10):
                if j < 8:
                    bank, half = ys[j]
                    u, ufree = tmp.get()
                    dve.wait(t_r, *ufree)
                    y = bank[:, half * T:(half + 1) * T]
                    t1 = dve.do(lambda e, j=j, u=u, y=y: e.scalar_tensor_tensor(
                        out=u[:, :], in0=y, scalar=col(gain, j), in1=R[:, 0:T], op0=ALU.mult, op1=ALU.mult))
                    us[j] = (u, t1)
                    if half == 1:
                        banks.put(bank, t1)
                if 1 <= j < 9:
                    i = j - 1
                    u, t1 = us[i]
                    dve.wait(t1)
                    t_xs[i] = dve.do(lambda e, i=i, u=u: e.tensor_tensor(xT[:, i, :], xT[:, i, :], u[:, :], ALU.add))
                    tmp.put(u, t_xs[i])
                    if pre is not None:
                        act.wait(t_xs[i])
                        hi[i] = act.do(lambda e, i=i: e.activation(hh[:, i, :], xT[:, i, :], ACT.Copy,
                                                                   scale=col(pre, i)))
                if j >= 2 and pre is not None:
                    low(j - 2)
                if pre is None and j >= 2 and j % 2 == 0:
                    nxt.add(xT[:, j - 2:j, :], 2 * T, t_xs[j - 1])
            Rt.put(R, us[7][1])
            if pre is not None:
                for j in range(0, 8, 2):
                    nxt.add(xT[:, j:j + 2, :], 2 * T, t_xs[j + 1])
            return t_h, nxt, t_xs

        epsc = sb("epsc", [P, 2])
        pool.do(lambda e: e.memset(epsc[:, 0:1], EPS), mark=False)
        pool.do(lambda e: e.memset(epsc[:, 1:2], float(np.pi / 2)), mark=False)
        pool.do(lambda e: e.memset(ones[:, :], 1.0), mark=False)
        pool.do(lambda e: e.memset(negones[:, :], -1.0), mark=False)
        pool.do(lambda e: e.memset(mask0[:, :], 0.0), mark=False)
        pool.do(lambda e: e.memset(ident[:, :], 0.0), mark=False)
        t_set = pool.do(lambda e: e.memset(tri[:, :], -1.0))
        pool.wait(t_set)
        pool.do(lambda e: e.memset(mask0[0:64, 192:256], NEG), mark=False)
        pool.do(lambda e: e.affine_select(out=ident[:, :], in_=ident[:, :], compare_op=ALU.not_equal, fill=1.0,
                                          base=0, pattern=[[-1, P]], channel_multiplier=1), mark=False)
        t_const = pool.do(lambda e: e.affine_select(out=tri[:, :], in_=tri[:, :], compare_op=ALU.is_ge, fill=0.0,
                                                    base=0, pattern=[[-1, P]], channel_multiplier=1))

        att = ExitStack()
        cosb, sinb, posi = adacc[:, 0:T], adacc[:, T:2 * T], adacc[:, 2 * T:3 * T].bitcast(I32)
        cq = yb
        cqh = sb("cqh", [P, 5, T], F32R, scope=att)
        cql = sb("cql", [P, 5, T], F32R, scope=att)

        def attention_buffers(scope, tag, nq, nk_):
            return dict(
                Q=sb("Q" + tag, [P, nq, T], scope=scope), K=sb("K" + tag, [P, nk_, T], scope=scope),
                V=sb("V" + tag, [P, 2, 1024], scope=scope),
                S=Pool([sb(f"S{tag}{i}", [P, 384], scope=scope) for i in range(3)]),
                PT=Pool([sb(f"PT{tag}{i}", [P, 384], scope=scope) for i in range(2)]),
                O=Pool([sb(f"O{tag}{i}", [P, 2, P], scope=scope) for i in range(2)]),
                oh=sb("oh" + tag, [P, 8, T], F32R, scope=scope), ol=sb("ol" + tag, [P, 8, T], F32R, scope=scope))

        A = attention_buffers(att, "0", 12, 10)
        Q0, K0, V0 = A["Q"], A["K"], A["V"]

        t_pos = sp.dma(posi, a["pos"], s_in[2], 16)

        def rope_table():
            ang, f1 = tmp.get()
            k_, f2 = tmp.get()
            r_, f3 = tmp.get()
            dve.wait(t_pos, t_cols, *f1, *f2, *f3)
            t = dve.do(lambda e: e.tensor_copy(r_[:, :], posi))
            dve.wait(t)
            t = dve.do(lambda e: e.tensor_scalar(ang[:, :], r_[:, :], col("inv"), None, ALU.mult))
            dve.wait(t)
            t = dve.do(lambda e: e.tensor_scalar(k_[:, :], ang[:, :], float(1 / (2 * np.pi)), MAGIC, ALU.mult,
                                                 ALU.add))
            dve.wait(t)
            t = dve.do(lambda e: e.tensor_scalar(k_[:, :], k_[:, :], -MAGIC, None, ALU.add))
            src, dst = ang, r_
            for c in (C1, C2, C3):
                dve.wait(t)
                t = dve.do(lambda e, c=c, s=src, d=dst: e.scalar_tensor_tensor(
                    out=d[:, :], in0=k_[:, :], scalar=-c, in1=s[:, :], op0=ALU.mult, op1=ALU.add))
                src, dst = dst, src
            dve.wait(t)
            t = dve.do(lambda e, s=src: e.tensor_scalar(s[:, :], s[:, :], 3.1415925, -3.1415925, ALU.min, ALU.max))
            act.wait(t, t_const)
            t1 = act.do(lambda e, s=src: e.activation(sinb, s[:, :], ACT.Sin))
            t2 = act.do(lambda e, s=src, d=dst: e.activation(d[:, :], s[:, :], ACT.Abs))
            act.wait(t2)
            t3 = act.do(lambda e, d=dst: e.activation(cosb, d[:, :], ACT.Sin, scale=-1.0, bias=epsc[:, 1:2]))
            for b in (ang, k_, r_):
                tmp.put(b, t1, t3)
            return [t1, t3]

        t_h = [split_scaled(xT[:, k, :], col("pre0", k), hh[:, k, :], hl[:, k, :], t_x) for k in range(8)]
        refill()
        stat0 = Stat(D)
        for k in range(0, 8, 2):
            stat0.add(xT[:, k:k + 2, :], 2 * T, t_x)

        def scaled(dst, src, R, t_src, t_r, free=()):
            dve.wait(t_src, t_r, *free)
            return dve.do(lambda e: e.tensor_tensor(dst, src, R[:, 0:T], ALU.mult))

        stat_kv, stat_q = Stat(256), Stat(384)
        t_cq = [None] * 5
        krt = []

        def evac_a(n, m, bank, t):
            R0, t_R0 = stat0.get()
            out = []
            for j in range(m):
                f = n + j
                src = bank[:, j * T:(j + 1) * T]
                if f < 5:
                    t1 = scaled(cq[:, f, :], src, R0, t, t_R0)
                    t_cq[f] = split_scaled(cq[:, f, :], col("gkv", f) if f < 2 else col("gq", f - 2), cqh[:, f, :],
                                           cql[:, f, :], t1)
                    if f == 1:
                        stat_kv.add(cq[:, 0:2, :], 2 * T, t1)
                    if f == 3:
                        stat_q.add(cq[:, 2:4, :], 2 * T, t1)
                    if f == 4:
                        stat_q.add(cq[:, 4, :], T, t1)
                else:
                    b, free = tmp.get()
                    t1 = scaled(b[:, :], src, R0, t, t_R0, free)
                    krt.append((b, t1))
                    if f == 6:
                        Rt.put(R0, t1)
                out.append(t1)
            return out

        gemm("wa", 7, 8, hh, hl, t_h, evac_a, lead=4)
        act.wait(t_cols)
        t_cact = act.do(lambda e: e.activation(cact[:, :], col("c", 0, 8), ACT.Silu))
        t_rope = rope_table()
        log_tables()

        def rotate(a1, a2, o1, o2, t_in):
            u, fu = tmp.get()
            v, fv = tmp.get()
            dve.wait(t_in, t_rope, *fu, *fv)
            dve.do(lambda e: e.tensor_tensor(u[:, :], a2, sinb, ALU.mult), mark=False)
            t2 = dve.do(lambda e: e.tensor_tensor(v[:, :], a1, sinb, ALU.mult))
            dve.wait(t2)
            dve.do(lambda e: e.tensor_tensor(o1, a1, cosb, ALU.mult), mark=False)
            t4 = dve.do(lambda e: e.tensor_tensor(o2, a2, cosb, ALU.mult))
            dve.wait(t4)
            dve.do(lambda e: e.tensor_tensor(o1, o1, u[:, :], ALU.subtract), mark=False)
            t6 = dve.do(lambda e: e.tensor_tensor(o2, o2, v[:, :], ALU.add))
            tmp.put(u, t6)
            tmp.put(v, t6)
            return t6

        t_K, t_V, t_Q = {}, {}, {}

        def evac_into(dst, toks, stat, free=(), base=0):
            def evac(n, m, bank, t):
                R, t_r = stat.get()
                dve.wait(t, t_r, *free)
                out = []
                for j in range(m):
                    tt = dve.do(lambda e, j=j: e.tensor_tensor(dst[:, base + n + j, :], bank[:, j * T:(j + 1) * T],
                                                               R[:, 0:T], ALU.mult))
                    toks[n + j] = tt
                    out.append(tt)
                return out
            return evac

        def evac_tokens(dst, toks, stat, free=()):
            def evac(g, tb, bank, t):
                R, t_r = stat.get() if stat is not None else (None, None)
                act.wait(t, t_r, *free)
                if R is None:
                    tt = act.do(lambda e: e.activation(dst[:, tb, g * 512:(g + 1) * 512], bank[:, :], ACT.Copy))
                else:
                    tt = act.do(lambda e: e.activation(dst[:, tb, g * 512:(g + 1) * 512], bank[:, :], ACT.Copy,
                                                       scale=R[:, T + tb:T + tb + 1]))
                toks[g] = tt
                return [tt]
            return evac

        gemm("wuk", 8, 2, cqh, cql, t_cq, evac_into(K0, t_K, stat_kv))
        gemm_tokens("wuv", 2, 2, cqh, cql, t_cq, evac_tokens(V0, t_V, stat_kv))
        (k1b, tk1), (k2b, tk2) = krt
        t_krope = rotate(k1b[:, :], k2b[:, :], K0[:, 8, :], K0[:, 9, :], tk2)
        tmp.put(k1b, t_krope)
        tmp.put(k2b, t_krope)

        def out_chunk(A, c, o, t_o):
            bank, free = banks.get()
            pe.wait(t_o, t_const, *free)
            pe.do(lambda e: e.transpose(bank[:, 0:P], o[:, 0, :], ident[:, :]), mark=False)
            t = pe.do(lambda e: e.transpose(bank[:, P:T], o[:, 1, :], ident[:, :]))
            A["O"].put(o, t)
            oh, ol = A["oh"][:, c, :], A["ol"][:, c, :]
            t_hl = split_plain(bank[:, 0:T], oh, ol, t)
            banks.put(bank, *t_hl)
            A["t_o"][c] = t_hl

        def values(A, h, dv, v0, left, right, t_in, scale, release):
            bank, free = banks.get()
            pe.wait(t_in, *free)
            pe.wait(*A["t_v"](h))
            VL = A["V"]
            p = left
            pe.do(lambda e: e.matmul(bank[:, 0:dv], p[:, 0:P], VL[:, 0, v0:v0 + dv], start=True, stop=True),
                  mark=False)
            pe.do(lambda e: e.matmul(bank[:, dv:2 * dv], p[:, P:T], VL[:, 0, v0:v0 + dv], start=True, stop=False),
                  mark=False)
            t = pe.do(lambda e: e.matmul(bank[:, dv:2 * dv], p[:, T:384], VL[:, 1, v0:v0 + dv], start=False,
                                         stop=True))
            release(t)
            per = P // dv
            if h % per == 0:
                A["o_now"] = A["O"].get()
                A["o_toks"] = []
            o, ofree = A["o_now"]
            at = (h % per) * dv
            toks = []
            for qb in range(2):
                dve.wait(t, *ofree)
                if scale is None:
                    tt = dve.do(lambda e, qb=qb: e.tensor_copy(o[:, qb, at:at + dv], bank[:, qb * dv:(qb + 1) * dv]))
                else:
                    rinv, t_rinv = scale
                    dve.wait(t_rinv)
                    tt = dve.do(lambda e, qb=qb: e.tensor_scalar(o[:, qb, at:at + dv], bank[:, qb * dv:(qb + 1) * dv],
                                                                 rinv[:, qb:qb + 1], None, ALU.mult))
                toks.append(tt)
            banks.put(bank, tt)
            A["o_toks"] += toks
            return h % per == per - 1, o, A["o_toks"], tt

        def soft_scores(A, h, parts, t_in, bias, scale):
            bank, free = banks.get()
            pe.wait(t_in, *free)
            n = len(parts)
            for i, (q, k) in enumerate(parts):
                t = pe.do(lambda e, q=q, k=k, i=i: e.matmul(bank[:, 0:P], q[:, 0:P], k[:, 0:P], start=(i == 0),
                                                            stop=(i == n - 1)), mark=False)
            for i, (q, k) in enumerate(parts):
                t = pe.do(lambda e, q=q, k=k, i=i: e.matmul(bank[:, P:384], q[:, P:T], k, start=(i == 0),
                                                            stop=(i == n - 1)), mark=(i == n - 1))
            s, sfree = A["S"].get()
            w, wfree = small.get()
            dve.wait(t, A["t_bias"], *sfree, *wfree)
            dve.do(lambda e: e.tensor_tensor_reduce(out=s[:, 0:P], in0=bank[:, 0:P], in1=bias[:, P:T], scale=1.0,
                                                    scalar=-3e38, op0=ALU.add, op1=ALU.max, accum_out=w[:, 0:1]))
            t1 = dve.do(lambda e: e.tensor_tensor_reduce(out=s[:, P:384], in0=bank[:, P:384], in1=bias[:, 0:T],
                                                         scale=1.0, scalar=-3e38, op0=ALU.add, op1=ALU.max,
                                                         accum_out=w[:, 1:2]))
            banks.put(bank, t1)
            dve.wait(t1)
            t2 = dve.do(lambda e: e.tensor_scalar(w[:, 2:4], w[:, 0:2], -scale, None, ALU.mult))
            act.wait(t2)
            act.do(lambda e: e.activation(s[:, 0:P], s[:, 0:P], ACT.Exp, scale=scale, bias=w[:, 2:3],
                                          accum_out=w[:, 4:5]))
            t3 = act.do(lambda e: e.activation(s[:, P:384], s[:, P:384], ACT.Exp, scale=scale, bias=w[:, 3:4],
                                               accum_out=w[:, 5:6]))
            return s, w, t3

        def soft_transposed(A, got):
            s, w, t3 = got
            bank, free = banks.get()
            pe.wait(t3, t_const, *free)
            for i in range(3):
                t = pe.do(lambda e, i=i: e.transpose(bank[:, i * P:(i + 1) * P], s[:, i * P:(i + 1) * P],
                                                     ident[:, :]), mark=(i == 2))
            A["S"].put(s, t)
            pt, pfree = A["PT"].get()
            act.wait(t, *pfree)
            t4 = act.do(lambda e: e.activation(pt[:, :], bank[:, 0:384], ACT.Copy))
            banks.put(bank, t4)
            dve.wait(t3)
            t5 = dve.do(lambda e: e.reciprocal(w[:, 6:8], w[:, 4:6]))
            return pt, w, t4, t5

        def soft_attention(A, heads, dv, parts_of, scale):
            before, whole = None, []
            for h in list(heads) + [None]:
                while h is not None and not A["have"](h):
                    yield
                if before is not None:
                    pt, w, t4, t5 = soft_transposed(A, before[1])
                    yield
                if whole:
                    out_chunk(A, *whole.pop(0))
                    yield
                if h is not None:
                    parts, t_in, bias = parts_of(h)
                    now = (h, soft_scores(A, h, parts, t_in, bias, scale))
                    yield
                if before is not None:
                    i = before[0]
                    full, o, toks, last = values(A, i, dv, A["v0"](i), pt, None, t4, (w[:, 6:8], t5),
                                                 lambda t: A["PT"].put(pt, t))
                    small.put(w, last)
                    if full:
                        whole.append((i * dv // P, o, toks))
                    yield
                before = now
            out_chunk(A, *whole.pop(0))

        t_qr = {}

        def mla_parts(h):
            g = h % 4
            c = h // 4
            lo, hi = 32 * g, 32 * g + 32
            return ([(Q0[:, h, :], K0[:, h, :]), (Q0[lo:hi, 8 + c, :], K0[lo:hi, 8, :]),
                     (Q0[lo:hi, 10 + c, :], K0[lo:hi, 9, :])], [t_Q[h], t_K[h], t_qr[c], t_krope], mask0)

        A.update(t_o=[None] * 8, t_v=lambda h: [t_V[h // 4]], v0=lambda h: h * P, t_bias=t_const,
                 have=lambda h: h in t_Q and (h // 4) in t_qr)
        background[0] = soft_attention(A, range(8), P, mla_parts, float(192.0 ** -0.5))

        ORDER = [8, 10, 9, 11, 0, 1, 2, 3, 4, 5, 6, 7]

        def evac_q(n, m, bank, t):
            R, t_r = stat_q.get()
            out = []
            dve.wait(t, t_r)
            for j in range(m):
                d = ORDER[n + j]
                tt = dve.do(lambda e, j=j, d=d: e.tensor_tensor(Q0[:, d, :], bank[:, j * T:(j + 1) * T], R[:, 0:T],
                                                                ALU.mult))
                if d < 8:
                    t_Q[d] = tt
                out.append(tt)
            if n < 4:
                c = n // 2
                t_qr[c] = rotate(Q0[:, 8 + c, :], Q0[:, 10 + c, :], Q0[:, 8 + c, :], Q0[:, 10 + c, :], tt)
            return out

        gemm("wuq", 12, 3, cqh[:, 2:5, :], cql[:, 2:5, :], t_cq[2:5], evac_q, pace=PACE[0])

        def project_out(name, A, pace):
            wts = Weights(name)
            stat = Stat(D, columns=False)
            held = []
            for _ in range(4):
                bank, free = banks.get()
                pe.wait(*free)
                held.append(bank)
            tiles = [(bank, j) for bank in held for j in range(2)]
            for k in range(8):
                while A["t_o"][k] is None:
                    step()
                t = product(wts, tiles, A["oh"], A["ol"], A["t_o"], [k], 8, pace)
                refill()
            for bank in held:
                stat.add(bank[:, :], 2 * T, t)
            return tiles, stat

        ys, stat = project_out("wo0", A, PACE[1])
        Rt.put(stat_kv.get()[0], t_V[1], t_K[7])
        Rt.put(stat_q.get()[0], t_Q[7])
        t_h, stat, t_xs = add_normed(ys, "post0", stat, "fpre0")
        att.close()

        def feed_forward(layer, t_h, stat1, pre):
            scope = ExitStack()
            ph = sb(f"ph{layer}", [P, NF, T], F32R, scope=scope)
            pl = sb(f"pl{layer}", [P, NF, T], F32R, scope=scope)
            t_p = [None] * NF
            late = []

            def first(n, bank, t):
                R, t_r = stat1.get()
                g, fg = tmp.get()
                u, fu = tmp.get()
                dve.wait(t, t_r, *fg, *fu)
                t1 = dve.do(lambda e: e.tensor_tensor(g[:, :], bank[:, 0:T], R[:, 0:T], ALU.mult))
                t2 = dve.do(lambda e: e.tensor_tensor(u[:, :], bank[:, T:2 * T], R[:, 0:T], ALU.mult))
                act.wait(t1)
                t3 = act.do(lambda e: e.activation(g[:, :], g[:, :], ACT.Silu))
                return g, u, t2, t3

            def second(n, g, u, t2, t3):
                dve.wait(t2, t3)
                t4 = dve.do(lambda e: e.tensor_tensor(u[:, :], u[:, :], g[:, :], ALU.mult))
                tmp.put(g, t4)
                act.wait(t4)
                t5 = act.do(lambda e: e.activation(ph[:, n, :], u[:, :], ACT.Copy))
                return u, t5

            def third(n, u, t5):
                dve.wait(t5)
                t6 = dve.do(lambda e: e.tensor_tensor(pl[:, n, :], u[:, :], ph[:, n, :].bitcast(F32), ALU.subtract))
                tmp.put(u, t6)
                t_p[n] = (t5, t6)

            stage2, stage3 = [], []

            def advance(n, item):
                if stage3:
                    third(*stage3.pop(0))
                if stage2:
                    m, *rest = stage2.pop(0)
                    stage3.append((m, *second(m, *rest)))
                if item is not None:
                    stage2.append((n, *item))

            def evac(n, m, bank, t):
                item = first(n // 2, bank, t)
                advance(n // 2, item)
                return [item[2]]

            gemm(f"gu{layer}", 2 * NF, 8, hh, hl, t_h, evac, lead=4)
            while stage2 or stage3:
                advance(None, None)
            log_tables()
            Rt.put(stat1.get()[0], t_p[NF - 1][1])
            stat = Stat(D, columns=False)
            ys = []

            def evac_y(n, m, bank, t):
                stat.add(bank[:, :], 2 * T, t)
                ys.extend([(bank, 0), (bank, 1)])

            gemm(f"dn{layer}", 8, NF, ph, pl, t_p, evac_y, keep=True)
            out = add_normed(ys, f"fpost{layer}", stat, pre)
            scope.close()
            return out

        t_h, stat, t_xs = feed_forward(0, t_h, stat, "kvsrc")
        stat_x1 = stat

        att = ExitStack()
        A = attention_buffers(att, "1", 8, 8)
        Q1, K1, V1 = A["Q"], A["K"], A["V"]
        bias1 = sb("bias1", [P, 16, T], scope=att)
        sp.wait(t_pe_now())
        t_bias = sp.dma(bias1[:, :, :], a["relb"], s_in[3], 16)
        pool.wait(t_bias)
        t_b8 = pool.do(lambda e: e.tensor_scalar(bias1[:, :, :], bias1[:, :, :], 8.0, None, ALU.mult))
        pool.wait(t_b8)
        t_bm = pool.do(lambda e: e.memset(bias1[0:64, :, 192:256], NEG))
        t_K, t_V, t_Q = {}, {}, {}
        gemm_tokens("wkv_v", 2, 8, hh, hl, t_h, evac_tokens(V1, t_V, stat_x1))
        gemm("wkv_k", 8, 8, hh, hl, t_h, evac_into(K1, t_K, stat_x1))
        t_h = [split_scaled(xT[:, k, :], col("pre1", k), hh[:, k, :], hl[:, k, :], t_xs[k], (t_K[7],))
               for k in range(8)]

        def b_parts(h, Q1=Q1, K1=K1, t_Q=t_Q, t_K=t_K):
            lo = 64 * (h % 2)
            c = h // 2
            return ([(Q1[lo:lo + 64, c, :], K1[lo:lo + 64, c, :])], [t_Q[c], t_K[c]], bias1[:, h, :])

        A.update(t_o=[None] * 8, t_v=lambda h, t_V=t_V: [t_V[h // 8]], v0=lambda h: h * 64, t_bias=t_bm,
                 have=lambda h, t_Q=t_Q: (h // 2) in t_Q)
        background[0] = soft_attention(A, range(16), 64, b_parts, 0.125)
        gemm("wq1", 8, 8, hh, hl, t_h, evac_into(Q1, t_Q, stat_x1), lead=4, pace=PACE[2])
        ys, stat = project_out("wo1", A, PACE[3])
        Rt.put(stat_x1.get()[0], t_Q[7], t_V[1])
        t_h, stat, t_xs = add_normed(ys, "post1", stat, "fpre1")
        att.close()
        t_h, stat, t_xs = feed_forward(1, t_h, stat, None)

        while ada_sums:
            ada_sum(*ada_sums.pop(0))
        dve.wait(mod_ready[0], mod_ready[1], mod_ready[2])
        dve.do(lambda e: e.scalar_tensor_tensor(out=gs2[:, 0:8], in0=modv[:, 8:16], scalar=1.0, in1=col("gmix", 0, 8),
                                                op0=ALU.add, op1=ALU.mult))
        t_gs = dve.do(lambda e: e.scalar_tensor_tensor(out=gs2[:, 8:16], in0=modv[:, 32:40], scalar=1.0,
                                                       in1=col("gffn", 0, 8), op0=ALU.add, op1=ALU.mult))

        def modulated(g0, s0, stat, t_xs, free=()):
            R, t_r = stat.get()
            out = []

            def low(j, u, t2):
                dve.wait(t2)
                t3 = dve.do(lambda e, j=j, u=u: e.scalar_tensor_tensor(
                    out=hl[:, j, :], in0=u[:, :], scalar=modv[:, s0 + j:s0 + j + 1], in1=hh[:, j, :].bitcast(F32),
                    op0=ALU.add, op1=ALU.subtract))
                tmp.put(u, t3)
                out.append((t2, t3))

            last = None
            for j in range(8):
                u, fu = tmp.get()
                dve.wait(t_xs[j], t_r, t_gs, *fu)
                t1 = dve.do(lambda e, j=j, u=u: e.scalar_tensor_tensor(
                    out=u[:, :], in0=xT[:, j, :], scalar=gs2[:, g0 + j:g0 + j + 1], in1=R[:, 0:T], op0=ALU.mult,
                    op1=ALU.mult))
                act.wait(t1, mod_ready[0], mod_ready[1], *free)
                t2 = act.do(lambda e, j=j, u=u: e.activation(hh[:, j, :], u[:, :], ACT.Identity,
                                                             bias=modv[:, s0 + j:s0 + j + 1]))
                if last is not None:
                    low(*last)
                last = (j, u, t2)
            low(*last)
            Rt.put(R, t1)
            return out

        t_h = modulated(0, 0, stat, t_xs)
        att = ExitStack()
        A = attention_buffers(att, "2", 8, 8)
        Q2, K2, V2 = A["Q"], A["K"], A["V"]
        gates = yb
        gates2 = adacc
        t_K, t_V, t_Q, t_G = {}, {}, {}, {}
        bias2 = sb("bias2", [P, 8, T], scope=att)
        sp.wait(t_pe_now())
        t_bias2 = sp.dma(bias2[:, :, :], a["relm"], s_in[4], 16)
        pool.wait(t_bias2)
        t_b8 = pool.do(lambda e: e.tensor_scalar(bias2[:, 0:8, :], bias2[:, 0:8, :], 8.0, None, ALU.mult))
        pool.wait(t_b8)
        t_bm2 = pool.do(lambda e: e.affine_select(out=bias2[:, 0:8, :], in_=bias2[:, 0:8, :], compare_op=ALU.is_ge,
                                                  fill=NEG, base=128, pattern=[[0, 8], [-1, T]],
                                                  channel_multiplier=1))

        def evac_copy(dst_of, toks):
            def evac(n, m, bank, t):
                act.wait(t)
                out = []
                for j in range(m):
                    tt = act.do(lambda e, j=j: e.activation(dst_of(n + j), bank[:, j * T:(j + 1) * T], ACT.Copy))
                    toks[n + j] = tt
                    out.append(tt)
                return out
            return evac

        gemm_tokens("win_v", 2, 8, hh, hl, t_h, evac_tokens(V2, t_V, None), )
        gemm("win_k", 8, 8, hh, hl, t_h, evac_copy(lambda n: K2[:, n, :], t_K))

        def m_parts(h, Q2=Q2, K2=K2, t_Q=t_Q, t_K=t_K):
            lo = 64 * (h % 2)
            c = h // 2
            return ([(Q2[lo:lo + 64, c, :], K2[lo:lo + 64, c, :])], [t_Q[c], t_K[c]], bias2[:, h, :])

        def stick_scores(A, h):
            lo = 64 * (h % 2)
            c = h // 2
            q, k = Q2[lo:lo + 64, c, :], K2[lo:lo + 64, c, :]
            bank, free = banks.get()
            pe.wait(t_Q[c], t_K[c], *free)
            pe.do(lambda e: e.matmul(bank[:, 0:T], k[:, 0:P], q, start=True, stop=True), mark=False)
            t = pe.do(lambda e: e.matmul(bank[:, T:384], k[:, P:T], q[:, P:T], start=False, stop=True,
                                         skip_group_check=True))
            s, sfree = A["S"].get()
            r, rfree = A["PT"].get()
            act.wait(t, *sfree)
            t1 = act.do(lambda e: e.activation(s[:, :], bank[:, 0:384], ACT.Abs))
            act.wait(t1)
            t2 = act.do(lambda e: e.activation(s[:, :], s[:, :], ACT.Exp, scale=-0.125))
            act.wait(t2)
            t3 = act.do(lambda e: e.activation(s[:, :], s[:, :], ACT.Ln, bias=ones[:, 0:1]))
            dve.wait(t1, *rfree)
            t4 = dve.do(lambda e: e.tensor_scalar(r[:, :], bank[:, 0:384], 0.0, None, ALU.max))
            dve.wait(t3, t4)
            t5 = dve.do(lambda e: e.scalar_tensor_tensor(out=r[:, :], in0=s[:, :], scalar=8.0, in1=r[:, :],
                                                         op0=ALU.mult, op1=ALU.add))
            A["S"].put(s, t5)
            t6 = past_only(r, t5)
            return bank, r, [t1, t4, t6]

        def past_only(r, t):
            pool.wait(t)
            pool.do(lambda e: e.affine_select(out=r[:, 0:P], in_=r[:, 0:P], compare_op=ALU.is_gt, fill=0.0,
                                              base=0, pattern=[[1, P]], channel_multiplier=-1), mark=False)
            return pool.do(lambda e: e.affine_select(out=r[:, T:384], in_=r[:, T:384], compare_op=ALU.is_gt, fill=0.0,
                                                     base=0, pattern=[[1, P]], channel_multiplier=-1))

        def stick_sums(A, got):
            bank, r, toks = got
            pe.wait(toks, t_const)
            pe.do(lambda e: e.matmul(bank[:, 0:T], tri[:, :], r[:, 0:T], start=False, stop=False,
                                     skip_group_check=True), mark=False)
            pe.do(lambda e: e.matmul(bank[:, P:T], negones[:, :], r[:, T:384], start=False, stop=False,
                                     skip_group_check=True), mark=False)
            t = pe.do(lambda e: e.matmul(bank[:, T:384], tri[:, :], r[:, T:384], start=False, stop=True,
                                         skip_group_check=True))
            s, sfree = A["S"].get()
            dve.wait(t, *sfree)
            t1 = dve.do(lambda e: e.tensor_scalar(s[:, :], bank[:, 0:384], 0.0, None, ALU.min))
            banks.put(bank, t1)
            A["PT"].put(r, t)
            act.wait(t1)
            t2 = act.do(lambda e: e.activation(s[:, :], s[:, :], ACT.Exp, scale=0.125))
            return s, past_only(s, t2)

        def stick_attention(A, heads):
            before, whole = None, []

            for h in list(heads) + [None]:
                while h is not None and not A["have"](h):
                    yield
                if before is not None:
                    s, t6 = stick_sums(A, before[1])
                    yield
                if whole:
                    out_chunk(A, *whole.pop(0))
                    yield
                if h is not None:
                    now = (h, stick_scores(A, h))
                    yield
                if before is not None:
                    i = before[0]
                    full, o, toks, _ = values(A, i, 64, i * 64, s, None, t6, None, lambda t: A["S"].put(s, t))
                    if full:
                        whole.append((i // 2, o, toks))
                    yield
                before = now
            out_chunk(A, *whole.pop(0))

        def both(A):
            yield from soft_attention(A, range(8), 64, m_parts, 0.125)
            yield
            yield from stick_attention(A, range(8, 16))

        A.update(t_o=[None] * 8, t_v=lambda h, t_V=t_V: [t_V[h // 8]], v0=lambda h: h * 64, t_bias=t_bm2,
                 have=lambda h, t_Q=t_Q: (h // 2) in t_Q)
        background[0] = both(A)
        gemm("win_q", 8, 8, hh, hl, t_h, evac_copy(lambda n: Q2[:, n, :], t_Q), pace=PACE[4])
        act.wait(acc_readers[0])
        gemm("win_g", 16, 8, hh, hl, t_h,
             evac_copy(lambda n: gates[:, n, :] if n < 8 else gates2[:, (n - 8) * T:(n - 7) * T], t_G), pace=PACE[5])
        drain()
        act.wait(t_G[15])
        t_g1 = act.do(lambda e: e.activation(gates[:, :, :], gates[:, :, :], ACT.Sigmoid))
        t_g2 = act.do(lambda e: e.activation(gates2[:, :], gates2[:, :], ACT.Sigmoid))
        log_tables()

        t_m = [None] * 8
        wts = Weights("wbr")
        for n in range(8):
            bank, free = banks.get()
            pe.wait(*free)
            for b in range(2):
                t = product(wts, [(bank, b)], A["oh"][:, 4 * b:4 * b + 4, :], A["ol"][:, 4 * b:4 * b + 4, :],
                            A["t_o"][4 * b:4 * b + 4], range(4), 4)
            u, fu = tmp.get()
            v, fv = tmp.get()
            dve.wait(t, t_g1, t_g2, *fu, *fv)
            t1 = dve.do(lambda e, n=n, u=u, bank=bank: e.tensor_tensor(u[:, :], bank[:, 0:T], gates[:, n, :],
                                                                       ALU.mult))
            t2 = dve.do(lambda e, n=n, v=v, bank=bank: e.tensor_tensor(v[:, :], bank[:, T:2 * T],
                                                                       gates2[:, n * T:(n + 1) * T], ALU.mult))
            banks.put(bank, t2)
            dve.wait(t1, t2)
            t3 = dve.do(lambda e, u=u, v=v: e.tensor_tensor(u[:, :], u[:, :], v[:, :], ALU.add))
            tmp.put(v, t3)
            t_m[n] = split_plain(u[:, :], hh[:, n, :], hl[:, n, :], t3)
            tmp.put(u, *t_m[n])
            refill()
        stat = Stat(D)
        t_xs = [None] * 8

        def evac_add(gate0, after):
            def evac(n, m, bank, t):
                out = []
                for j in range(m):
                    dve.wait(t)
                    tt = dve.do(lambda e, j=j: e.scalar_tensor_tensor(
                        out=xT[:, n + j, :], in0=bank[:, j * T:(j + 1) * T],
                        scalar=modv[:, gate0 + n + j:gate0 + n + j + 1], in1=xT[:, n + j, :], op0=ALU.mult,
                        op1=ALU.add))
                    t_xs[n + j] = tt
                    out.append(tt)
                after.add(xT[:, n:n + 2, :], 2 * T, tt)
                return out
            return evac

        gemm("wout", 8, 8, hh, hl, t_m, evac_add(16, stat), lead=4)
        att.close()
        t_h = modulated(8, 24, stat, t_xs)

        ffn = ExitStack()
        ph = sb("ph2", [P, NF, T], F32R, scope=ffn)
        pl = sb("pl2", [P, NF, T], F32R, scope=ffn)
        t_p = [None] * NF

        def centre(f, src, t):
            c, fc = tmp.get()
            act.wait(t, *fc)
            t1 = act.do(lambda e: e.activation(c[:, :], src, ACT.Identity, scale=col("cw2", f), bias=col("cb", f)))
            return c, t1

        def convolved(f, c, src, t1):
            dve.wait(t1)
            return dve.do(lambda e: e.scalar_tensor_tensor(out=c[:, 1:T], in0=src[:, 0:T - 1], scalar=col("cw1", f),
                                                           in1=c[:, 1:T], op0=ALU.mult, op1=ALU.add))

        def convolved2(f, c, src, t2):
            dve.wait(t2)
            return dve.do(lambda e: e.scalar_tensor_tensor(out=c[:, 2:T], in0=src[:, 0:T - 2], scalar=col("cw0", f),
                                                           in1=c[:, 2:T], op0=ALU.mult, op1=ALU.add))

        stage2, stage3 = [], []

        def second(n, v, tv, g, tg):
            dve.wait(tv, tg)
            t4 = dve.do(lambda e: e.tensor_tensor(v[:, :], v[:, :], g[:, :], ALU.mult))
            tmp.put(g, t4)
            act.wait(t4)
            return v, act.do(lambda e: e.activation(ph[:, n, :], v[:, :], ACT.Copy))

        def third(n, u, t5):
            dve.wait(t5)
            t6 = dve.do(lambda e: e.tensor_tensor(pl[:, n, :], u[:, :], ph[:, n, :].bitcast(F32), ALU.subtract))
            tmp.put(u, t6)
            t_p[n] = (t5, t6)

        def advance(item):
            if stage3:
                third(*stage3.pop(0))
            if stage2:
                m, *rest = stage2.pop(0)
                stage3.append((m, *second(m, *rest)))
            if item is not None:
                stage2.append(item)

        def evac_up(n, m, bank, t):
            f = n // 2
            v, tv = centre(f, bank[:, 0:T], t)
            g, tg = centre(NF + f, bank[:, T:2 * T], t)
            tv = convolved(f, v, bank[:, 0:T], tg)
            tg = convolved(NF + f, g, bank[:, T:2 * T], tg)
            tv = convolved2(f, v, bank[:, 0:T], tv)
            tg = convolved2(NF + f, g, bank[:, T:2 * T], tg)
            act.wait(tg)
            tg2 = act.do(lambda e: e.activation(g[:, :], g[:, :], ACT.Gelu_apprx_tanh))
            advance((f, v, tv, g, tg2))
            return [tv, tg]

        gemm("up2", 2 * NF, 8, hh, hl, t_h, evac_up, lead=4)
        while stage2 or stage3:
            advance(None)
        log_tables()
        stat = Stat(D, columns=False)
        gemm("dn2", 8, NF, ph, pl, t_p, evac_add(40, stat))
        ffn.close()
        R6, t_R6 = stat.get()
        for j in range(8):
            dve.wait(t_xs[j], t_R6)
            t = dve.do(lambda e, j=j: e.scalar_tensor_tensor(out=yb[:, j, :], in0=xT[:, j, :], scalar=col("gfin", j),
                                                             in1=R6[:, 0:T], op0=ALU.mult, op1=ALU.mult))
            if j % 4 == 3:
                sp.wait(t)
                sp.dma(a["out"][:, j - 3:j + 1, :], yb[:, j - 3:j + 1, :], s_out, 0)
        sp.wait((s_out, 32))
        assert wants["split"] == len(pieces)

        with nc.Block() as block:
            @block.sync
            def _(e):
                sp.play(e)

            @block.tensor
            def _(e):
                pe.play(e)

            @block.scalar
            def _(e):
                act.play(e)

            @block.vector
            def _(e):
                dve.play(e)

            @block.gpsimd
            def _(e):
                pool.play(e)


def _tiles(w, order=None):
    k, n = w.shape
    t = w.reshape(k // P, P, n // P, P).transpose(2, 0, 1, 3)
    return t if order is None else t[order]


def _lead(tiles):
    n, k = tiles.shape[:2]
    return np.concatenate([tiles[:4].swapaxes(0, 1).reshape(4 * k, P, P), tiles[4:].reshape(-1, P, P)])


def _by_chunk(tiles):
    return tiles.swapaxes(0, 1)


def _pieces(tiles):
    tiles = tiles.reshape(-1, P, P)
    return np.concatenate([tiles[i:i + PIECE].transpose(1, 0, 2).reshape(-1) for i in range(0, len(tiles), PIECE)])[None]


def _both(a, b):
    t = np.stack([_tiles(a), _tiles(b)], axis=1)
    return t.reshape(-1, *t.shape[2:])


def _tokens(w):
    k, n = w.shape
    return _pieces(w.reshape(k // P, P, n // 512, 4, P).transpose(2, 0, 3, 1, 4))


def _bucket_index():
    n = np.arange(256)
    large = 16 + (np.log(np.maximum(n, 16).astype(np.float32) / np.float32(16)) / np.float32(np.log(8.0))
                  * np.float32(16)).astype(np.int32)
    return np.where(n < 16, n, np.minimum(large, 31))


def _host(i):
    f = {k: np.asarray(v) for k, v in i.items()}
    o = {}
    o["xT"] = f["x"][0].T.reshape(8, P, T).transpose(1, 0, 2)
    o["pos"] = np.broadcast_to(f["positions"][0][None, :], (P, T))
    c8 = lambda v: v.reshape(-1, P).T
    inv = (np.float32(1.0) / (np.float32(10000.0) ** (np.arange(0, 64, 2, dtype=np.float32) / np.float32(64))))
    parts = dict(pre0=f["attn_pre_g"][0], pre1=f["attn_pre_g"][1], post0=f["attn_post_g"][0],
                 post1=f["attn_post_g"][1], fpre0=f["ffn_pre_g"][0], fpre1=f["ffn_pre_g"][1],
                 fpost0=f["ffn_post_g"][0], fpost1=f["ffn_post_g"][1], kvsrc=f["kv_src_g"], gq=f["mla_g_q"][0],
                 gkv=f["mla_g_kv"][0], gmix=f["g_mix_2"][0], gffn=f["g_ffn_2"][0], gfin=f["g_final_2"],
                 c=f["c_2"][0], bada=f["b_ada_2"][0], cw0=f["w_conv_2"][0, 0], cw1=f["w_conv_2"][0, 1],
                 cw2=f["w_conv_2"][0, 2], cb=f["b_conv_2"][0], inv=np.tile(inv.astype(np.float32), 4))
    o["cols"] = np.concatenate([c8(parts[n]) for n in COLS], axis=1)
    wa = f["mla_w_a"][0]
    k1, k2 = wa[:, 640:672], wa[:, 672:704]
    o["wa"] = _pieces(_lead(_tiles(np.concatenate([wa[:, 384:640], wa[:, :384]] + [k1] * 4 + [k2] * 4, axis=1))))
    uq = f["mla_w_uq"][0].reshape(384, 8, 192)
    rope = [uq[:, 4 * g:4 * g + 4, 128 + 32 * s:160 + 32 * s].reshape(384, P) for g in range(2) for s in range(2)]
    o["wuq"] = _pieces(_tiles(np.concatenate(rope + [uq[:, :, :128].reshape(384, 1024)], axis=1)))
    ukv = f["mla_w_ukv"][0].reshape(256, 8, 256)
    o["wuk"] = _pieces(_tiles(ukv[:, :, :128].reshape(256, 1024)))
    o["wuv"] = _tokens(ukv[:, :, 128:].reshape(256, 1024))
    o["wo0"] = _pieces(_by_chunk(_tiles(f["mla_w_o"][0])))
    for l in range(2):
        o[f"gu{l}"] = _pieces(_lead(_both(f["ffn_w_gate"][l], f["ffn_w_up"][l])))
        o[f"dn{l}"] = _pieces(_tiles(f["ffn_w_down"][l]))
    o["wkv_k"] = _pieces(_tiles(f["w_kv_shared"][:, :1024]))
    o["wkv_v"] = _tokens(f["w_kv_shared"][:, 1024:])
    o["wq1"] = _pieces(_lead(_tiles(f["b_w_q"][0])))
    o["wo1"] = _pieces(_by_chunk(_tiles(f["b_w_o"][0])))
    d = 128 + np.arange(P)[:, None] - np.arange(T)[None, :]
    o["relb"] = f["b_rel_table"][0][:, np.clip(d, -63, 256) + 63].transpose(1, 0, 2)
    o["relm"] = f["rel_bias_2"][:, _bucket_index()[np.clip(d, 0, 255)]].transpose(1, 0, 2)
    w = f["w_in_2"][0]
    qa, ka, va, qb, kb, vb = (w[:, 512 * j:512 * (j + 1)] for j in range(6))
    o["win_v"] = _tokens(np.concatenate([va, vb], axis=1))
    o["win_k"] = _pieces(_tiles(np.concatenate([ka, kb], axis=1)))
    o["win_q"] = _pieces(_tiles(np.concatenate([qa, qb], axis=1)))
    o["win_g"] = _pieces(_tiles(w[:, 3072:]))
    o["wbr"] = _pieces(np.stack([_tiles(f["w_br_moba_2"][0]), _tiles(f["w_br_sb_2"][0])], axis=1))
    o["wout"] = _pieces(_lead(_tiles(f["w_out_2"][0])))
    up = f["w_up_2"][0]
    o["up2"] = _pieces(_lead(_both(up[:, :FF], up[:, FF:])))
    o["dn2"] = _pieces(_tiles(f["w_down_2"][0]))
    o["wada"] = _pieces(f["w_ada_2"][0].reshape(8, P, 3, 16, P).transpose(2, 0, 3, 1, 4))
    return {k: np.ascontiguousarray(v) for k, v in o.items()}


def kernel(**inputs):
    import concourse.bacc as _bacc
    from concourse import mybir as _mybir
    from concourse.bass_utils import run_bass_kernel_spmd as _run

    nc = _bacc.Bacc("TRN2", target_bir_lowering=False, num_devices=1)
    arrays, aps = {}, {}
    for name, v in _host(inputs).items():
        arrays[f"in_{name}"] = v
        aps[name] = nc.dram_tensor(f"in_{name}", v.shape, _mybir.dt.from_np(v.dtype), kind="ExternalInput").ap()
    aps["out"] = nc.dram_tensor("out_0", (P, 8, T), F32, kind="ExternalOutput").ap()
    build(nc, aps)
    r = _run(nc, [arrays], core_ids=[0])
    got = r.results[0]["out_0"]
    return np.ascontiguousarray(got.transpose(1, 0, 2).reshape(D, T).T[None])
```

```python
from contextlib import ExitStack

import numpy as np
import concourse.bass as bass
from concourse import mybir

F32 = mybir.dt.float32
F32R = mybir.dt.float32r
I32 = mybir.dt.int32
ALU = mybir.AluOpType
ACT = mybir.ActivationFunctionType

T = 256
P = 128
D = 1024
FF = 2816
NF = FF // P
PIECE = 16
RAW = 4
SPLIT = 3
EPS = 1e-6
NEG = -1e30
PACE = (0.4, 0.5, 0.6, 0.6, 0.5, 0.4)
C1 = 6.28125
C2 = float(np.float32(0.0019353071795864769).view(np.uint32) & 0xFFFFF000 and
           (np.array([np.float32(0.0019353071795864769).view(np.uint32) & 0xFFFFE000], np.uint32).view(np.float32)[0]))
C3 = float(2.0 * np.pi - C1 - C2)
MAGIC = 12582912.0

COLS = {}
_at = 0
for _name, _n in (("pre0", 8), ("pre1", 8), ("post0", 8), ("post1", 8), ("fpre0", 8), ("fpre1", 8), ("fpost0", 8),
                  ("fpost1", 8), ("kvsrc", 8), ("gq", 3), ("gkv", 2), ("gmix", 8), ("gffn", 8), ("gfin", 8), ("c", 8),
                  ("bada", 48), ("cw0", 44), ("cw1", 44), ("cw2", 44), ("cb", 44), ("inv", 1)):
    COLS[_name] = (_at, _n)
    _at += _n
NCOL = _at

STREAM = [("wa", 56), ("wuk", 16), ("wuv", 16), ("wuq", 36), ("wo0", 64), ("gu0", 352), ("dn0", 176),
          ("wkv_v", 64), ("wkv_k", 64), ("wq1", 64), ("wo1", 64), ("gu1", 352), ("dn1", 176),
          ("win_v", 64), ("win_k", 64), ("win_q", 64), ("win_g", 128), ("wbr", 64), ("wout", 64),
          ("up2", 704 // 2), ("dn2", 176)]


class Lane:

    def __init__(self, name, sem):
        self.name, self.sem, self.count, self.ops, self.seen = name, sem, 0, [], {}

    def wait(self, *tokens):
        for t in tokens:
            if t is None:
                continue
            if isinstance(t, list) or isinstance(t[0], tuple):
                self.wait(*t)
                continue
            sem, value = t
            if self.seen.get(id(sem), 0) < value:
                self.seen[id(sem)] = value
                self.ops.append(lambda e, s=sem, v=value: e.wait_ge(s, v))

    def do(self, fn, mark=True):
        if not mark:
            self.ops.append(fn)
            return None
        self.count += 1
        self.ops.append(lambda e: fn(e).then_inc(self.sem, 1))
        return (self.sem, self.count)

    def dma(self, out, src, sem, value):
        self.ops.append(lambda e: e.dma_start(out, src).then_inc(sem, 16))
        return (sem, value)

    def play(self, e):
        for op in self.ops:
            op(e)


class Pool:

    def __init__(self, items):
        self.free = [(x, []) for x in items]

    def get(self):
        assert self.free, "no buffer is free"
        return self.free.pop(0)

    def put(self, item, *readers):
        self.free.append((item, list(readers)))


def build(nc, a):
    ctx = ExitStack()
    with ctx:
        def sb(name, shape, dt=F32, scope=ctx):
            return scope.enter_context(nc.sbuf_tensor("s_" + name, shape, dt))

        def sem(name):
            return ctx.enter_context(nc.semaphore(name))

        pe, act, dve, pool, sp = (Lane(n, sem("done_" + n)) for n in ("pe", "act", "dve", "pool", "sp"))

        raw = [sb(f"raw{i}", [P, PIECE * P]) for i in range(RAW)]
        whi = [sb(f"whi{i}", [P, PIECE * P], F32R) for i in range(SPLIT)]
        wlo = [sb(f"wlo{i}", [P, PIECE * P], F32R) for i in range(SPLIT)]
        xT = sb("xT", [P, 8, T])
        hh = sb("hh", [P, 8, T], F32R)
        hl = sb("hl", [P, 8, T], F32R)
        yb = sb("yb", [P, 8, T])
        adacc = sb("adacc", [P, 2048])
        cols = sb("cols", [P, NCOL])
        modv = sb("modv", [P, 48])
        cact = sb("cact", [P, 8])
        gs2 = sb("gs2", [P, 16])
        mask0 = sb("mask0", [P, T])
        ones = sb("ones", [P, P])
        tri = sb("tri", [P, P])
        negones = sb("negones", [P, P])
        ident = sb("ident", [P, P])
        Rt = Pool([sb(f"R{i}", [P, T + 2]) for i in range(3)])
        Lt = Pool([sb(f"L{i}", [P, T + 2]) for i in range(1)])
        sqacc = Pool([sb(f"sqacc{i}", [P, 2 * T]) for i in range(2)])
        squares = Pool([yb[:, 2 * i:2 * i + 2, :] for i in (3, 2, 1, 0)])
        tmp = Pool([sb(f"tmp{i}", [P, T]) for i in range(7)])
        small = Pool([sb(f"small{i}", [P, 8]) for i in range(6)])

        banks = Pool([ctx.enter_context(nc.psum_tensor(f"bank{i}", [P, 512], F32)) for i in range(8)])

        s_raw = [sem(f"s_raw{i}") for i in range(RAW)]
        s_in = [sem(f"s_in{i}") for i in range(6)]
        s_first = [sem(f"s_first{i}") for i in range(3)]
        s_out = sem("s_out")

        def col(name, j=0, n=1):
            at = COLS[name][0] + j
            return cols[:, at:at + n]

        cosb, sinb, posi = adacc[:, 0:T], adacc[:, T:2 * T], adacc[:, 2 * T:3 * T].bitcast(I32)
        t_pos = []

        t_cols = sp.dma(cols[:, :], a["cols"], s_in[1], 16)
        t_x = [sp.dma(xT[:, 0:4, :], a["xT"][:, 0:4, :], s_in[0], 16)] * 4

        pieces = []
        for name, n in STREAM:
            at = 0
            while at < n:
                k = min(PIECE, n - at)
                pieces.append(("w", name, at, k))
                at += k
        ada = [("ada", "wada", i * PIECE, PIECE) for i in range(24)]
        merged = []
        fed = 0
        for p in pieces:
            merged.append(p)
            if p[1] == "wkv_k" and p[2] in (16, 48):
                merged.append(ada.pop(0))
            if p[1] in ("gu0", "dn0", "gu1", "dn1"):
                fed += 1
                if fed in (5, 9, 13, 17, 21, 24, 27, 30) or (
                        fed > 33 and (fed % 3 == 0 or (p[1] == "dn1" and fed % 3 == 1))):
                    merged += ada[:1]
                    del ada[:1]
        assert not ada
        pieces = merged
        wants = {"dma": 0, "split": 0, "use": 0}
        slot_readers = [(None, [])] * RAW
        ada_sums = []
        split_free = Pool(list(range(SPLIT)))
        ready = {}
        acc_readers = [None]
        ada_done = {}

        def load_next():
            i = wants["dma"]
            _, name, at, k = pieces[i]
            assert i < RAW or slot_readers[i % RAW][0] == i - RAW
            sp.wait(*slot_readers[i % RAW][1])
            src = a[name][:, at * P * P:(at + k) * P * P].rearrange("a (p n) -> (a p) n", p=P)
            if i == 0:
                for c in range(4):
                    sp.dma(raw[0][:, 512 * c:512 * (c + 1)], src[:, 512 * c:512 * (c + 1)],
                           s_raw[0] if c == 3 else s_first[c], 0)
            else:
                sp.dma(raw[i % RAW][:, 0:k * P], src, s_raw[i % RAW], 0)
            wants["dma"] += 1
            if i == 0:
                t_x.extend([sp.dma(xT[:, 4:8, :], a["xT"][:, 4:8, :], s_in[5], 16)] * 4)
                t_pos.append(sp.dma(posi, a["pos"], s_in[2], 16))

        def arrived(i, c=3):
            if i == 0 and c < 3:
                return (s_first[c], 16)
            return (s_raw[i % RAW], 16 * (i // RAW + 1))

        pending = []
        t_cact = []
        fine = [False]
        background = [None]

        def load_ahead():
            while wants["dma"] < len(pieces) and (
                    wants["dma"] < RAW or slot_readers[wants["dma"] % RAW][0] == wants["dma"] - RAW):
                load_next()

        slow = []

        def split_slowly():
            i = wants["split"]
            kind, _, at, k = pieces[i]
            wants["split"] += 1
            src = raw[i % RAW]
            if kind == "ada":
                def parts():
                    load_ahead()
                    for c in range(4):
                        t = ada_product(i, slice(512 * c, 512 * (c + 1)))
                        if c < 3:
                            yield
                    ada_end(i, t)
                    load_ahead()
                slow.append(parts())
                return
            s, free = split_free.get()
            ready[i] = (s, [])

            def parts():
                load_ahead()
                t_hi = None
                high = 4 if i == 0 else 8
                for lo in range(0, k, 4):
                    w = slice(lo * P, min(lo + 4, k) * P)
                    if lo % high == 0:
                        w2 = slice(lo * P, min(lo + high, k) * P)
                        act.wait(arrived(i, lo // 4), *free)
                        t_hi = act.do(lambda e, w2=w2: e.activation(whi[s][:, w2], src[:, w2], ACT.Copy))
                        if i > 0:
                            yield
                    dve.wait(arrived(i, lo // 4), t_hi, *free)
                    t_lo = dve.do(lambda e, w=w: e.tensor_tensor(wlo[s][:, w], src[:, w], whi[s][:, w].bitcast(F32),
                                                                 ALU.subtract))
                    ready[i][1].append((t_hi, t_lo))
                    if lo + 4 < k:
                        yield
                slot_readers[i % RAW] = (i, [t_hi, t_lo] + ([t for r in ready[i][1] for t in r] if i == 0 else []))
                load_ahead()

            slow.append(parts())

        def slow_part():
            if slow:
                try:
                    next(slow[0])
                except StopIteration:
                    slow.pop(0)

        def split_high():
            while slow:
                slow_part()
            i = wants["split"]
            load_ahead()
            kind, _, at, k = pieces[i]
            wants["split"] += 1
            if kind == "ada":
                pending.append((i, None, None, ()))
                return
            s, free = split_free.get()
            src, w = raw[i % RAW], k * P
            act.wait(arrived(i), *free)
            t_hi = act.do(lambda e: e.activation(whi[s][:, 0:w], src[:, 0:w], ACT.Copy))
            pending.append((i, s, t_hi, free))

        def split_low():
            i, s, t_hi, free = pending.pop(0)
            _, _, at, k = pieces[i]
            src, w = raw[i % RAW], k * P
            if s is None:
                ada_end(i, ada_product(i, slice(0, 2048)))
                return
            dve.wait(arrived(i), t_hi, *free)
            t_lo = dve.do(lambda e: e.tensor_tensor(wlo[s][:, 0:w], src[:, 0:w], whi[s][:, 0:w].bitcast(F32),
                                                    ALU.subtract))
            slot_readers[i % RAW] = (i, [t_hi, t_lo])
            ready[i] = (s, [(t_hi, t_lo)] * 4)

        def ada_product(i, w):
            kc, src = (pieces[i][2] // PIECE) % 8, raw[i % RAW]
            if kc == 0 and ada_sums:
                ada_sum(*ada_sums.pop(0))
            if not t_cact:
                act.wait(t_cols)
                t_cact.append(act.do(lambda e: e.activation(cact[:, :], col("c", 0, 8), ACT.Silu)))
            dve.wait(arrived(i), t_cact[0])
            if kc == 0:
                dve.wait(acc_readers[0])
                return dve.do(lambda e: e.tensor_scalar(adacc[:, w], src[:, w], cact[:, 0:1], None, ALU.mult))
            dve.wait(ada_done["t"])
            return dve.do(lambda e: e.scalar_tensor_tensor(out=adacc[:, w], in0=src[:, w], scalar=cact[:, kc:kc + 1],
                                                           in1=adacc[:, w], op0=ALU.mult, op1=ALU.add))

        def ada_end(i, t):
            ada_done["t"] = t
            at = pieces[i][2]
            if (at // PIECE) % 8 == 7:
                ada_sums.append((at // PIECE // 8, t, wants["use"]))
            slot_readers[i % RAW] = (i, [t])

        def refill_high():
            while (wants["split"] < len(pieces) and wants["split"] < wants["use"] + RAW
                   and (split_free.free or pieces[wants["split"]][0] == "ada")):
                if (fine[0] or background[0] is not None) and not pending:
                    split_slowly()
                else:
                    split_high()

        def refill_low():
            while pending:
                split_low()
            while ada_sums and ada_sums[0][0] == 1 and wants["use"] > ada_sums[0][2] + 2:
                ada_sum(*ada_sums.pop(0))

        def refill():
            refill_high()
            refill_low()

        def ada_sum(g, t_acc, _, later=None):
            bank, free = banks.get()
            pe.wait(t_acc, t_const, *free)
            for j in range(16):
                t = pe.do(lambda e, j=j: e.matmul(bank[:, j:j + 1], adacc[:, j * P:(j + 1) * P], ones[:, 0:1],
                                                  start=True, stop=True), mark=(j == 15))
            acc_readers[0] = t

            def with_bias():
                dve.wait(t, t_cols)
                t2 = dve.do(lambda e: e.tensor_tensor(modv[:, g * 16:(g + 1) * 16], bank[:, 0:16],
                                                      col("bada", g * 16, 16), ALU.add))
                banks.put(bank, t2)
                mod_ready[g] = t2

            if later is None:
                with_bias()
            else:
                later.append(with_bias)

        mod_ready = {}

        class Weights:

            def __init__(self, name):
                self.name, self.left, self.at, self.i = name, 0, 0, None

            def tile(self, n=1):
                if self.left == 0:
                    i = wants["use"]
                    while pieces[i][0] == "ada":
                        i += 1
                    assert pieces[i][1] == self.name, (pieces[i], self.name)
                    wants["use"] = i + 1
                    while wants["split"] <= i:
                        split_high()
                    refill()
                    self.i, self.left, self.at = i, pieces[i][3], 0
                    self.s, self.parts = ready[i]
                at = self.at
                while len(self.parts) <= at // 4:
                    slow_part()
                pe.wait(self.parts[at // 4])
                self.at += n
                self.left -= n
                return (whi[self.s][:, at * P:(at + n) * P], wlo[self.s][:, at * P:(at + n) * P])

            def used(self, t):
                split_free.put(self.s, t)

        def product(wts, tiles, xh, xl, t_x, ks, nk, pace=0, marks=None):
            for k in ks:
                pe.wait(*t_x[k])
                a_h, a_l = xh[:, k, :], xl[:, k, :]
                for bank, j in tiles:
                    hi, lo = wts.tile()
                    out = bank[:, j * T:(j + 1) * T]
                    first = k == 0 and (j == 0 or len(tiles) == 1)
                    pe.do(lambda e, o=out, w=hi, x=a_h, f=first: e.matmul(o, w, x, start=f, stop=False,
                                                                          skip_group_check=True), mark=False)
                    pe.do(lambda e, o=out, w=hi, x=a_l: e.matmul(o, w, x, start=False, stop=False,
                                                                 skip_group_check=True), mark=False)
                    t = pe.do(lambda e, o=out, w=lo, x=a_h, k=k: e.matmul(o, w, x, start=False, stop=(k == nk - 1),
                                                                          skip_group_check=True),
                              mark=(wts.left == 0 or k == nk - 1))
                    if wts.left == 0:
                        wts.used(t)
                    if marks is not None and k == nk - 1:
                        marks.append(t)
                    walk(pace)
            return t

        credit = [0.0]

        def walk(pace):
            slow_part()
            credit[0] += pace
            while credit[0] >= 1:
                credit[0] -= 1
                step()

        def step():
            if background[0] is not None:
                try:
                    next(background[0])
                except StopIteration:
                    background[0] = None

        def drain():
            n = 0
            while background[0] is not None:
                step()
                n += 1
                assert n < 10000, "the background is stuck"

        def gemm(name, ntiles, nk, xh, xl, t_x, evac, lead=0, pace=0, keep=False):
            wts = Weights(name)
            credit[0] = 0.0
            n = 0
            while n < ntiles:
                group = []
                lead_now = lead if n == 0 else 0
                for b in range(max(1, lead_now // 2)):
                    bank, free = banks.get()
                    pe.wait(*free)
                    group.append((n + 2 * b, bank, min(2, ntiles - n - 2 * b)))
                if lead_now:
                    tiles = [(bank, j) for _, bank, m in group for j in range(m)]
                    t = product(wts, tiles, xh, xl, t_x, range(nk), nk, pace)
                else:
                    for j in range(group[0][2]):
                        t = product(wts, [(group[0][1], j)], xh, xl, t_x, range(nk), nk, pace)
                refill_high()
                for at, bank, m in group:
                    readers = evac(at, m, bank, t)
                    if not keep:
                        banks.put(bank, *readers)
                    n += m
                refill_low()

        def gemm_tokens(name, ngroups, nk, xh, xl, t_x, evac):
            wts = Weights(name)
            for g in range(ngroups):
                b0, f0 = banks.get()
                b1, f1 = banks.get()
                pe.wait(*f0, *f1)
                for k in range(nk):
                    hi, lo = wts.tile(4)
                    pe.wait(*t_x[k])
                    for tb, bank in ((0, b0), (1, b1)):
                        a_h, a_l = xh[:, k, tb * P:(tb + 1) * P], xl[:, k, tb * P:(tb + 1) * P]
                        pe.do(lambda e, b=bank, x=a_h, w=hi, k=k: e.matmul(b[:, :], x, w, start=(k == 0), stop=False),
                              mark=False)
                        pe.do(lambda e, b=bank, x=a_h, w=lo: e.matmul(b[:, :], x, w, start=False, stop=False),
                              mark=False)
                        t = pe.do(lambda e, b=bank, x=a_l, w=hi, k=k: e.matmul(b[:, :], x, w, start=False,
                                                                               stop=(k == nk - 1)))
                    if wts.left == 0:
                        wts.used(t)
                refill_high()
                for tb, bank in ((0, b0), (1, b1)):
                    banks.put(bank, *evac(g, tb, bank, t))
                refill_low()

        def t_pe_now():
            return (pe.sem, pe.count)

        class Stat:

            def __init__(self, n, columns=False):
                self.n, self.columns = n, columns
                self.t = None
                self.done = None
                self.bank = None
                self.begun = False

            def add(self, src, w, t_src):
                if self.t is None:
                    assert w == 2 * T
                    self.acc, free = sqacc.get()
                    act.wait(t_src, *free)
                    self.t = act.do(lambda e: e.activation(self.acc[:, :], src, ACT.Square))
                    return self.t
                sq, free = squares.get()
                act.wait(t_src, *free)
                n = w // T
                if n == 1:
                    sq_ = sq[:, 0, :]
                    acc = self.acc[:, 0:w]
                else:
                    sq_ = sq
                    acc = self.acc[:, :].rearrange("p (a b) -> p a b", a=2)
                t = act.do(lambda e: e.activation(sq_, src, ACT.Square))
                dve.wait(t, self.t)
                self.t = dve.do(lambda e: e.tensor_tensor(acc, acc, sq_, ALU.add))
                squares.put(sq, self.t)
                return t

            def begin(self):
                self.bank, free = banks.get()
                pe.wait(self.t, t_const, *free)
                if self.t is None:
                    return
                acc = self.acc
                self.first(acc[:, 0:T])
                self.t_sum = self.first(acc[:, T:2 * T])
                if not self.columns:
                    sqacc.put(acc, self.t_sum)

            def first(self, src):
                out, start = self.bank[:, 0:T], not self.begun
                self.begun = True
                return pe.do(lambda e: e.matmul(out, ones[:, :], src, start=start, stop=True,
                                                skip_group_check=True))

            def add_late(self, src, t_src):
                assert not self.columns
                if self.bank is None:
                    self.begin()
                sq, free = squares.get()
                act.wait(t_src, *free)
                t = act.do(lambda e: e.activation(sq, src, ACT.Square))
                pe.wait(t)
                self.first(sq[:, 0, :])
                self.t_sum = self.first(sq[:, 1, :])
                squares.put(sq, self.t_sum)
                return t

            def get(self):
                if self.done is not None:
                    return self.done
                if self.bank is None:
                    self.begin()
                bank, t, w = self.bank, self.t_sum, T
                if self.columns:
                    w = T + 2
                    acc = self.acc
                    for b in range(2):
                        at = T + b
                        pe.do(lambda e, at=at, b=b: e.matmul(bank[:, at:at + 1], acc[:, b * P:(b + 1) * P],
                                                             ones[:, 0:1], start=True, stop=False), mark=False)
                        t = pe.do(lambda e, at=at, b=b: e.matmul(bank[:, at:at + 1], acc[:, T + b * P:T + (b + 1) * P],
                                                                 ones[:, 0:1], start=False, stop=True))
                    sqacc.put(acc, t)
                R, rfree = Rt.get()
                log, lfree = Lt.get()
                act.wait(t, t_const, *lfree)
                t1 = act.do(lambda e: e.activation(log[:, 0:w], bank[:, 0:w], ACT.Ln, scale=1.0 / self.n,
                                                   bias=epsc[:, 0:1]))
                banks.put(bank, t1)
                act.wait(t1, *rfree)
                t2 = act.do(lambda e: e.activation(R[:, 0:w], log[:, 0:w], ACT.Exp, scale=-0.5))
                Lt.put(log, t2)
                self.done = (R, t2)
                return self.done

        def split_scaled(src, gain, oh, ol, t_src, free=()):
            act.wait(t_src, t_cols, *free)
            t_h = act.do(lambda e: e.activation(oh, src, ACT.Copy, scale=gain))
            dve.wait(t_h, t_src, t_cols, *free)
            t_l = dve.do(lambda e: e.scalar_tensor_tensor(out=ol, in0=src, scalar=gain, in1=oh.bitcast(F32),
                                                          op0=ALU.mult, op1=ALU.subtract))
            return (t_h, t_l)

        def split_plain(src, oh, ol, t_src, free=()):
            act.wait(t_src, *free)
            t_h = act.do(lambda e: e.activation(oh, src, ACT.Copy))
            dve.wait(t_h, t_src, *free)
            t_l = dve.do(lambda e: e.tensor_tensor(ol, src, oh.bitcast(F32), ALU.subtract))
            return (t_h, t_l)

        def pair(bank):
            return bank[:, :].rearrange("p (a b) -> p a b", a=2)

        def log_tables():
            act.do(lambda e: e.preload_act_table_set("natural_log_exp_and_others"), mark=False)

        def add_normed(ys, gain, stat, pre, columns=False):
            R, t_r = stat.get()
            later = []
            if gain.startswith("fpost"):
                while ada_sums:
                    ada_sum(*ada_sums.pop(0), later)
            t_xs, t_h, us = [None] * 8, [None] * 8, [None] * 8
            hi = [None] * 8
            nxt = Stat(D, columns)

            def low(j):
                dve.wait(hi[j])
                t_l = dve.do(lambda e, j=j: e.scalar_tensor_tensor(
                    out=hl[:, j, :], in0=xT[:, j, :], scalar=col(pre, j), in1=hh[:, j, :].bitcast(F32),
                    op0=ALU.mult, op1=ALU.subtract))
                t_h[j] = (hi[j], t_l)

            for j in range(9):
                if j < 8:
                    bank, half = ys[j]
                    u, ufree = tmp.get()
                    dve.wait(t_r, *ufree)
                    y = bank[:, half * T:(half + 1) * T]
                    t1 = dve.do(lambda e, j=j, u=u, y=y: e.scalar_tensor_tensor(
                        out=u[:, :], in0=y, scalar=col(gain, j), in1=R[:, 0:T], op0=ALU.mult, op1=ALU.mult))
                    us[j] = (u, t1)
                    if half == 1:
                        banks.put(bank, t1)
                    i = j
                    u, t1 = us[i]
                    dve.wait(t1)
                    t_xs[i] = dve.do(lambda e, i=i, u=u: e.tensor_tensor(xT[:, i, :], xT[:, i, :], u[:, :], ALU.add))
                    tmp.put(u, t_xs[i])
                    if pre is not None:
                        act.wait(t_xs[i])
                        hi[i] = act.do(lambda e, i=i: e.activation(hh[:, i, :], xT[:, i, :], ACT.Copy,
                                                                   scale=col(pre, i)))
                if 1 <= j < 9 and pre is not None:
                    low(j - 1)
                if pre is None and j % 2 == 1 and j < 8:
                    nxt.add_late(xT[:, j - 1:j + 1, :], t_xs[j])
            for fn in later:
                fn()
            Rt.put(R, us[7][1])
            if pre is not None:
                for j in range(0, 8, 2):
                    nxt.add(xT[:, j:j + 2, :], 2 * T, t_xs[j + 1])
            return t_h, nxt, t_xs

        epsc = sb("epsc", [P, 2])
        pool.do(lambda e: e.memset(epsc[:, 0:1], EPS), mark=False)
        pool.do(lambda e: e.memset(epsc[:, 1:2], float(np.pi / 2)), mark=False)
        pool.do(lambda e: e.memset(ones[:, :], 1.0), mark=False)
        pool.do(lambda e: e.memset(negones[:, :], -1.0), mark=False)
        pool.do(lambda e: e.memset(mask0[:, :], 0.0), mark=False)
        pool.do(lambda e: e.memset(ident[:, :], 0.0), mark=False)
        t_set = pool.do(lambda e: e.memset(tri[:, :], -1.0))
        pool.wait(t_set)
        pool.do(lambda e: e.memset(mask0[0:64, 192:256], NEG), mark=False)
        pool.do(lambda e: e.affine_select(out=ident[:, :], in_=ident[:, :], compare_op=ALU.not_equal, fill=1.0,
                                          base=0, pattern=[[-1, P]], channel_multiplier=1), mark=False)
        t_const = pool.do(lambda e: e.affine_select(out=tri[:, :], in_=tri[:, :], compare_op=ALU.is_ge, fill=0.0,
                                                    base=0, pattern=[[-1, P]], channel_multiplier=1))

        att = ExitStack()
        cq = yb
        held_cq = [squares.free.pop() for _ in range(3)]
        cqh = sb("cqh", [P, 5, T], F32R, scope=att)
        cql = sb("cql", [P, 5, T], F32R, scope=att)

        def attention_buffers(scope, tag, nq, nk_, out=None):
            oh, ol = out or (sb("oh" + tag, [P, 8, T], F32R, scope=scope), sb("ol" + tag, [P, 8, T], F32R, scope=scope))
            return dict(
                Q=sb("Q" + tag, [P, nq, T], scope=scope), K=sb("K" + tag, [P, nk_, T], scope=scope),
                V=sb("V" + tag, [P, 2, 1024], scope=scope),
                S=Pool([sb(f"S{tag}{i}", [P, 384], scope=scope) for i in range(3)]),
                PT=Pool([sb(f"PT{tag}{i}", [P, 384], scope=scope) for i in range(2)]),
                O=Pool([sb(f"O{tag}{i}", [P, 2, P], scope=scope) for i in range(2)]),
                oh=oh, ol=ol)

        A = attention_buffers(att, "0", 12, 10)
        Q0, K0, V0 = A["Q"], A["K"], A["V"]

        def rope_table():
            ang, f1 = tmp.get()
            k_, f2 = tmp.get()
            r_, f3 = tmp.get()
            dve.wait(*t_pos, t_cols, *f1, *f2, *f3)
            t = dve.do(lambda e: e.tensor_copy(r_[:, :], posi))
            dve.wait(t)
            t = dve.do(lambda e: e.tensor_scalar(ang[:, :], r_[:, :], col("inv"), None, ALU.mult))
            dve.wait(t)
            t = dve.do(lambda e: e.tensor_scalar(k_[:, :], ang[:, :], float(1 / (2 * np.pi)), MAGIC, ALU.mult,
                                                 ALU.add))
            dve.wait(t)
            t = dve.do(lambda e: e.tensor_scalar(k_[:, :], k_[:, :], -MAGIC, None, ALU.add))
            src, dst = ang, r_
            for c in (C1, C2, C3):
                dve.wait(t)
                t = dve.do(lambda e, c=c, s=src, d=dst: e.scalar_tensor_tensor(
                    out=d[:, :], in0=k_[:, :], scalar=-c, in1=s[:, :], op0=ALU.mult, op1=ALU.add))
                src, dst = dst, src
            dve.wait(t)
            t = dve.do(lambda e, s=src: e.tensor_scalar(s[:, :], s[:, :], 3.1415925, -3.1415925, ALU.min, ALU.max))
            act.wait(t, t_const)
            t1 = act.do(lambda e, s=src: e.activation(sinb, s[:, :], ACT.Sin))
            t2 = act.do(lambda e, s=src, d=dst: e.activation(d[:, :], s[:, :], ACT.Abs))
            act.wait(t2)
            t3 = act.do(lambda e, d=dst: e.activation(cosb, d[:, :], ACT.Sin, scale=-1.0, bias=epsc[:, 1:2]))
            for b in (ang, k_, r_):
                tmp.put(b, t1, t3)
            return [t1, t3]

        fine[0] = True
        refill_high()
        load_ahead()
        t_h = []
        for k in range(8):
            t_h.append(split_scaled(xT[:, k, :], col("pre0", k), hh[:, k, :], hl[:, k, :], t_x[k]))
            if k in (1, 3, 5, 7):
                slow_part()
        stat0 = Stat(D)
        for k in range(0, 8, 2):
            stat0.add(xT[:, k:k + 2, :], 2 * T, t_x[k])

        def scaled(dst, src, R, t_src, t_r, free=()):
            dve.wait(t_src, t_r, *free)
            return dve.do(lambda e: e.tensor_tensor(dst, src, R[:, 0:T], ALU.mult))

        stat_kv, stat_q = Stat(256, columns=True), Stat(384)
        t_cq = [None] * 5
        krt = []

        def evac_a(n, m, bank, t):
            R0, t_R0 = stat0.get()
            out = []
            for j in range(m):
                f = n + j
                src = bank[:, j * T:(j + 1) * T]
                if f < 5:
                    t1 = scaled(cq[:, f, :], src, R0, t, t_R0)
                    t_cq[f] = split_scaled(cq[:, f, :], col("gkv", f) if f < 2 else col("gq", f - 2), cqh[:, f, :],
                                           cql[:, f, :], t1)
                    if f == 1:
                        stat_kv.add(cq[:, 0:2, :], 2 * T, t1)
                    if f == 3:
                        stat_q.add(cq[:, 2:4, :], 2 * T, t1)
                    if f == 4:
                        stat_q.add(cq[:, 4, :], T, t1)
                else:
                    b, free = tmp.get()
                    t1 = scaled(b[:, :], src, R0, t, t_R0, free)
                    krt.append((b, t1))
                    if f == 6:
                        Rt.put(R0, t1)
                out.append(t1)
            return out

        for _ in range(5):
            slow_part()
        t_rope = rope_table()
        log_tables()
        gemm("wa", 7, 8, hh, hl, t_h, evac_a, lead=4)
        fine[0] = False

        def rotate(a1, a2, o1, o2, t_in):
            u, fu = tmp.get()
            v, fv = tmp.get()
            dve.wait(t_in, t_rope, *fu, *fv)
            dve.do(lambda e: e.tensor_tensor(u[:, :], a2, sinb, ALU.mult), mark=False)
            t2 = dve.do(lambda e: e.tensor_tensor(v[:, :], a1, sinb, ALU.mult))
            dve.wait(t2)
            dve.do(lambda e: e.tensor_tensor(o1, a1, cosb, ALU.mult), mark=False)
            t4 = dve.do(lambda e: e.tensor_tensor(o2, a2, cosb, ALU.mult))
            dve.wait(t4)
            dve.do(lambda e: e.tensor_tensor(o1, o1, u[:, :], ALU.subtract), mark=False)
            t6 = dve.do(lambda e: e.tensor_tensor(o2, o2, v[:, :], ALU.add))
            tmp.put(u, t6)
            tmp.put(v, t6)
            return t6

        t_K, t_V, t_Q = {}, {}, {}

        def evac_into(dst, toks, stat, free=(), base=0):
            def evac(n, m, bank, t):
                R, t_r = stat.get()
                dve.wait(t, t_r, *free)
                out = []
                for j in range(m):
                    tt = dve.do(lambda e, j=j: e.tensor_tensor(dst[:, base + n + j, :], bank[:, j * T:(j + 1) * T],
                                                               R[:, 0:T], ALU.mult))
                    toks[n + j] = tt
                    out.append(tt)
                return out
            return evac

        def evac_tokens(dst, toks, stat, free=()):
            def evac(g, tb, bank, t):
                R, t_r = stat.get() if stat is not None else (None, None)
                act.wait(t, t_r, *free)
                if R is None:
                    tt = act.do(lambda e: e.activation(dst[:, tb, g * 512:(g + 1) * 512], bank[:, :], ACT.Copy))
                else:
                    tt = act.do(lambda e: e.activation(dst[:, tb, g * 512:(g + 1) * 512], bank[:, :], ACT.Copy,
                                                       scale=R[:, T + tb:T + tb + 1]))
                toks[g] = tt
                return [tt]
            return evac

        for buffer, _ in held_cq:
            squares.put(buffer, *t_cq)
        gemm("wuk", 8, 2, cqh, cql, t_cq, evac_into(K0, t_K, stat_kv))
        gemm_tokens("wuv", 2, 2, cqh, cql, t_cq, evac_tokens(V0, t_V, stat_kv))
        (k1b, tk1), (k2b, tk2) = krt
        t_krope = rotate(k1b[:, :], k2b[:, :], K0[:, 8, :], K0[:, 9, :], tk2)
        tmp.put(k1b, t_krope)
        tmp.put(k2b, t_krope)

        def out_chunk(A, c, o, t_o):
            bank, free = banks.get()
            pe.wait(t_o, t_const, *free)
            pe.do(lambda e: e.transpose(bank[:, 0:P], o[:, 0, :], ident[:, :]), mark=False)
            t = pe.do(lambda e: e.transpose(bank[:, P:T], o[:, 1, :], ident[:, :]))
            A["O"].put(o, t)
            oh, ol = A["oh"][:, c, :], A["ol"][:, c, :]
            t_hl = split_plain(bank[:, 0:T], oh, ol, t)
            banks.put(bank, *t_hl)
            A["t_o"][c] = t_hl

        def values(A, h, dv, v0, left, right, t_in, scale, release):
            bank, free = banks.get()
            pe.wait(t_in, *free)
            pe.wait(*A["t_v"](h))
            VL = A["V"]
            p = left
            pe.do(lambda e: e.matmul(bank[:, 0:dv], p[:, 0:P], VL[:, 0, v0:v0 + dv], start=True, stop=True),
                  mark=False)
            pe.do(lambda e: e.matmul(bank[:, dv:2 * dv], p[:, P:T], VL[:, 0, v0:v0 + dv], start=True, stop=False),
                  mark=False)
            t = pe.do(lambda e: e.matmul(bank[:, dv:2 * dv], p[:, T:384], VL[:, 1, v0:v0 + dv], start=False,
                                         stop=True))
            release(t)
            per = P // dv
            if h % per == 0:
                A["o_now"] = A["O"].get()
                A["o_toks"] = []
            o, ofree = A["o_now"]
            at = (h % per) * dv
            toks = []
            for qb in range(2):
                dve.wait(t, *ofree)
                if scale is None:
                    tt = dve.do(lambda e, qb=qb: e.tensor_copy(o[:, qb, at:at + dv], bank[:, qb * dv:(qb + 1) * dv]))
                else:
                    rinv, t_rinv = scale
                    dve.wait(t_rinv)
                    tt = dve.do(lambda e, qb=qb: e.tensor_scalar(o[:, qb, at:at + dv], bank[:, qb * dv:(qb + 1) * dv],
                                                                 rinv[:, qb:qb + 1], None, ALU.mult))
                toks.append(tt)
            banks.put(bank, tt)
            A["o_toks"] += toks
            return h % per == per - 1, o, A["o_toks"], tt

        def soft_scores(A, h, parts, t_in, bias, scale):
            bank, free = banks.get()
            pe.wait(t_in, *free)
            n = len(parts)
            for i, (q, k) in enumerate(parts):
                t = pe.do(lambda e, q=q, k=k, i=i: e.matmul(bank[:, 0:P], q[:, 0:P], k[:, 0:P], start=(i == 0),
                                                            stop=(i == n - 1)), mark=False)
            for i, (q, k) in enumerate(parts):
                t = pe.do(lambda e, q=q, k=k, i=i: e.matmul(bank[:, P:384], q[:, P:T], k, start=(i == 0),
                                                            stop=(i == n - 1)), mark=(i == n - 1))
            s, sfree = A["S"].get()
            w, wfree = small.get()
            dve.wait(t, A["t_bias"], *sfree, *wfree)
            dve.do(lambda e: e.tensor_tensor_reduce(out=s[:, 0:P], in0=bank[:, 0:P], in1=bias[:, P:T], scale=1.0,
                                                    scalar=-3e38, op0=ALU.add, op1=ALU.max, accum_out=w[:, 0:1]))
            t1 = dve.do(lambda e: e.tensor_tensor_reduce(out=s[:, P:384], in0=bank[:, P:384], in1=bias[:, 0:T],
                                                         scale=1.0, scalar=-3e38, op0=ALU.add, op1=ALU.max,
                                                         accum_out=w[:, 1:2]))
            banks.put(bank, t1)
            dve.wait(t1)
            t2 = dve.do(lambda e: e.tensor_scalar(w[:, 2:4], w[:, 0:2], -scale, None, ALU.mult))
            act.wait(t2)
            act.do(lambda e: e.activation(s[:, 0:P], s[:, 0:P], ACT.Exp, scale=scale, bias=w[:, 2:3],
                                          accum_out=w[:, 4:5]))
            t3 = act.do(lambda e: e.activation(s[:, P:384], s[:, P:384], ACT.Exp, scale=scale, bias=w[:, 3:4],
                                               accum_out=w[:, 5:6]))
            return s, w, t3

        def soft_transposed(A, got):
            s, w, t3 = got
            bank, free = banks.get()
            pe.wait(t3, t_const, *free)
            for i in range(3):
                t = pe.do(lambda e, i=i: e.transpose(bank[:, i * P:(i + 1) * P], s[:, i * P:(i + 1) * P],
                                                     ident[:, :]), mark=(i == 2))
            A["S"].put(s, t)
            pt, pfree = A["PT"].get()
            act.wait(t, *pfree)
            t4 = act.do(lambda e: e.activation(pt[:, :], bank[:, 0:384], ACT.Copy))
            banks.put(bank, t4)
            dve.wait(t3)
            t5 = dve.do(lambda e: e.reciprocal(w[:, 6:8], w[:, 4:6]))
            return pt, w, t4, t5

        def soft_attention(A, heads, dv, parts_of, scale, depth=2):
            ahead, whole = [], []
            for h in list(heads) + [None] * depth:
                while h is not None and not A["have"](h):
                    yield
                before = ahead.pop(0) if len(ahead) == depth or (h is None and ahead) else None
                if before is not None:
                    pt, w, t4, t5 = soft_transposed(A, before[1])
                    yield
                if whole:
                    out_chunk(A, *whole.pop(0))
                    yield
                if h is not None:
                    parts, t_in, bias = parts_of(h)
                    ahead.append((h, soft_scores(A, h, parts, t_in, bias, scale)))
                    yield
                if before is not None:
                    i = before[0]
                    full, o, toks, last = values(A, i, dv, A["v0"](i), pt, None, t4, (w[:, 6:8], t5),
                                                 lambda t: A["PT"].put(pt, t))
                    small.put(w, last)
                    if full:
                        whole.append((i * dv // P, o, toks))
                    yield
            out_chunk(A, *whole.pop(0))

        t_qr = {}

        def mla_parts(h):
            g = h % 4
            c = h // 4
            lo, hi = 32 * g, 32 * g + 32
            return ([(Q0[:, h, :], K0[:, h, :]), (Q0[lo:hi, 8 + c, :], K0[lo:hi, 8, :]),
                     (Q0[lo:hi, 10 + c, :], K0[lo:hi, 9, :])], [t_Q[h], t_K[h], t_qr[c], t_krope], mask0)

        A.update(t_o=[None] * 8, t_v=lambda h: [t_V[h // 4]], v0=lambda h: h * P, t_bias=t_const,
                 have=lambda h: h in t_Q and (h // 4) in t_qr)
        background[0] = soft_attention(A, range(8), P, mla_parts, float(192.0 ** -0.5), 1)

        ORDER = [8, 10, 9, 11, 0, 1, 2, 3, 4, 5, 6, 7]

        def evac_q(n, m, bank, t):
            R, t_r = stat_q.get()
            out = []
            dve.wait(t, t_r)
            for j in range(m):
                d = ORDER[n + j]
                tt = dve.do(lambda e, j=j, d=d: e.tensor_tensor(Q0[:, d, :], bank[:, j * T:(j + 1) * T], R[:, 0:T],
                                                                ALU.mult))
                if d < 8:
                    t_Q[d] = tt
                out.append(tt)
            if n < 4:
                c = n // 2
                t_qr[c] = rotate(Q0[:, 8 + c, :], Q0[:, 10 + c, :], Q0[:, 8 + c, :], Q0[:, 10 + c, :], tt)
            return out

        gemm("wuq", 12, 3, cqh[:, 2:5, :], cql[:, 2:5, :], t_cq[2:5], evac_q, pace=PACE[0])

        def project_out(name, A, pace):
            wts = Weights(name)
            stat = Stat(D)
            held = []
            for _ in range(4):
                bank, free = banks.get()
                pe.wait(*free)
                held.append(bank)
            tiles = [(bank, j) for bank in held for j in range(2)]
            for k in range(8):
                while A["t_o"][k] is None:
                    step()
                marks = []
                product(wts, tiles, A["oh"], A["ol"], A["t_o"], [k], 8, pace, marks)
                if k < 7:
                    refill()
            for i, bank in enumerate(held):
                if i < 3:
                    stat.add(bank[:, :], 2 * T, marks[2 * i + 1])
                else:
                    stat.add_late(pair(bank), marks[2 * i + 1])
            return tiles, stat

        ys, stat = project_out("wo0", A, PACE[1])
        Rt.put(stat_kv.get()[0], t_V[1], t_K[7])
        Rt.put(stat_q.get()[0], t_Q[7])
        t_h, stat, t_xs = add_normed(ys, "post0", stat, "fpre0")
        att.close()

        def feed_forward(layer, t_h, stat1, pre):
            scope = ExitStack()
            ph = sb(f"ph{layer}", [P, NF, T], F32R, scope=scope)
            pl = sb(f"pl{layer}", [P, NF, T], F32R, scope=scope)
            t_p = [None] * NF
            late = []

            def first(n, bank, t):
                R, t_r = stat1.get()
                g, fg = tmp.get()
                u, fu = tmp.get()
                dve.wait(t, t_r, *fg, *fu)
                t1 = dve.do(lambda e: e.tensor_tensor(g[:, :], bank[:, 0:T], R[:, 0:T], ALU.mult))
                t2 = dve.do(lambda e: e.tensor_tensor(u[:, :], bank[:, T:2 * T], R[:, 0:T], ALU.mult))
                act.wait(t1)
                t3 = act.do(lambda e: e.activation(g[:, :], g[:, :], ACT.Silu))
                return g, u, t2, t3

            def second(n, g, u, t2, t3):
                dve.wait(t2, t3)
                t4 = dve.do(lambda e: e.tensor_tensor(u[:, :], u[:, :], g[:, :], ALU.mult))
                tmp.put(g, t4)
                act.wait(t4)
                t5 = act.do(lambda e: e.activation(ph[:, n, :], u[:, :], ACT.Copy))
                return u, t5

            def third(n, u, t5):
                dve.wait(t5)
                t6 = dve.do(lambda e: e.tensor_tensor(pl[:, n, :], u[:, :], ph[:, n, :].bitcast(F32), ALU.subtract))
                tmp.put(u, t6)
                t_p[n] = (t5, t6)

            stage2, stage3 = [], []

            def advance(n, item):
                if stage3:
                    third(*stage3.pop(0))
                if stage2:
                    m, *rest = stage2.pop(0)
                    stage3.append((m, *second(m, *rest)))
                if item is not None:
                    stage2.append((n, *item))

            def evac(n, m, bank, t):
                item = first(n // 2, bank, t)
                advance(n // 2, item)
                return [item[2]]

            fine[0] = False
            gemm(f"gu{layer}", 2 * NF, 8, hh, hl, t_h, evac, lead=4)
            while stage2 or stage3:
                advance(None, None)
            log_tables()
            Rt.put(stat1.get()[0], t_p[NF - 1][1])
            stat = Stat(D)
            ys = []

            def evac_y(n, m, bank, t):
                if n < 6:
                    stat.add(bank[:, :], 2 * T, t)
                else:
                    stat.add_late(pair(bank), t)
                ys.extend([(bank, 0), (bank, 1)])

            fine[0] = True
            gemm(f"dn{layer}", 8, NF, ph, pl, t_p, evac_y, lead=2, keep=True)
            fine[0] = False
            out = add_normed(ys, f"fpost{layer}", stat, pre, pre == "kvsrc")
            scope.close()
            return out

        t_h, stat, t_xs = feed_forward(0, t_h, stat, "kvsrc")
        stat_x1 = stat

        att = ExitStack()
        A = attention_buffers(att, "1", 8, 8, (hh, hl))
        qh = sb("qh", [P, 8, T], F32R, scope=att)
        ql = sb("ql", [P, 8, T], F32R, scope=att)
        Q1, K1, V1 = A["Q"], A["K"], A["V"]
        bias1 = sb("bias1", [P, 16, T], scope=att)
        t_free = t_pe_now()
        sp.wait(t_free)
        t_bias = sp.dma(bias1[:, :, :], a["relb"], s_in[3], 16)
        pool.wait(t_bias)
        t_b8 = pool.do(lambda e: e.tensor_scalar(bias1[:, :, :], bias1[:, :, :], 8.0, None, ALU.mult))
        pool.wait(t_b8)
        t_bm = pool.do(lambda e: e.memset(bias1[0:64, :, 192:256], NEG))
        t_K, t_V, t_Q = {}, {}, {}
        gemm_tokens("wkv_v", 2, 8, hh, hl, t_h, evac_tokens(V1, t_V, stat_x1))
        t_q = [split_scaled(xT[:, k, :], col("pre1", k), qh[:, k, :], ql[:, k, :], t_xs[k], (t_free,))
               for k in range(8)]
        gemm("wkv_k", 8, 8, hh, hl, t_h, evac_into(K1, t_K, stat_x1))

        def b_parts(h, Q1=Q1, K1=K1, t_Q=t_Q, t_K=t_K):
            lo = 64 * (h % 2)
            c = h // 2
            return ([(Q1[lo:lo + 64, c, :], K1[lo:lo + 64, c, :])], [t_Q[c], t_K[c]], bias1[:, h, :])

        A.update(t_o=[None] * 8, t_v=lambda h, t_V=t_V: [t_V[h // 8]], v0=lambda h: h * 64, t_bias=t_bm,
                 have=lambda h, t_Q=t_Q: (h // 2) in t_Q)
        background[0] = soft_attention(A, range(16), 64, b_parts, 0.125)
        gemm("wq1", 8, 8, qh, ql, t_q, evac_into(Q1, t_Q, stat_x1), lead=2, pace=PACE[2])
        ys, stat = project_out("wo1", A, PACE[3])
        Rt.put(stat_x1.get()[0], t_Q[7], t_V[1])
        t_h, stat, t_xs = add_normed(ys, "post1", stat, "fpre1")
        att.close()
        t_h, stat, t_xs = feed_forward(1, t_h, stat, None)

        while ada_sums:
            ada_sum(*ada_sums.pop(0))
        dve.wait(mod_ready[0], mod_ready[1], mod_ready[2])
        dve.do(lambda e: e.scalar_tensor_tensor(out=gs2[:, 0:8], in0=modv[:, 8:16], scalar=1.0, in1=col("gmix", 0, 8),
                                                op0=ALU.add, op1=ALU.mult))
        t_gs = dve.do(lambda e: e.scalar_tensor_tensor(out=gs2[:, 8:16], in0=modv[:, 32:40], scalar=1.0,
                                                       in1=col("gffn", 0, 8), op0=ALU.add, op1=ALU.mult))

        def modulated(g0, s0, stat, t_xs, free=()):
            R, t_r = stat.get()
            out = []

            def low(j, u, t2):
                dve.wait(t2)
                t3 = dve.do(lambda e, j=j, u=u: e.scalar_tensor_tensor(
                    out=hl[:, j, :], in0=u[:, :], scalar=modv[:, s0 + j:s0 + j + 1], in1=hh[:, j, :].bitcast(F32),
                    op0=ALU.add, op1=ALU.subtract))
                tmp.put(u, t3)
                out.append((t2, t3))

            last = None
            for j in range(8):
                u, fu = tmp.get()
                dve.wait(t_xs[j], t_r, t_gs, *fu)
                t1 = dve.do(lambda e, j=j, u=u: e.scalar_tensor_tensor(
                    out=u[:, :], in0=xT[:, j, :], scalar=gs2[:, g0 + j:g0 + j + 1], in1=R[:, 0:T], op0=ALU.mult,
                    op1=ALU.mult))
                act.wait(t1, mod_ready[0], mod_ready[1], *free)
                t2 = act.do(lambda e, j=j, u=u: e.activation(hh[:, j, :], u[:, :], ACT.Identity,
                                                             bias=modv[:, s0 + j:s0 + j + 1]))
                if last is not None:
                    low(*last)
                last = (j, u, t2)
            low(*last)
            Rt.put(R, t1)
            return out

        t_h = modulated(0, 0, stat, t_xs)
        att = ExitStack()
        A = attention_buffers(att, "2", 8, 8)
        Q2, K2, V2 = A["Q"], A["K"], A["V"]
        gates = yb
        held_g = [squares.get() for _ in range(4)]
        gates2 = adacc
        t_K, t_V, t_Q, t_G = {}, {}, {}, {}
        bias2 = sb("bias2", [P, 8, T], scope=att)
        sp.wait(t_pe_now())
        t_bias2 = sp.dma(bias2[:, :, :], a["relm"], s_in[4], 16)
        pool.wait(t_bias2)
        t_b8 = pool.do(lambda e: e.tensor_scalar(bias2[:, 0:8, :], bias2[:, 0:8, :], 8.0, None, ALU.mult))
        pool.wait(t_b8)
        t_bm2 = pool.do(lambda e: e.affine_select(out=bias2[:, 0:8, :], in_=bias2[:, 0:8, :], compare_op=ALU.is_ge,
                                                  fill=NEG, base=128, pattern=[[0, 8], [-1, T]],
                                                  channel_multiplier=1))

        def evac_copy(dst_of, toks):
            def evac(n, m, bank, t):
                act.wait(t)
                out = []
                for j in range(m):
                    tt = act.do(lambda e, j=j: e.activation(dst_of(n + j), bank[:, j * T:(j + 1) * T], ACT.Copy))
                    toks[n + j] = tt
                    out.append(tt)
                return out
            return evac

        gemm_tokens("win_v", 2, 8, hh, hl, t_h, evac_tokens(V2, t_V, None), )
        gemm("win_k", 8, 8, hh, hl, t_h, evac_copy(lambda n: K2[:, n, :], t_K))

        def m_parts(h, Q2=Q2, K2=K2, t_Q=t_Q, t_K=t_K):
            lo = 64 * (h % 2)
            c = h // 2
            return ([(Q2[lo:lo + 64, c, :], K2[lo:lo + 64, c, :])], [t_Q[c], t_K[c]], bias2[:, h, :])

        def stick_scores(A, h):
            lo = 64 * (h % 2)
            c = h // 2
            q, k = Q2[lo:lo + 64, c, :], K2[lo:lo + 64, c, :]
            bank, free = banks.get()
            pe.wait(t_Q[c], t_K[c], *free)
            pe.do(lambda e: e.matmul(bank[:, 0:T], k[:, 0:P], q, start=True, stop=True), mark=False)
            t = pe.do(lambda e: e.matmul(bank[:, T:384], k[:, P:T], q[:, P:T], start=False, stop=True,
                                         skip_group_check=True))
            s, sfree = A["S"].get()
            r, rfree = A["PT"].get()
            act.wait(t, *sfree)
            t1 = act.do(lambda e: e.activation(s[:, :], bank[:, 0:384], ACT.Abs))
            act.wait(t1)
            t2 = act.do(lambda e: e.activation(s[:, :], s[:, :], ACT.Exp, scale=-0.125))
            act.wait(t2)
            t3 = act.do(lambda e: e.activation(s[:, :], s[:, :], ACT.Ln, bias=ones[:, 0:1]))
            dve.wait(t1, *rfree)
            t4 = dve.do(lambda e: e.tensor_scalar(r[:, :], bank[:, 0:384], 0.0, None, ALU.max))
            dve.wait(t3, t4)
            t5 = dve.do(lambda e: e.scalar_tensor_tensor(out=r[:, :], in0=s[:, :], scalar=8.0, in1=r[:, :],
                                                         op0=ALU.mult, op1=ALU.add))
            A["S"].put(s, t5)
            t6 = past_only(r, t5)
            return bank, r, [t1, t4, t6]

        def past_only(r, t):
            pool.wait(t)
            pool.do(lambda e: e.affine_select(out=r[:, 0:P], in_=r[:, 0:P], compare_op=ALU.is_gt, fill=0.0,
                                              base=0, pattern=[[1, P]], channel_multiplier=-1), mark=False)
            return pool.do(lambda e: e.affine_select(out=r[:, T:384], in_=r[:, T:384], compare_op=ALU.is_gt, fill=0.0,
                                                     base=0, pattern=[[1, P]], channel_multiplier=-1))

        def stick_sums(A, got):
            bank, r, toks = got
            pe.wait(toks, t_const)
            pe.do(lambda e: e.matmul(bank[:, 0:T], tri[:, :], r[:, 0:T], start=False, stop=False,
                                     skip_group_check=True), mark=False)
            pe.do(lambda e: e.matmul(bank[:, P:T], negones[:, :], r[:, T:384], start=False, stop=False,
                                     skip_group_check=True), mark=False)
            t = pe.do(lambda e: e.matmul(bank[:, T:384], tri[:, :], r[:, T:384], start=False, stop=True,
                                         skip_group_check=True))
            s, sfree = A["S"].get()
            dve.wait(t, *sfree)
            t1 = dve.do(lambda e: e.tensor_scalar(s[:, :], bank[:, 0:384], 0.0, None, ALU.min))
            banks.put(bank, t1)
            A["PT"].put(r, t)
            act.wait(t1)
            t2 = act.do(lambda e: e.activation(s[:, :], s[:, :], ACT.Exp, scale=0.125))
            return s, past_only(s, t2)

        def stick_attention(A, heads):
            ahead, whole = [], []

            for h in list(heads) + [None] * 2:
                while h is not None and not A["have"](h):
                    yield
                before = ahead.pop(0) if len(ahead) == 2 or (h is None and ahead) else None
                if before is not None:
                    s, t6 = stick_sums(A, before[1])
                    yield
                if whole:
                    out_chunk(A, *whole.pop(0))
                    yield
                if h is not None:
                    ahead.append((h, stick_scores(A, h)))
                    yield
                if before is not None:
                    i = before[0]
                    full, o, toks, _ = values(A, i, 64, i * 64, s, None, t6, None, lambda t: A["S"].put(s, t))
                    if full:
                        whole.append((i // 2, o, toks))
                    yield
            out_chunk(A, *whole.pop(0))

        def both(A):
            yield from soft_attention(A, range(8), 64, m_parts, 0.125)
            yield
            yield from stick_attention(A, range(8, 16))

        A.update(t_o=[None] * 8, t_v=lambda h, t_V=t_V: [t_V[h // 8]], v0=lambda h: h * 64, t_bias=t_bm2,
                 have=lambda h, t_Q=t_Q: (h // 2) in t_Q)
        background[0] = both(A)
        act.wait(*[t for _, free in held_g for t in free])
        gemm("win_q", 8, 8, hh, hl, t_h, evac_copy(lambda n: Q2[:, n, :], t_Q), pace=PACE[4])
        act.wait(acc_readers[0])
        gemm("win_g", 16, 8, hh, hl, t_h,
             evac_copy(lambda n: gates[:, n, :] if n < 8 else gates2[:, (n - 8) * T:(n - 7) * T], t_G), pace=PACE[5])
        drain()
        act.wait(t_G[15])
        t_g1 = act.do(lambda e: e.activation(gates[:, :, :], gates[:, :, :], ACT.Sigmoid))
        t_g2 = act.do(lambda e: e.activation(gates2[:, :], gates2[:, :], ACT.Sigmoid))
        log_tables()

        t_m = [None] * 8

        def mixed_low(n, u, t_hi):
            dve.wait(t_hi)
            t_lo = dve.do(lambda e: e.tensor_tensor(hl[:, n, :], u[:, :], hh[:, n, :].bitcast(F32), ALU.subtract))
            t_m[n] = (t_hi, t_lo)
            tmp.put(u, t_lo)

        low = None
        wts = Weights("wbr")
        for n in range(8):
            bank, free = banks.get()
            pe.wait(*free)
            for b in range(2):
                t = product(wts, [(bank, b)], A["oh"][:, 4 * b:4 * b + 4, :], A["ol"][:, 4 * b:4 * b + 4, :],
                            A["t_o"][4 * b:4 * b + 4], range(4), 4)
            refill_high()
            u, fu = tmp.get()
            v, fv = tmp.get()
            dve.wait(t, t_g1, t_g2, *fu, *fv)
            t1 = dve.do(lambda e, n=n, u=u, bank=bank: e.tensor_tensor(u[:, :], bank[:, 0:T], gates[:, n, :],
                                                                       ALU.mult))
            t2 = dve.do(lambda e, n=n, v=v, bank=bank: e.tensor_tensor(v[:, :], bank[:, T:2 * T],
                                                                       gates2[:, n * T:(n + 1) * T], ALU.mult))
            banks.put(bank, t2)
            if low is not None:
                mixed_low(*low)
            dve.wait(t1, t2)
            t3 = dve.do(lambda e, u=u, v=v: e.tensor_tensor(u[:, :], u[:, :], v[:, :], ALU.add))
            tmp.put(v, t3)
            act.wait(t3)
            low = (n, u, act.do(lambda e, n=n, u=u: e.activation(hh[:, n, :], u[:, :], ACT.Copy)))
            refill_low()
        mixed_low(*low)
        for buffer, _ in held_g:
            squares.put(buffer, t1)
        stat = Stat(D)
        t_xs = [None] * 8

        def evac_add(gate0, after):
            def evac(n, m, bank, t):
                out = []
                for j in range(m):
                    dve.wait(t)
                    tt = dve.do(lambda e, j=j: e.scalar_tensor_tensor(
                        out=xT[:, n + j, :], in0=bank[:, j * T:(j + 1) * T],
                        scalar=modv[:, gate0 + n + j:gate0 + n + j + 1], in1=xT[:, n + j, :], op0=ALU.mult,
                        op1=ALU.add))
                    t_xs[n + j] = tt
                    out.append(tt)
                if n < 6:
                    after.add(xT[:, n:n + 2, :], 2 * T, tt)
                else:
                    after.add_late(xT[:, n:n + 2, :], tt)
                return out
            return evac

        gemm("wout", 8, 8, hh, hl, t_m, evac_add(16, stat), lead=4)
        att.close()
        t_h = modulated(8, 24, stat, t_xs)

        ffn = ExitStack()
        ph = sb("ph2", [P, NF, T], F32R, scope=ffn)
        pl = sb("pl2", [P, NF, T], F32R, scope=ffn)
        t_p = [None] * NF

        def centre(f, src, t):
            c, fc = tmp.get()
            act.wait(t, *fc)
            t1 = act.do(lambda e: e.activation(c[:, :], src, ACT.Identity, scale=col("cw2", f), bias=col("cb", f)))
            return c, t1

        def convolved(f, c, src, t1):
            dve.wait(t1)
            return dve.do(lambda e: e.scalar_tensor_tensor(out=c[:, 1:T], in0=src[:, 0:T - 1], scalar=col("cw1", f),
                                                           in1=c[:, 1:T], op0=ALU.mult, op1=ALU.add))

        def convolved2(f, c, src, t2):
            dve.wait(t2)
            return dve.do(lambda e: e.scalar_tensor_tensor(out=c[:, 2:T], in0=src[:, 0:T - 2], scalar=col("cw0", f),
                                                           in1=c[:, 2:T], op0=ALU.mult, op1=ALU.add))

        stage2, stage3 = [], []

        def second(n, v, tv, g, tg):
            dve.wait(tv, tg)
            t4 = dve.do(lambda e: e.tensor_tensor(v[:, :], v[:, :], g[:, :], ALU.mult))
            tmp.put(g, t4)
            act.wait(t4)
            return v, act.do(lambda e: e.activation(ph[:, n, :], v[:, :], ACT.Copy))

        def third(n, u, t5):
            dve.wait(t5)
            t6 = dve.do(lambda e: e.tensor_tensor(pl[:, n, :], u[:, :], ph[:, n, :].bitcast(F32), ALU.subtract))
            tmp.put(u, t6)
            t_p[n] = (t5, t6)

        def advance(item):
            if stage3:
                third(*stage3.pop(0))
            if stage2:
                m, *rest = stage2.pop(0)
                stage3.append((m, *second(m, *rest)))
            if item is not None:
                stage2.append(item)

        def evac_up(n, m, bank, t):
            f = n // 2
            v, tv = centre(f, bank[:, 0:T], t)
            g, tg = centre(NF + f, bank[:, T:2 * T], t)
            tv = convolved(f, v, bank[:, 0:T], tg)
            tg = convolved(NF + f, g, bank[:, T:2 * T], tg)
            tv = convolved2(f, v, bank[:, 0:T], tv)
            tg = convolved2(NF + f, g, bank[:, T:2 * T], tg)
            act.wait(tg)
            tg2 = act.do(lambda e: e.activation(g[:, :], g[:, :], ACT.Gelu_apprx_tanh))
            advance((f, v, tv, g, tg2))
            return [tv, tg]

        gemm("up2", 2 * NF, 8, hh, hl, t_h, evac_up, lead=4)
        while stage2 or stage3:
            advance(None)
        log_tables()
        stat = Stat(D)
        gemm("dn2", 8, NF, ph, pl, t_p, evac_add(40, stat), lead=2)
        ffn.close()
        R6, t_R6 = stat.get()
        dve.wait(*[t for _, free in squares.free for t in free])
        for j in range(8):
            dve.wait(t_xs[j], t_R6)
            t = dve.do(lambda e, j=j: e.scalar_tensor_tensor(out=yb[:, j, :], in0=xT[:, j, :], scalar=col("gfin", j),
                                                             in1=R6[:, 0:T], op0=ALU.mult, op1=ALU.mult))
            if j % 2 == 1:
                sp.wait(t)
                sp.dma(a["out"][:, j - 1:j + 1, :], yb[:, j - 1:j + 1, :], s_out, 0)
        sp.wait((s_out, 64))
        assert wants["split"] == len(pieces)

        with nc.Block() as block:
            @block.sync
            def _(e):
                sp.play(e)

            @block.tensor
            def _(e):
                pe.play(e)

            @block.scalar
            def _(e):
                act.play(e)

            @block.vector
            def _(e):
                dve.play(e)

            @block.gpsimd
            def _(e):
                pool.play(e)


def _tiles(w, order=None):
    k, n = w.shape
    t = w.reshape(k // P, P, n // P, P).transpose(2, 0, 1, 3)
    return t if order is None else t[order]


def _lead(tiles, m=4):
    n, k = tiles.shape[:2]
    return np.concatenate([tiles[:m].swapaxes(0, 1).reshape(m * k, P, P), tiles[m:].reshape(-1, P, P)])


def _by_chunk(tiles):
    return tiles.swapaxes(0, 1)


def _pieces(tiles):
    tiles = tiles.reshape(-1, P, P)
    return np.concatenate([tiles[i:i + PIECE].transpose(1, 0, 2).reshape(-1) for i in range(0, len(tiles), PIECE)])[None]


def _both(a, b):
    t = np.stack([_tiles(a), _tiles(b)], axis=1)
    return t.reshape(-1, *t.shape[2:])


def _tokens(w):
    k, n = w.shape
    return _pieces(w.reshape(k // P, P, n // 512, 4, P).transpose(2, 0, 3, 1, 4))


def _bucket_index():
    n = np.arange(256)
    large = 16 + (np.log(np.maximum(n, 16).astype(np.float32) / np.float32(16)) / np.float32(np.log(8.0))
                  * np.float32(16)).astype(np.int32)
    return np.where(n < 16, n, np.minimum(large, 31))


def _host(i):
    f = {k: np.asarray(v) for k, v in i.items()}
    o = {}
    o["xT"] = f["x"][0].T.reshape(8, P, T).transpose(1, 0, 2)
    o["pos"] = np.broadcast_to(f["positions"][0][None, :], (P, T))
    c8 = lambda v: v.reshape(-1, P).T
    inv = (np.float32(1.0) / (np.float32(10000.0) ** (np.arange(0, 64, 2, dtype=np.float32) / np.float32(64))))
    parts = dict(pre0=f["attn_pre_g"][0], pre1=f["attn_pre_g"][1], post0=f["attn_post_g"][0],
                 post1=f["attn_post_g"][1], fpre0=f["ffn_pre_g"][0], fpre1=f["ffn_pre_g"][1],
                 fpost0=f["ffn_post_g"][0], fpost1=f["ffn_post_g"][1], kvsrc=f["kv_src_g"], gq=f["mla_g_q"][0],
                 gkv=f["mla_g_kv"][0], gmix=f["g_mix_2"][0], gffn=f["g_ffn_2"][0], gfin=f["g_final_2"],
                 c=f["c_2"][0], bada=f["b_ada_2"][0], cw0=f["w_conv_2"][0, 0], cw1=f["w_conv_2"][0, 1],
                 cw2=f["w_conv_2"][0, 2], cb=f["b_conv_2"][0], inv=np.tile(inv.astype(np.float32), 4))
    o["cols"] = np.concatenate([c8(parts[n]) for n in COLS], axis=1)
    wa = f["mla_w_a"][0]
    k1, k2 = wa[:, 640:672], wa[:, 672:704]
    o["wa"] = _pieces(_lead(_tiles(np.concatenate([wa[:, 384:640], wa[:, :384]] + [k1] * 4 + [k2] * 4, axis=1))))
    uq = f["mla_w_uq"][0].reshape(384, 8, 192)
    rope = [uq[:, 4 * g:4 * g + 4, 128 + 32 * s:160 + 32 * s].reshape(384, P) for g in range(2) for s in range(2)]
    o["wuq"] = _pieces(_tiles(np.concatenate(rope + [uq[:, :, :128].reshape(384, 1024)], axis=1)))
    ukv = f["mla_w_ukv"][0].reshape(256, 8, 256)
    o["wuk"] = _pieces(_tiles(ukv[:, :, :128].reshape(256, 1024)))
    o["wuv"] = _tokens(ukv[:, :, 128:].reshape(256, 1024))
    o["wo0"] = _pieces(_by_chunk(_tiles(f["mla_w_o"][0])))
    for l in range(2):
        o[f"gu{l}"] = _pieces(_lead(_both(f["ffn_w_gate"][l], f["ffn_w_up"][l])))
        o[f"dn{l}"] = _pieces(_lead(_tiles(f["ffn_w_down"][l]), 2))
    o["wkv_k"] = _pieces(_tiles(f["w_kv_shared"][:, :1024]))
    o["wkv_v"] = _tokens(f["w_kv_shared"][:, 1024:])
    o["wq1"] = _pieces(_lead(_tiles(f["b_w_q"][0]), 2))
    o["wo1"] = _pieces(_by_chunk(_tiles(f["b_w_o"][0])))
    d = 128 + np.arange(P)[:, None] - np.arange(T)[None, :]
    o["relb"] = f["b_rel_table"][0][:, np.clip(d, -63, 256) + 63].transpose(1, 0, 2)
    o["relm"] = f["rel_bias_2"][:, _bucket_index()[np.clip(d, 0, 255)]].transpose(1, 0, 2)
    w = f["w_in_2"][0]
    qa, ka, va, qb, kb, vb = (w[:, 512 * j:512 * (j + 1)] for j in range(6))
    o["win_v"] = _tokens(np.concatenate([va, vb], axis=1))
    o["win_k"] = _pieces(_tiles(np.concatenate([ka, kb], axis=1)))
    o["win_q"] = _pieces(_tiles(np.concatenate([qa, qb], axis=1)))
    o["win_g"] = _pieces(_tiles(w[:, 3072:]))
    o["wbr"] = _pieces(np.stack([_tiles(f["w_br_moba_2"][0]), _tiles(f["w_br_sb_2"][0])], axis=1))
    o["wout"] = _pieces(_lead(_tiles(f["w_out_2"][0])))
    up = f["w_up_2"][0]
    o["up2"] = _pieces(_lead(_both(up[:, :FF], up[:, FF:])))
    o["dn2"] = _pieces(_lead(_tiles(f["w_down_2"][0]), 2))
    o["wada"] = _pieces(f["w_ada_2"][0].reshape(8, P, 3, 16, P).transpose(2, 0, 3, 1, 4))
    return {k: np.ascontiguousarray(v) for k, v in o.items()}


def kernel(**inputs):
    import concourse.bacc as _bacc
    from concourse import mybir as _mybir
    from concourse.bass_utils import run_bass_kernel_spmd as _run

    nc = _bacc.Bacc("TRN2", target_bir_lowering=False, num_devices=1)
    arrays, aps = {}, {}
    for name, v in _host(inputs).items():
        arrays[f"in_{name}"] = v
        aps[name] = nc.dram_tensor(f"in_{name}", v.shape, _mybir.dt.from_np(v.dtype), kind="ExternalInput").ap()
    aps["out"] = nc.dram_tensor("out_0", (P, 8, T), F32, kind="ExternalOutput").ap()
    build(nc, aps)
    r = _run(nc, [arrays], core_ids=[0])
    got = r.results[0]["out_0"]
    return np.ascontiguousarray(got.transpose(1, 0, 2).reshape(D, T).T[None])
```
